# Optimizing a Trainium2 kernel written in Bass

```python
import jax, jax.numpy as jnp
from jax import lax
import numpy as np
import math

D_MODEL = 1024
BATCH = 1
SEQ = 512
DEPTH = 1

D_RNN = D_MODEL
RNN_HEADS = 8
RNN_HEAD_DIM = D_RNN // RNN_HEADS
RNN_CONV_WIDTH = 4
RGLRU_C = 8.0
D_CONV = D_MODEL
CONF_KERNEL = 31
D_FF = ((8 * D_MODEL // 3 + 127) // 128) * 128
N_BRANCH = 2
N_SUBLAYER = 3
FFN_RES_WEIGHT = 0.5
DEEPNORM_ALPHA = (2.0 * DEPTH) ** 0.25
DEEPNORM_BETA = (8.0 * DEPTH) ** -0.25
LN_EPS = 1e-5
IN_SPLITS = (D_RNN, 2 * D_RNN, 2 * D_RNN + 2 * D_CONV, 2 * D_RNN + 2 * D_CONV + D_MODEL)
D_IN = 2 * D_RNN + 2 * D_CONV + N_BRANCH * D_MODEL


def layer_norm(x, g, b):
    xf = x.astype(jnp.float32)
    mu = jnp.mean(xf, axis=-1, keepdims=True)
    xc = xf - mu
    var = jnp.mean(jnp.square(xc), axis=-1, keepdims=True)
    y = (xc * lax.rsqrt(var + LN_EPS)).astype(x.dtype)
    return y * g + b

def modulate(x, shift, scale):
    return x * (1 + scale[:, None, :]) + shift[:, None, :]

def causal_depthwise_conv(x, w, b):
    k = w.shape[0]
    y = lax.conv_general_dilated(
        x, w[:, None, :], window_strides=(1,), padding=[(k - 1, 0)],
        dimension_numbers=('NWC', 'WIO', 'NWC'), feature_group_count=x.shape[-1])
    return y + b

def swiglu(u, w_gate, w_up, w_down):
    return (jax.nn.silu(u @ w_gate) * (u @ w_up)) @ w_down

def rg_lru(x, w_r, b_r, w_i, b_i, lam):
    bsz, seq, _ = x.shape
    xh = x.reshape(bsz, seq, RNN_HEADS, RNN_HEAD_DIM)
    r = jax.nn.sigmoid(jnp.einsum('bshd,hde->bshe', xh, w_r).reshape(bsz, seq, D_RNN) + b_r)
    i = jax.nn.sigmoid(jnp.einsum('bshd,hde->bshe', xh, w_i).reshape(bsz, seq, D_RNN) + b_i)
    log_a = (-RGLRU_C * jax.nn.softplus(-lam.astype(jnp.float32))) * r.astype(jnp.float32)
    a = jnp.exp(log_a)
    bterm = jnp.sqrt(-jnp.expm1(2.0 * log_a)) * (i * x).astype(jnp.float32)

    def combine(left, right):
        a1, b1 = left
        a2, b2 = right
        return a1 * a2, a2 * b1 + b2

    _, h = lax.associative_scan(combine, (a, bterm), axis=1)
    return h.astype(x.dtype)

def first_inputs(seed: int = 0) -> dict:
    key = jax.random.key(seed)
    ks = jax.random.split(key, 40)
    f32 = jnp.float32

    def nrm(k, shape, scale):
        return jax.random.normal(k, shape, f32) * scale

    def gain(k, n):
        return 1.0 + 0.02 * jax.random.normal(k, (n,), f32)

    a0 = jax.random.uniform(ks[14], (D_RNN,), f32, 0.9, 0.999) ** (1.0 / RGLRU_C)
    lam = jnp.log(a0) - jnp.log1p(-a0)
    return {
        'x': nrm(ks[0], (BATCH, SEQ, D_MODEL), 1.0),
        'c': nrm(ks[1], (BATCH, D_MODEL), 1.0),
        'ada_w': nrm(ks[2], (D_MODEL, 3 * N_SUBLAYER * D_MODEL), 0.2 * D_MODEL ** -0.5),
        'ada_b': nrm(ks[3], (3 * N_SUBLAYER * D_MODEL,), 0.01),
        'ffn1_w_gate': nrm(ks[4], (D_MODEL, D_FF), D_MODEL ** -0.5),
        'ffn1_w_up': nrm(ks[5], (D_MODEL, D_FF), D_MODEL ** -0.5),
        'ffn1_w_down': nrm(ks[6], (D_FF, D_MODEL), DEEPNORM_BETA * D_FF ** -0.5),
        'ln1_g': gain(ks[7], D_MODEL),
        'ln1_b': nrm(ks[8], (D_MODEL,), 0.02),
        'w_in': nrm(ks[9], (D_MODEL, D_IN), D_MODEL ** -0.5),
        'rnn_conv_w': nrm(ks[10], (RNN_CONV_WIDTH, D_RNN), RNN_CONV_WIDTH ** -0.5),
        'rnn_conv_b': nrm(ks[11], (D_RNN,), 0.01),
        'rglru_w_r': nrm(ks[12], (RNN_HEADS, RNN_HEAD_DIM, RNN_HEAD_DIM), RNN_HEAD_DIM ** -0.5),
        'rglru_b_r': nrm(ks[13], (D_RNN,), 0.01),
        'rglru_w_i': nrm(ks[15], (RNN_HEADS, RNN_HEAD_DIM, RNN_HEAD_DIM), RNN_HEAD_DIM ** -0.5),
        'rglru_b_i': nrm(ks[16], (D_RNN,), 0.01),
        'rglru_lambda': lam,
        'rnn_w_proj': nrm(ks[17], (D_RNN, D_MODEL), D_RNN ** -0.5),
        'conf_dw_w': nrm(ks[18], (CONF_KERNEL, D_CONV), CONF_KERNEL ** -0.5),
        'conf_dw_b': nrm(ks[19], (D_CONV,), 0.01),
        'conf_ln_g': gain(ks[20], D_CONV),
        'conf_ln_b': nrm(ks[21], (D_CONV,), 0.02),
        'conf_w_proj': nrm(ks[22], (D_CONV, D_MODEL), D_CONV ** -0.5),
        'mix_w_out': nrm(ks[23], (D_MODEL, D_MODEL), DEEPNORM_BETA * D_MODEL ** -0.5),
        'ln2_g': gain(ks[24], D_MODEL),
        'ln2_b': nrm(ks[25], (D_MODEL,), 0.02),
        'ffn2_w_gate': nrm(ks[26], (D_MODEL, D_FF), D_MODEL ** -0.5),
        'ffn2_w_up': nrm(ks[27], (D_MODEL, D_FF), D_MODEL ** -0.5),
        'ffn2_w_down': nrm(ks[28], (D_FF, D_MODEL), DEEPNORM_BETA * D_FF ** -0.5),
        'ln3_g': gain(ks[29], D_MODEL),
        'ln3_b': nrm(ks[30], (D_MODEL,), 0.02),
    }

def first_block(x, c, ada_w, ada_b, ffn1_w_gate, ffn1_w_up, ffn1_w_down, ln1_g, ln1_b,
              w_in, rnn_conv_w, rnn_conv_b, rglru_w_r, rglru_b_r, rglru_w_i, rglru_b_i,
              rglru_lambda, rnn_w_proj, conf_dw_w, conf_dw_b, conf_ln_g, conf_ln_b,
              conf_w_proj, mix_w_out, ln2_g, ln2_b, ffn2_w_gate, ffn2_w_up, ffn2_w_down,
              ln3_g, ln3_b):
    mod = jax.nn.silu(c) @ ada_w + ada_b
    sh1, sc1, g1, sh2, sc2, g2, sh3, sc3, g3 = jnp.split(mod, 3 * N_SUBLAYER, axis=-1)

    for _ in range(DEPTH):
        u = modulate(x, sh1, sc1)
        y = swiglu(u, ffn1_w_gate, ffn1_w_up, ffn1_w_down)
        x = layer_norm(DEEPNORM_ALPHA * x + FFN_RES_WEIGHT * (1 + g1[:, None, :]) * y, ln1_g, ln1_b)

        u = modulate(x, sh2, sc2)
        proj = u @ w_in
        xr, gr, conf_in, gate_a, gate_b = jnp.split(proj, IN_SPLITS, axis=-1)

        xr = causal_depthwise_conv(xr, rnn_conv_w, rnn_conv_b)
        hr = rg_lru(xr, rglru_w_r, rglru_b_r, rglru_w_i, rglru_b_i, rglru_lambda)
        ya = (hr * jax.nn.gelu(gr)) @ rnn_w_proj

        glu = conf_in[..., :D_CONV] * jax.nn.sigmoid(conf_in[..., D_CONV:])
        hb = causal_depthwise_conv(glu, conf_dw_w, conf_dw_b)
        hb = jax.nn.silu(layer_norm(hb, conf_ln_g, conf_ln_b))
        yb = hb @ conf_w_proj

        merged = jax.nn.sigmoid(gate_a) * ya + jax.nn.sigmoid(gate_b) * yb
        out = merged @ mix_w_out
        x = layer_norm(DEEPNORM_ALPHA * x + (1 + g2[:, None, :]) * out, ln2_g, ln2_b)

        u = modulate(x, sh3, sc3)
        y = swiglu(u, ffn2_w_gate, ffn2_w_up, ffn2_w_down)
        x = layer_norm(DEEPNORM_ALPHA * x + FFN_RES_WEIGHT * (1 + g3[:, None, :]) * y, ln3_g, ln3_b)
    return x


_first_inputs = first_inputs


def first_inputs(seed=0):
    import zlib

    import numpy as np

    out = dict(_first_inputs(seed))
    spreads = {}
    factors = {'ada_b': 5.461,
     'ln1_g': 2.801,
     'rnn_conv_b': 6.954,
     'rglru_b_r': 8.0,
     'rglru_b_i': 8.0,
     'conf_dw_b': 8.0,
     'conf_ln_g': 8.0,
     'conf_ln_b': 8.0,
     'ln2_g': 2.829,
     'ln2_b': 2.781,
     'ln3_g': 2.931,
     'ln3_b': 2.769}
    for name, (base, spread) in spreads.items():
        noise = np.random.default_rng([zlib.crc32(name.encode()), seed]).standard_normal(out[name].shape)
        drawn = base * np.exp(spread * noise) if base else spread * noise
        out[name] = __import__('jax').numpy.asarray(drawn.astype(out[name].dtype))
    for name, factor in factors.items():
        out[name] = (out[name] * factor).astype(out[name].dtype)
    return out


_narrow_inputs = first_inputs


def first_inputs(seed=0):

    out = dict(_narrow_inputs(seed))
    wider = {'ln1_b': 3.69,
     'rglru_b_r': 12.0,
     'rglru_b_i': 9.02,
     'conf_ln_g': 6.16,
     'conf_ln_b': 5.49,
     'ln3_g': 3.3,
     'ln3_b': 3.3}
    for name, times in wider.items():
        mean = out[name].mean()
        out[name] = (mean + times * (out[name] - mean)).astype(out[name].dtype)
    return out


CHUNK = 64
RMS_EPS = 1e-6
N_BRANCHES = 3
GLA_HEADS = 4
GLA_DK = 128
GLA_DV = 128
GLA_GATE_RANK = 16
GLA_GATE_NORM = 16.0
GLA_KEY_W = GLA_HEADS * GLA_DK
GLA_VAL_W = GLA_HEADS * GLA_DV
ATT_HEADS = 8
ATT_HD = 64
ATT_W = ATT_HEADS * ATT_HD
ATT_LEFT_CHUNKS = 8
REL_MAX = 256
REL_SIZE = REL_MAX + CHUNK
GDN_HEADS = 4
GDN_DK = 128
GDN_DV = 128
GDN_KEY_W = GDN_HEADS * GDN_DK
GDN_VAL_W = GDN_HEADS * GDN_DV
GDN_CONV_CH = 2 * GDN_KEY_W + GDN_VAL_W
CONV_W = 4
FFN_HIDDEN = -(-(8 * D_MODEL) // (3 * 256)) * 256
IN_WIDTHS = (GLA_KEY_W, GLA_KEY_W, GLA_VAL_W, GLA_VAL_W, GLA_GATE_RANK,
             ATT_W, ATT_W, ATT_W,
             GDN_KEY_W, GDN_KEY_W, GDN_VAL_W, GDN_VAL_W, GDN_HEADS, GDN_HEADS,
             N_BRANCHES * D_MODEL)
IN_W = sum(IN_WIDTHS)


F32 = jnp.float32

def rmsnorm(x, g):
    xf = x.astype(F32)
    y = xf * lax.rsqrt(jnp.mean(xf * xf, axis=-1, keepdims=True) + RMS_EPS)
    return (y * g.astype(F32)).astype(x.dtype)

def gated_head_rmsnorm(o, gate, g, n_heads):
    b, s, w = o.shape
    oh = o.reshape(b, s, n_heads, w // n_heads).astype(F32)
    oh = oh * lax.rsqrt(jnp.mean(oh * oh, axis=-1, keepdims=True) + RMS_EPS) * g.astype(F32)
    return oh.reshape(b, s, w) * jax.nn.silu(gate.astype(F32))

def l2norm(t):
    return t * lax.rsqrt(jnp.sum(t * t, axis=-1, keepdims=True) + RMS_EPS)

def to_chunks(t, n_heads):
    b, s, w = t.shape
    return t.reshape(b, s // CHUNK, CHUNK, n_heads, w // n_heads).transpose(0, 3, 1, 2, 4)

def from_chunks(t):
    b, h, n, c, d = t.shape
    return t.transpose(0, 2, 3, 1, 4).reshape(b, n * c, h * d)

def causal_depthwise_conv_2(x, w):
    return lax.conv_general_dilated(
        x, w[:, None, :].astype(x.dtype), window_strides=(1,), padding=[(CONV_W - 1, 0)],
        dimension_numbers=('NWC', 'WIO', 'NWC'), feature_group_count=x.shape[-1])

def gla_mixer(q, k, v, r, gate_lr, w_gate_up, b_gate, norm_g):
    b, s, _ = q.shape
    log_a = jax.nn.log_sigmoid((gate_lr @ w_gate_up + b_gate).astype(F32)) / GLA_GATE_NORM
    qc = to_chunks(q.astype(F32) * GLA_DK ** -0.5, GLA_HEADS)
    kc = to_chunks(k.astype(F32), GLA_HEADS)
    vc = to_chunks(v.astype(F32), GLA_HEADS)
    gc = jnp.cumsum(to_chunks(log_a, GLA_HEADS), axis=3)
    causal = jnp.tril(jnp.ones((CHUNK, CHUNK), dtype=bool))

    def step(state, inp):
        q_, k_, v_, g_ = inp
        diff = jnp.where(causal[:, :, None], g_[:, :, :, None, :] - g_[:, :, None, :, :], -jnp.inf)
        scores = jnp.einsum('bhik,bhijk->bhij', q_, jnp.exp(diff) * k_[:, :, None, :, :])
        g_last = g_[:, :, -1, :]
        o = (jnp.einsum('bhik,bhkv->bhiv', q_ * jnp.exp(g_), state)
             + jnp.einsum('bhij,bhjv->bhiv', scores, v_))
        state = (jnp.exp(g_last)[..., None] * state
                 + jnp.einsum('bhjk,bhjv->bhkv', k_ * jnp.exp(g_last[:, :, None, :] - g_), v_))
        return state, o

    init = jnp.zeros((b, GLA_HEADS, GLA_DK, GLA_DV), F32)
    xs = (jnp.moveaxis(qc, 2, 0), jnp.moveaxis(kc, 2, 0), jnp.moveaxis(vc, 2, 0), jnp.moveaxis(gc, 2, 0))
    _, o = lax.scan(step, init, xs)
    o = from_chunks(jnp.moveaxis(o, 0, 2))
    return gated_head_rmsnorm(o, r, norm_g, GLA_HEADS).astype(q.dtype)

def chunk_band_attention(q, k, v, rel_bias):
    b, s, _ = q.shape
    n = s // CHUNK
    left = ATT_LEFT_CHUNKS * CHUNK
    band = left + CHUNK

    def heads(t):
        return t.reshape(b, s, ATT_HEADS, ATT_HD).transpose(0, 2, 1, 3)

    qh = heads(q) * ATT_HD ** -0.5
    kh = jnp.pad(heads(k), ((0, 0), (0, 0), (left, 0), (0, 0)))
    vh = jnp.pad(heads(v), ((0, 0), (0, 0), (left, 0), (0, 0)))
    rel = jnp.arange(CHUNK)[:, None] + left - jnp.arange(band)[None, :]
    bias = rel_bias[:, jnp.clip(rel, -(CHUNK - 1), REL_MAX) + (CHUNK - 1)].astype(F32)

    def one_chunk(c):
        start = c * CHUNK
        q_ = lax.dynamic_slice_in_dim(qh, start, CHUNK, axis=2)
        k_ = lax.dynamic_slice_in_dim(kh, start, band, axis=2)
        v_ = lax.dynamic_slice_in_dim(vh, start, band, axis=2)
        scores = jnp.einsum('bhid,bhjd->bhij', q_, k_, preferred_element_type=F32) + bias
        valid = (start - left + jnp.arange(band)) >= 0
        p = jax.nn.softmax(jnp.where(valid, scores, -jnp.inf), axis=-1)
        return jnp.einsum('bhij,bhjd->bhid', p.astype(v_.dtype), v_)

    o = lax.map(one_chunk, jnp.arange(n))
    return o.transpose(1, 0, 3, 2, 4).reshape(b, s, ATT_W)

def gated_deltanet(q, k, v, z, a, b_logit, conv_w, a_log, dt_bias, norm_g):
    out_dtype = q.dtype
    qkv = causal_depthwise_conv_2(jnp.concatenate([q, k, v], axis=-1), conv_w)
    qkv = jax.nn.silu(qkv.astype(F32))
    q, k, v = jnp.split(qkv, [GDN_KEY_W, 2 * GDN_KEY_W], axis=-1)
    log_alpha = -jnp.exp(a_log.astype(F32)) * jax.nn.softplus(a.astype(F32) + dt_bias.astype(F32))
    beta = jax.nn.sigmoid(b_logit.astype(F32))
    qc = l2norm(to_chunks(q, GDN_HEADS)) * GDN_DK ** -0.5
    kc = l2norm(to_chunks(k, GDN_HEADS))
    vc = to_chunks(v, GDN_HEADS)
    gc = jnp.cumsum(to_chunks(log_alpha, GDN_HEADS)[..., 0], axis=-1)
    bc = to_chunks(beta, GDN_HEADS)
    incl = jnp.tril(jnp.ones((CHUNK, CHUNK), dtype=bool))
    strict = jnp.tril(jnp.ones((CHUNK, CHUNK), dtype=bool), k=-1)
    gamma = jnp.exp(jnp.where(incl, gc[..., :, None] - gc[..., None, :], -jnp.inf))
    k_beta = kc * bc
    a_mat = jnp.where(strict, jnp.einsum('bhnid,bhnjd->bhnij', k_beta, kc) * gamma, 0.0)
    rhs = jnp.concatenate([vc * bc, k_beta * jnp.exp(gc)[..., None]], axis=-1)
    sol = lax.linalg.triangular_solve(a_mat + jnp.eye(CHUNK, dtype=F32), rhs,
                                      left_side=True, lower=True, unit_diagonal=True)
    u = sol[..., :GDN_DV]
    w = sol[..., GDN_DV:]
    attn_qk = jnp.where(incl, jnp.einsum('bhnid,bhnjd->bhnij', qc, kc) * gamma, 0.0)

    def step(state, inp):
        q_, k_, u_, w_, g_, a_ = inp
        v_new = u_ - jnp.einsum('bhik,bhkv->bhiv', w_, state)
        o = (jnp.einsum('bhik,bhkv->bhiv', q_ * jnp.exp(g_)[..., None], state)
             + jnp.einsum('bhij,bhjv->bhiv', a_, v_new))
        g_last = g_[..., -1]
        state = (state * jnp.exp(g_last)[..., None, None]
                 + jnp.einsum('bhjk,bhjv->bhkv', k_ * jnp.exp(g_last[..., None] - g_)[..., None], v_new))
        return state, o

    bsz = qc.shape[0]
    init = jnp.zeros((bsz, GDN_HEADS, GDN_DK, GDN_DV), F32)
    xs = tuple(jnp.moveaxis(t, 2, 0) for t in (qc, kc, u, w, gc, attn_qk))
    _, o = lax.scan(step, init, xs)
    o = from_chunks(jnp.moveaxis(o, 0, 2))
    return gated_head_rmsnorm(o, z, norm_g, GDN_HEADS).astype(out_dtype)

def split_columns(t, widths):
    bounds, acc = [], 0
    for wdt in widths[:-1]:
        acc += wdt
        bounds.append(acc)
    return jnp.split(t, bounds, axis=-1)

def hybrid_layer(x, mix_norm_g, w_in, gla_w_gate_up, gla_b_gate, gla_norm_g, att_rel_bias,
                 gdn_conv_w, gdn_a_log, gdn_dt_bias, gdn_norm_g, w_branch_gla, w_branch_att,
                 w_branch_gdn, w_out, ffn_norm_g, w_ffn_in, w_ffn_out):
    b, s, _ = x.shape
    h = rmsnorm(x, mix_norm_g)
    proj = h @ w_in
    (gla_q, gla_k, gla_v, gla_r, gla_lr, att_q, att_k, att_v,
     gdn_q, gdn_k, gdn_v, gdn_z, gdn_a, gdn_b, merge) = split_columns(proj, IN_WIDTHS)
    o_gla = gla_mixer(gla_q, gla_k, gla_v, gla_r, gla_lr, gla_w_gate_up, gla_b_gate, gla_norm_g)
    o_att = chunk_band_attention(att_q, att_k, att_v, att_rel_bias)
    o_gdn = gated_deltanet(gdn_q, gdn_k, gdn_v, gdn_z, gdn_a, gdn_b, gdn_conv_w, gdn_a_log,
                           gdn_dt_bias, gdn_norm_g)
    gates = jax.nn.sigmoid(merge.astype(F32)).reshape(b, s, N_BRANCHES, D_MODEL)
    y = (gates[:, :, 0] * (o_gla @ w_branch_gla).astype(F32)
         + gates[:, :, 1] * (o_att @ w_branch_att).astype(F32)
         + gates[:, :, 2] * (o_gdn @ w_branch_gdn).astype(F32))
    x = x + y.astype(x.dtype) @ w_out
    h2 = rmsnorm(x, ffn_norm_g)
    gate, up = jnp.split(h2 @ w_ffn_in, 2, axis=-1)
    return x + (jax.nn.silu(gate) * up) @ w_ffn_out

def second_inputs(seed: int = 0) -> dict:
    key = jax.random.key(seed)
    ks = jax.random.split(key, 20)

    def nrm(k, shape, fan_in):
        return jax.random.normal(k, shape, F32) * fan_in ** -0.5

    def gain(k, shape):
        return 1.0 + 0.01 * jax.random.normal(k, shape, F32)

    dt = jnp.exp(jax.random.uniform(ks[9], (DEPTH, GDN_HEADS), F32)
                 * (math.log(0.1) - math.log(0.001)) + math.log(0.001))
    return {
        'x': jax.random.normal(ks[0], (BATCH, SEQ, D_MODEL), F32),
        'mix_norm_g': gain(ks[1], (DEPTH, D_MODEL)),
        'w_in': nrm(ks[2], (DEPTH, D_MODEL, IN_W), D_MODEL),
        'gla_w_gate_up': nrm(ks[3], (DEPTH, GLA_GATE_RANK, GLA_KEY_W), GLA_GATE_RANK),
        'gla_b_gate': 0.1 * jax.random.normal(ks[4], (DEPTH, GLA_KEY_W), F32),
        'gla_norm_g': gain(ks[5], (DEPTH, GLA_DV)),
        'att_rel_bias': 0.1 * jax.random.normal(ks[6], (DEPTH, ATT_HEADS, REL_SIZE), F32),
        'gdn_conv_w': nrm(ks[7], (DEPTH, CONV_W, GDN_CONV_CH), CONV_W),
        'gdn_a_log': jnp.log(jax.random.uniform(ks[8], (DEPTH, GDN_HEADS), F32, 1.0, 16.0)),
        'gdn_dt_bias': dt + jnp.log(-jnp.expm1(-dt)),
        'gdn_norm_g': gain(ks[10], (DEPTH, GDN_DV)),
        'w_branch_gla': nrm(ks[11], (DEPTH, GLA_VAL_W, D_MODEL), GLA_VAL_W),
        'w_branch_att': nrm(ks[12], (DEPTH, ATT_W, D_MODEL), ATT_W),
        'w_branch_gdn': nrm(ks[13], (DEPTH, GDN_VAL_W, D_MODEL), GDN_VAL_W),
        'w_out': nrm(ks[14], (DEPTH, D_MODEL, D_MODEL), D_MODEL),
        'ffn_norm_g': gain(ks[15], (DEPTH, D_MODEL)),
        'w_ffn_in': nrm(ks[16], (DEPTH, D_MODEL, 2 * FFN_HIDDEN), D_MODEL),
        'w_ffn_out': nrm(ks[17], (DEPTH, FFN_HIDDEN, D_MODEL), FFN_HIDDEN),
        'final_norm_g': gain(ks[18], (D_MODEL,)),
    }

def second_block(x, mix_norm_g, w_in, gla_w_gate_up, gla_b_gate, gla_norm_g, att_rel_bias,
              gdn_conv_w, gdn_a_log, gdn_dt_bias, gdn_norm_g, w_branch_gla, w_branch_att,
              w_branch_gdn, w_out, ffn_norm_g, w_ffn_in, w_ffn_out, final_norm_g):
    for l in range(DEPTH):
        x = hybrid_layer(x, mix_norm_g[l], w_in[l], gla_w_gate_up[l], gla_b_gate[l], gla_norm_g[l],
                         att_rel_bias[l], gdn_conv_w[l], gdn_a_log[l], gdn_dt_bias[l], gdn_norm_g[l],
                         w_branch_gla[l], w_branch_att[l], w_branch_gdn[l], w_out[l], ffn_norm_g[l],
                         w_ffn_in[l], w_ffn_out[l])
    return rmsnorm(x, final_norm_g)


_first_inputs_2 = second_inputs


def second_inputs(seed=0):
    import zlib

    import numpy as np

    out = dict(_first_inputs_2(seed))
    spreads = {}
    factors = {'mix_norm_g': 5.848,
     'gla_b_gate': 3.924,
     'gla_norm_g': 8.0,
     'att_rel_bias': 8.0,
     'gdn_norm_g': 8.0,
     'ffn_norm_g': 8.0,
     'final_norm_g': 5.818}
    for name, (base, spread) in spreads.items():
        noise = np.random.default_rng([zlib.crc32(name.encode()), seed]).standard_normal(out[name].shape)
        drawn = base * np.exp(spread * noise) if base else spread * noise
        out[name] = __import__('jax').numpy.asarray(drawn.astype(out[name].dtype))
    for name, factor in factors.items():
        out[name] = (out[name] * factor).astype(out[name].dtype)
    return out


_narrow_inputs_2 = second_inputs


def second_inputs(seed=0):

    out = dict(_narrow_inputs_2(seed))
    wider = {'gla_norm_g': 5.88,
     'att_rel_bias': 3.5,
     'gdn_norm_g': 6.34,
     'ffn_norm_g': 5.47,
     'final_norm_g': 6.53}
    for name, times in wider.items():
        mean = out[name].mean()
        out[name] = (mean + times * (out[name] - mean)).astype(out[name].dtype)
    return out


NORM_EPS = 1e-6
CHUNK_3 = 128
N_BRANCHES_3 = 2
GMLP_WIDTH = D_MODEL
GMLP_GROUPS = 8
GMLP_GROUP_DIM = GMLP_WIDTH // GMLP_GROUPS
SSM_EXPAND = 2
D_INNER = SSM_EXPAND * D_MODEL
HEAD_DIM = 64
N_SSM_HEADS = D_INNER // HEAD_DIM
N_SSM_GROUPS = 8
HEADS_PER_GROUP = N_SSM_HEADS // N_SSM_GROUPS
D_STATE = 128
CONV_WIDTH = 4
CONV_DIM = D_INNER + 2 * N_SSM_GROUPS * D_STATE
SSM_NORM_GROUP = D_INNER // N_SSM_GROUPS
D_FF_3 = 4 * D_MODEL
IN_PROJ_DIM = 2 * GMLP_WIDTH + D_INNER + CONV_DIM + N_SSM_HEADS + N_BRANCHES_3 * D_MODEL
_SPLITS = tuple(np.cumsum([2 * GMLP_WIDTH, D_INNER, CONV_DIM, N_SSM_HEADS]).tolist())


def rms_norm(x, g, eps=NORM_EPS):
    xf = x.astype(jnp.float32)
    out = xf * lax.rsqrt(jnp.mean(xf * xf, axis=-1, keepdims=True) + eps)
    return out.astype(x.dtype) * g

def layer_norm_3(x, g, b, eps=NORM_EPS):
    xf = x.astype(jnp.float32)
    mu = jnp.mean(xf, axis=-1, keepdims=True)
    var = jnp.mean(jnp.square(xf - mu), axis=-1, keepdims=True)
    out = (xf - mu) * lax.rsqrt(var + eps)
    return out.astype(x.dtype) * g + b

def gmlp_spatial_gating(uv, v_g, v_b, w_spatial, b_spatial):
    bsz, seqlen, _ = uv.shape
    nc = seqlen // CHUNK_3
    z = jax.nn.gelu(uv, approximate=False)
    u, v = jnp.split(z, 2, axis=-1)
    v = layer_norm_3(v, v_g, v_b)
    v = v.reshape(bsz, nc, CHUNK_3, GMLP_GROUPS, GMLP_GROUP_DIM)
    causal = jnp.tril(jnp.ones((CHUNK_3, CHUNK_3), dtype=bool))
    w = jnp.where(causal[None], w_spatial, jnp.zeros_like(w_spatial))
    s = jnp.einsum("gij,bcjgd->bcigd", w, v) + b_spatial.T[None, None, :, :, None]
    return u * s.reshape(bsz, seqlen, GMLP_WIDTH)

def causal_depthwise_conv_3(x, w, b):
    y = lax.conv_general_dilated(
        x, w, window_strides=(1,), padding=[(CONV_WIDTH - 1, 0)],
        dimension_numbers=("NWC", "WIO", "NWC"), feature_group_count=x.shape[-1])
    return y + b

def ssd_chunked(xh, dt, a, bm, cm):
    bsz, seqlen = xh.shape[:2]
    nc = seqlen // CHUNK_3
    xc = xh.reshape(bsz, nc, CHUNK_3, N_SSM_GROUPS, HEADS_PER_GROUP, HEAD_DIM)
    dtc = dt.reshape(bsz, nc, CHUNK_3, N_SSM_GROUPS, HEADS_PER_GROUP)
    bc = bm.reshape(bsz, nc, CHUNK_3, N_SSM_GROUPS, D_STATE)
    cc = cm.reshape(bsz, nc, CHUNK_3, N_SSM_GROUPS, D_STATE)
    xdt = xc * dtc[..., None]
    da = (dtc * a).astype(jnp.float32).transpose(0, 3, 4, 1, 2)
    cs = jnp.cumsum(da, axis=-1)
    causal = jnp.tril(jnp.ones((CHUNK_3, CHUNK_3), dtype=bool))
    seg = cs[..., :, None] - cs[..., None, :]
    lmat = jnp.exp(jnp.where(causal, seg, -jnp.inf))
    cb = jnp.einsum("bclgn,bcsgn->bgcls", cc, bc)
    m = cb[:, :, None] * lmat
    y_diag = jnp.einsum("bgrcls,bcsgrp->bclgrp", m, xdt)
    decay_states = jnp.exp(cs[..., -1:] - cs)
    states = jnp.einsum("bcsgn,bgrcs,bcsgrp->bcgrpn", bc, decay_states, xdt)
    chunk_decay = jnp.exp(cs[..., -1])

    def step(h, inp):
        st, dec = inp
        return h * dec[..., None, None] + st, h

    h0 = jnp.zeros_like(states[:, 0])
    _, prev = lax.scan(step, h0, (jnp.moveaxis(states, 1, 0), jnp.moveaxis(chunk_decay, -1, 0)))
    prev = jnp.moveaxis(prev, 0, 1)
    y_off = jnp.einsum("bclgn,bcgrpn,bgrcl->bclgrp", cc, prev, jnp.exp(cs))
    y = (y_diag + y_off).reshape(bsz, seqlen, N_SSM_GROUPS, HEADS_PER_GROUP, HEAD_DIM)
    return y.astype(xh.dtype)

def mamba2_branch(z, xbc, dt_raw, conv_w, conv_b, dt_bias, a_log, d_skip, ssm_norm_g):
    bsz, seqlen, _ = z.shape
    xbc = jax.nn.silu(causal_depthwise_conv_3(xbc, conv_w, conv_b))
    xs, bm, cm = jnp.split(xbc, [D_INNER, D_INNER + N_SSM_GROUPS * D_STATE], axis=-1)
    xh = xs.reshape(bsz, seqlen, N_SSM_GROUPS, HEADS_PER_GROUP, HEAD_DIM)
    bm = bm.reshape(bsz, seqlen, N_SSM_GROUPS, D_STATE)
    cm = cm.reshape(bsz, seqlen, N_SSM_GROUPS, D_STATE)
    dt = jax.nn.softplus(dt_raw + dt_bias).reshape(bsz, seqlen, N_SSM_GROUPS, HEADS_PER_GROUP)
    a = -jnp.exp(a_log.astype(jnp.float32)).reshape(N_SSM_GROUPS, HEADS_PER_GROUP)
    y = ssd_chunked(xh, dt, a, bm, cm)
    y = y + d_skip.reshape(N_SSM_GROUPS, HEADS_PER_GROUP)[:, :, None] * xh
    y = y.reshape(bsz, seqlen, D_INNER)
    yg = (y * jax.nn.silu(z)).reshape(bsz, seqlen, N_SSM_GROUPS, SSM_NORM_GROUP)
    yf = yg.astype(jnp.float32)
    yn = yf * lax.rsqrt(jnp.mean(yf * yf, axis=-1, keepdims=True) + NORM_EPS)
    return yn.reshape(bsz, seqlen, D_INNER).astype(z.dtype) * ssm_norm_g

def third_inputs(seed: int = 0) -> dict:
    key = jax.random.key(seed)
    ks = jax.random.split(key, 24)
    L = DEPTH

    def nrm(k, shape, scale):
        return jax.random.normal(k, shape, jnp.float32) * scale

    x = nrm(ks[0], (BATCH, SEQ, D_MODEL), 1.0)
    norm_mix_g = 1.0 + nrm(ks[1], (L, D_MODEL), 0.02)
    w_in = nrm(ks[2], (L, D_MODEL, IN_PROJ_DIM), D_MODEL ** -0.5)
    conv_w = nrm(ks[3], (L, CONV_WIDTH, 1, CONV_DIM), CONV_WIDTH ** -0.5)
    conv_b = nrm(ks[4], (L, CONV_DIM), 0.02)
    dt0 = jnp.exp(jax.random.uniform(ks[5], (L, N_SSM_HEADS), jnp.float32,
                                     minval=math.log(1e-3), maxval=math.log(1e-1)))
    dt_bias = dt0 + jnp.log(-jnp.expm1(-dt0))
    a_log = jnp.log(jax.random.uniform(ks[6], (L, N_SSM_HEADS), jnp.float32, minval=1.0, maxval=16.0))
    d_skip = 1.0 + nrm(ks[7], (L, N_SSM_HEADS), 0.02)
    ssm_norm_g = 1.0 + nrm(ks[8], (L, D_INNER), 0.02)
    v_norm_g = 1.0 + nrm(ks[9], (L, GMLP_WIDTH), 0.02)
    v_norm_b = nrm(ks[10], (L, GMLP_WIDTH), 0.02)
    w_spatial = nrm(ks[11], (L, GMLP_GROUPS, CHUNK_3, CHUNK_3), CHUNK_3 ** -0.5)
    b_spatial = 1.0 + nrm(ks[12], (L, GMLP_GROUPS, CHUNK_3), 0.02)
    b_gates = nrm(ks[13], (L, N_BRANCHES_3 * D_MODEL), 0.02)
    w_proj_a = nrm(ks[14], (L, GMLP_WIDTH, D_MODEL), GMLP_WIDTH ** -0.5)
    w_proj_b = nrm(ks[15], (L, D_INNER, D_MODEL), D_INNER ** -0.5)
    w_out = nrm(ks[16], (L, D_MODEL, D_MODEL), D_MODEL ** -0.5)
    norm_mlp_g = 1.0 + nrm(ks[17], (L, D_MODEL), 0.02)
    w_mlp_up = nrm(ks[18], (L, D_MODEL, D_FF_3), D_MODEL ** -0.5)
    w_mlp_down = nrm(ks[19], (L, D_FF_3, D_MODEL), D_FF_3 ** -0.5)
    norm_final_g = 1.0 + nrm(ks[20], (D_MODEL,), 0.02)
    return {"x": x, "norm_mix_g": norm_mix_g, "w_in": w_in, "conv_w": conv_w, "conv_b": conv_b,
            "dt_bias": dt_bias, "a_log": a_log, "d_skip": d_skip, "ssm_norm_g": ssm_norm_g,
            "v_norm_g": v_norm_g, "v_norm_b": v_norm_b, "w_spatial": w_spatial, "b_spatial": b_spatial,
            "b_gates": b_gates, "w_proj_a": w_proj_a, "w_proj_b": w_proj_b, "w_out": w_out,
            "norm_mlp_g": norm_mlp_g, "w_mlp_up": w_mlp_up, "w_mlp_down": w_mlp_down,
            "norm_final_g": norm_final_g}

def third_block(x, norm_mix_g, w_in, conv_w, conv_b, dt_bias, a_log, d_skip, ssm_norm_g,
              v_norm_g, v_norm_b, w_spatial, b_spatial, b_gates, w_proj_a, w_proj_b, w_out,
              norm_mlp_g, w_mlp_up, w_mlp_down, norm_final_g):
    for i in range(DEPTH):
        h = rms_norm(x, norm_mix_g[i])
        proj = h @ w_in[i]
        uv, z, xbc, dt_raw, gate_logits = jnp.split(proj, _SPLITS, axis=-1)
        y_a = gmlp_spatial_gating(uv, v_norm_g[i], v_norm_b[i], w_spatial[i], b_spatial[i])
        y_b = mamba2_branch(z, xbc, dt_raw, conv_w[i], conv_b[i], dt_bias[i], a_log[i],
                            d_skip[i], ssm_norm_g[i])
        gates = jax.nn.sigmoid(gate_logits + b_gates[i])
        gate_a, gate_b = jnp.split(gates, 2, axis=-1)
        merged = gate_a * (y_a @ w_proj_a[i]) + gate_b * (y_b @ w_proj_b[i])
        x = x + merged @ w_out[i]
        h2 = rms_norm(x, norm_mlp_g[i])
        x = x + jnp.square(jax.nn.relu(h2 @ w_mlp_up[i])) @ w_mlp_down[i]
    return rms_norm(x, norm_final_g)


_first_inputs_3 = third_inputs


def third_inputs(seed=0):
    import zlib

    import numpy as np

    out = dict(_first_inputs_3(seed))
    spreads = {}
    factors = {'norm_mix_g': 2.928,
     'conv_b': 22.114,
     'd_skip': 64.0,
     'ssm_norm_g': 48.16,
     'v_norm_g': 39.654,
     'v_norm_b': 41.889,
     'b_spatial': 27.455,
     'b_gates': 8.0,
     'norm_mlp_g': 11.492,
     'norm_final_g': 8.851}
    for name, (base, spread) in spreads.items():
        noise = np.random.default_rng([zlib.crc32(name.encode()), seed]).standard_normal(out[name].shape)
        drawn = base * np.exp(spread * noise) if base else spread * noise
        out[name] = __import__('jax').numpy.asarray(drawn.astype(out[name].dtype))
    for name, factor in factors.items():
        out[name] = (out[name] * factor).astype(out[name].dtype)
    return out


_narrow_inputs_3 = third_inputs


def third_inputs(seed=0):

    out = dict(_narrow_inputs_3(seed))
    wider = {'d_skip': 10.08,
     'ssm_norm_g': 5.52,
     'v_norm_g': 4.82,
     'v_norm_b': 4.81,
     'b_spatial': 4.7,
     'norm_final_g': 3.36}
    for name, times in wider.items():
        mean = out[name].mean()
        out[name] = (mean + times * (out[name] - mean)).astype(out[name].dtype)
    return out


def setup_inputs(seed=0):
    out = dict(first_inputs(seed))
    for name, value in second_inputs(seed + 1).items():
        if name != "x":
            out[name + "_2"] = value
    for name, value in third_inputs(seed + 2).items():
        if name != "x":
            out[name + "_3"] = value
    return out


def reference(
    x, c, ada_w, ada_b, ffn1_w_gate, ffn1_w_up, ffn1_w_down, ln1_g, ln1_b, w_in, rnn_conv_w,
    rnn_conv_b, rglru_w_r, rglru_b_r, rglru_w_i, rglru_b_i, rglru_lambda, rnn_w_proj, conf_dw_w,
    conf_dw_b, conf_ln_g, conf_ln_b, conf_w_proj, mix_w_out, ln2_g, ln2_b, ffn2_w_gate,
    ffn2_w_up, ffn2_w_down, ln3_g, ln3_b, mix_norm_g_2, w_in_2, gla_w_gate_up_2, gla_b_gate_2,
    gla_norm_g_2, att_rel_bias_2, gdn_conv_w_2, gdn_a_log_2, gdn_dt_bias_2, gdn_norm_g_2,
    w_branch_gla_2, w_branch_att_2, w_branch_gdn_2, w_out_2, ffn_norm_g_2, w_ffn_in_2,
    w_ffn_out_2, final_norm_g_2, norm_mix_g_3, w_in_3, conv_w_3, conv_b_3, dt_bias_3, a_log_3,
    d_skip_3, ssm_norm_g_3, v_norm_g_3, v_norm_b_3, w_spatial_3, b_spatial_3, b_gates_3,
    w_proj_a_3, w_proj_b_3, w_out_3, norm_mlp_g_3, w_mlp_up_3, w_mlp_down_3, norm_final_g_3,
):
    x = first_block(
        x, c, ada_w, ada_b, ffn1_w_gate, ffn1_w_up, ffn1_w_down, ln1_g, ln1_b, w_in, rnn_conv_w,
        rnn_conv_b, rglru_w_r, rglru_b_r, rglru_w_i, rglru_b_i, rglru_lambda, rnn_w_proj,
        conf_dw_w, conf_dw_b, conf_ln_g, conf_ln_b, conf_w_proj, mix_w_out, ln2_g, ln2_b,
        ffn2_w_gate, ffn2_w_up, ffn2_w_down, ln3_g, ln3_b,
    )
    x = second_block(
        x, mix_norm_g_2, w_in_2, gla_w_gate_up_2, gla_b_gate_2, gla_norm_g_2, att_rel_bias_2,
        gdn_conv_w_2, gdn_a_log_2, gdn_dt_bias_2, gdn_norm_g_2, w_branch_gla_2, w_branch_att_2,
        w_branch_gdn_2, w_out_2, ffn_norm_g_2, w_ffn_in_2, w_ffn_out_2, final_norm_g_2,
    )
    return third_block(
        x, norm_mix_g_3, w_in_3, conv_w_3, conv_b_3, dt_bias_3, a_log_3, d_skip_3, ssm_norm_g_3,
        v_norm_g_3, v_norm_b_3, w_spatial_3, b_spatial_3, b_gates_3, w_proj_a_3, w_proj_b_3,
        w_out_3, norm_mlp_g_3, w_mlp_up_3, w_mlp_down_3, norm_final_g_3,
    )


_drawn_inputs = setup_inputs


def setup_inputs(seed=0):
    import zlib

    import numpy as np

    out = dict(_drawn_inputs(seed))
    spreads = {}
    factors = {}
    for name, (base, spread) in spreads.items():
        noise = np.random.default_rng([zlib.crc32(name.encode()), seed]).standard_normal(out[name].shape)
        drawn = base * np.exp(spread * noise) if base else spread * noise
        out[name] = __import__('jax').numpy.asarray(drawn.astype(out[name].dtype))
    for name, factor in factors.items():
        out[name] = (out[name] * factor).astype(out[name].dtype)
    return out
```

```python
import numpy as np
import concourse.bass as bass
from concourse import mybir

F32 = mybir.dt.float32
ALU = mybir.AluOpType
ACT = mybir.ActivationFunctionType
AX = mybir.AxisListType

P = 128
T = 512
D = 1024
KD = D // P
BLK = T // P
FF = 2816
KF = FF // P
UNIT = 8
RING = 8
ALPHA = 2.0 ** 0.25
CH = 64
NCH = T // CH
LEVELS = (32, 16, 8, 4, 2, 1)
HEADS = 4
DK = 128
ATT_HEADS, ATT_HD = 8, 64
REL = 320
MH, MG, MP = 32, 8, 64
MHG = MH // MG
CONF_TAPS = 31
NEG = -1.0e30

VECTORS = [
    ("ada_b", 72), ("ln1_g", 8), ("ln1_b", 8), ("rnn_conv_w", 32), ("rnn_conv_b", 8), ("rglru_b_r", 8),
    ("rglru_b_i", 8), ("rglru_lambda", 8), ("conf_dw_w", 8 * CONF_TAPS), ("conf_dw_b", 8), ("conf_ln_g", 8),
    ("conf_ln_b", 8), ("ln2_g", 8), ("ln2_b", 8), ("ln3_g", 8), ("ln3_b", 8),
    ("mix_norm_g_2", 8), ("gla_b_gate_2", 4), ("gla_norm_g_2", 1), ("gdn_conv_w_2", 48), ("gdn_norm_g_2", 1),
    ("ffn_norm_g_2", 8), ("final_norm_g_2", 8),
    ("norm_mix_g_3", 8), ("conv_w_3", 128), ("conv_b_3", 32), ("ssm_norm_g_3", 16), ("v_norm_g_3", 8),
    ("v_norm_b_3", 8), ("b_gates_3", 16), ("norm_mlp_g_3", 8), ("norm_final_g_3", 8), ("d_skip_3", 16),
    ("gdn_a_log_2", 1), ("gdn_dt_bias_2", 1), ("dt_bias_3", 1), ("a_log_3", 1),
]
VCOL = {}
_n = 0
for _name, _w in VECTORS:
    VCOL[_name] = _n
    _n += _w
NVEC = _n

CONSTS = [("ident", P), ("one", P), ("mean_model", P), ("mean_head", P), ("mean_group", P),
          ("incl64", P), ("strict64", P), ("causal", P)] + [(f"level{s}", P) for s in LEVELS] + [
          ("start64", T), ("start128", T)]
CCOL = {}
_n = 0
for _name, _w in CONSTS:
    CCOL[_name] = (_n, _w)
    _n += _w
NCONST = _n


def constants():
    j, i = np.meshgrid(np.arange(P), np.arange(P), indexing="ij")
    same = j // CH == i // CH
    made = {
        "ident": j == i, "one": np.ones((P, P)), "mean_model": np.full((P, P), 1.0 / D),
        "mean_head": np.full((P, P), 1.0 / DK), "mean_group": np.full((P, P), 1.0 / 256),
        "incl64": same & (j <= i), "strict64": same & (j < i), "causal": j <= i,
        "start64": np.broadcast_to(np.arange(T) % CH != 0, (P, T)),
        "start128": np.broadcast_to(np.arange(T) % P != 0, (P, T)),
    }
    for s in LEVELS:
        made[f"level{s}"] = (j // (2 * s) == i // (2 * s)) & (j % (2 * s) < s) & (i % (2 * s) >= s)
    return np.concatenate([made[n].astype(np.float32) for n, _ in CONSTS], axis=1)


class Lane:

    def __init__(self, nc, name, chained):
        self.sem, self.count, self.queue, self.seen, self.chained = nc.alloc_semaphore(name), 0, [], {}, chained
        self.name = name

    def last(self):
        return (self.name, self.sem, self.count) if self.count else None

    def wait(self, *marks):
        for m in marks:
            if m is None:
                continue
            if isinstance(m, list):
                self.wait(*m)
                continue
            name, sem, value = m
            if self.seen.get(name, 0) < value:
                self.seen[name] = value
                self.queue.append(lambda e, s=sem, v=value: e.wait_ge(s, v))

    def issue(self, make, *marks):
        self.wait(*marks)
        self.queue.append(make)

    def step(self, make, *marks):
        if self.chained:
            self.wait(self.last())
        self.wait(*marks)
        self.count += 1
        self.queue.append(lambda e: make(e).then_inc(self.sem, 1))
        return self.last()

    def run(self, engine):
        for make in self.queue:
            make(engine)


class Banks:

    def __init__(self, pe, tensors):
        self.pe, self.aps, self.free, self.at = pe, [t[:, :] for t in tensors], [None] * len(tensors), 0

    def take(self):
        n = self.at
        self.at = (n + 1) % len(self.aps)
        self.pe.wait(self.free[n])
        return n, self.aps[n]


def pump(main, filler, every=1):
    for n, _ in enumerate(main):
        if n % every == 0:
            next(filler, None)


def drain(*gens):
    for g in gens:
        for _ in g:
            pass


class Program:
    def __init__(self, nc, dram):
        self.nc, self.dram = nc, dram
        self.plan, self.plan_cols = [], 0
        self.PE = Lane(nc, "pe_steps", False)
        self.AC = Lane(nc, "act_steps", True)
        self.VE = Lane(nc, "dve_steps", True)
        self.GP = Lane(nc, "pool_steps", True)
        self.SP = Lane(nc, "sp_steps", False)

        sb = nc.alloc_sbuf_tensor
        self.ring = sb("weight_ring", [P, RING, UNIT * P], F32)
        self.ring_sem = [nc.alloc_semaphore(f"ring_loaded{i}") for i in range(RING)]
        self.ring_loads = [0] * RING
        self.ring_free = [None] * RING
        self.ring_at = 0
        self.work = sb("work", [P, 72, T], F32)
        self.scratch = sb("scratch", [P, 5, T], F32)
        self.vec = sb("vector_columns", [P, NVEC], F32)
        self.con = sb("constant_columns", [P, NCONST], F32)
        self.mod = sb("modulation", [P, 72], F32)
        self.small = sb("small", [P, 256], F32)
        self.small_w = sb("narrow_weights", [P, KD, 64], F32)
        self.gate_up = sb("gla_gate_up", [16, T], F32)
        banks = [nc.alloc_psum_tensor(f"bank{i}", [P, T], F32) for i in range(8)]
        self.lin = Banks(self.PE, banks[:4])
        self.mat = Banks(self.PE, banks[4:])
        self.load_count = 0

    def t(self, i, n=None):
        return self.work[:, i, :] if n is None else self.work[:, i:i + n, :]

    def v(self, name, j=0, rows=P):
        c = VCOL[name] + j
        return self.vec[0:rows, c:c + 1]

    def c(self, name):
        a, w = CCOL[name]
        return self.con[:, a:a + w]

    def load(self, out, src, *marks):
        self.load_count += 1
        name = f"load{self.load_count}"
        sem = self.nc.alloc_semaphore(name)
        self.SP.issue(lambda e: e.dma_start(out, src).then_inc(sem, 16), *marks)
        return name, sem, 16

    def unit(self, blocks):
        slot = self.ring_at
        self.ring_at = (slot + 1) % RING
        cols = len(blocks) * P
        src = self.dram["weights"][self.plan_cols * P:(self.plan_cols + cols) * P].rearrange("(p c) -> p c", p=P)
        self.plan.append(blocks)
        self.plan_cols += cols
        self.ring_loads[slot] += 1
        dst = self.ring[:, slot, 0:cols]
        sem = self.ring_sem[slot]
        self.SP.issue(lambda e: e.dma_start(dst, src).then_inc(sem, 16), self.ring_free[slot])
        return dst, (f"ring{slot}", sem, 16 * self.ring_loads[slot]), slot

    def release(self, slot, mark):
        self.ring_free[slot] = mark

    def act(self, out, x, func, *marks, scale=1.0, bias=0.0, total=None):
        kw = {} if total is None else {"accum_out": total}
        if func == ACT.Copy:
            return self.AC.step(lambda e: e.activation(out, x, func, scale=scale), *marks)
        return self.AC.step(lambda e: e.activation(out, x, func, scale=scale, bias=bias, **kw), *marks)

    def tt(self, out, a, b, op, *marks, lane=None):
        return (lane or self.VE).step(lambda e: e.tensor_tensor(out, a, b, op), *marks)

    def ts(self, out, a, s1, s2, op0, op1, *marks, lane=None):
        if op1 is None:
            return (lane or self.VE).step(lambda e: e.tensor_scalar(out, a, s1, None, op0), *marks)
        return (lane or self.VE).step(lambda e: e.tensor_scalar(out, a, s1, s2, op0, op1), *marks)

    def stt(self, out, a, s, b, op0, op1, *marks):
        return self.VE.step(lambda e: e.scalar_tensor_tensor(out=out, in0=a, scalar=s, in1=b, op0=op0, op1=op1),
                            *marks)

    def copy(self, out, x, *marks):
        return self.VE.step(lambda e: e.tensor_copy(out, x), *marks)

    def scan(self, out, keep, x, *marks):
        return self.VE.step(lambda e: e.tensor_tensor_scan(out, keep, x, 0.0, ALU.mult, ALU.add), *marks)

    def mm(self, out, lhsT, rhs, start, stop, *marks, step=False):
        make = lambda e: e.matmul(out, lhsT, rhs, start=start, stop=stop, skip_group_check=True)
        return self.PE.step(make, *marks) if step else self.PE.issue(make, *marks)

    def tr(self, out, x, rows, *marks, step=False):
        ident = self.c("ident")[0:rows, 0:rows]
        make = lambda e: e.transpose(out, x, ident)
        return self.PE.step(make, *marks) if step else self.PE.issue(make, *marks)

    def meet(self):
        lanes = [self.PE, self.AC, self.VE, self.GP]
        marks = [x.last() for x in lanes]
        for x in lanes:
            x.wait(*[m for y, m in zip(lanes, marks) if y is not x])
        return marks

    def product(self, bank, name, f, src, marks, kts, start=True, stop=True):
        last = None
        for k0 in range(0, kts, UNIT):
            ks = range(k0, min(k0 + UNIT, kts))
            w, loaded, slot = self.unit([(name, k, f) for k in ks])
            self.PE.wait(loaded)
            for k in ks:
                last = self.mm(bank, w[:, (k - k0) * P:(k - k0 + 1) * P], src(k), start and k == 0,
                               stop and k == kts - 1, marks[k] if marks else None, step=(k == ks[-1]))
            self.release(slot, last)
        return last

    def linear(self, name, fs, src, marks, kts, evacuate):
        for f in fs:
            n, bank = self.lin.take()
            m = self.product(bank, name, f, src, marks, kts)
            self.lin.free[n] = evacuate(f, bank, m)
            yield

    def token_major(self, name, f0, src, marks, out, done):
        banks = [self.lin.take() for _ in range(BLK)]
        for k0 in range(0, KD, 2):
            w, loaded, slot = self.unit([(name, k, f0 + f) for k in (k0, k0 + 1) for f in range(4)])
            self.PE.wait(loaded)
            for k in (k0, k0 + 1):
                for b in range(BLK):
                    m = self.mm(banks[b][1], src(k)[:, b * P:(b + 1) * P], w[:, (k - k0) * T:(k - k0 + 1) * T],
                                k == 0, k == KD - 1, marks[k] if marks else None, step=(k % 2 == 1 and b == BLK - 1))
            self.release(slot, m)
            yield
        for b in range(BLK):
            done[b] = self.act(out(b), banks[b][1], ACT.Copy, m)
            self.lin.free[banks[b][0]] = done[b]
        yield

    def inverse_std(self, bank, n, mark, eps, std, pool):
        a = self.act(std, bank, ACT.Sqrt, mark, self.VE.last(), bias=self.eps[eps])
        pool.free[n] = a
        return self.VE.step(lambda e: e.reciprocal(std, std), a)

    def layer_norm(self, pre, pre_marks, out, evacuate_func, g, b):
        S = self.scratch
        n, bank = self.mat.take()
        for k in range(KD):
            m = self.mm(bank, self.c("mean_model"), pre(k), k == 0, k == KD - 1, pre_marks[k], step=(k == KD - 1))
        sq_read = [None, None]
        n2, bank2 = self.mat.take()
        for k in range(KD):
            cen = self.tt(pre(k), pre(k), bank, ALU.subtract, m)
            s = self.act(S[:, k % 2, :], pre(k), ACT.Square, cen, sq_read[k % 2])
            m2 = sq_read[k % 2] = self.mm(bank2, self.c("mean_model"), S[:, k % 2, :], k == 0, k == KD - 1, s,
                                          step=True)
        self.mat.free[n] = cen
        r = self.inverse_std(bank2, n2, m2, 1e-5, S[:, 2, :], self.mat)
        marks = []
        for k in range(KD):
            y = self.tt(pre(k), pre(k), S[:, 2, :], ALU.mult, r)
            marks.append(self.act(out(k), pre(k), evacuate_func, y, scale=self.v(g, k), bias=self.v(b, k)))
        return marks

    def rms_norm(self, x, x_marks, out, g):
        S = self.scratch
        n, bank = self.mat.take()
        sq_read = [None, None]
        for k in range(KD):
            s = self.act(S[:, k % 2, :], x(k), ACT.Square, x_marks[k], sq_read[k % 2])
            m = sq_read[k % 2] = self.mm(bank, self.c("mean_model"), S[:, k % 2, :], k == 0, k == KD - 1, s, step=True)
        r = self.inverse_std(bank, n, m, 1e-6, S[:, 2, :], self.mat)
        return [self.stt(out(k), x(k), self.v(g, k), S[:, 2, :], ALU.mult, ALU.mult, r) for k in range(KD)]

    def setup(self):
        d = self.dram
        vl = self.load(self.vec[:, :], d["vectors"])
        xl = self.load(self.t(0, 8), d["x"].rearrange("p (k t) -> p k t", k=KD))
        cl = self.load(self.con[:, :], d["constants"])
        sl = self.load(self.small_w[:, :, :], d["small_weights"].rearrange("p (k m) -> p k m", k=KD))
        gl = self.load(self.gate_up[:, :], d["gla_w_gate_up"])
        for lane in (self.PE, self.AC, self.VE, self.GP):
            lane.wait(vl, xl, cl, sl, gl)
        self.eps = {1e-5: self.small[:, 0:1], 1e-6: self.small[:, 1:2]}
        self.unit_bias = self.small[:, 2:3]
        self.zero_bias = self.small[:, 3:4]
        for i, val in enumerate((1e-5, 1e-6, 1.0, 0.0)):
            self.VE.step(lambda e, i=i, val=val: e.memset(self.small[:, i:i + 1], val))
        self.AC.wait(self.VE.last())

    def modulation(self, lo, hi):
        for j in range(lo, hi):
            w, loaded, slot = self.unit([("ada_w_T", k, j) for k in range(KD)])
            junk = self.scratch[:, 3:5, :].rearrange("p a t -> p (a t)")
            m = self.VE.step(lambda e, w=w, j=j: e.tensor_tensor_reduce(
                out=junk, in0=w, in1=self.c_act, scale=1.0, scalar=0.0, op0=ALU.mult, op1=ALU.add,
                accum_out=self.mod[:, j:j + 1]), loaded, self.c_ready)
            self.release(slot, m)
            yield
        self.tt(self.mod[:, lo:hi], self.mod[:, lo:hi], self.vec[:, VCOL["ada_b"] + lo:VCOL["ada_b"] + hi], ALU.add)
        for which in range(9):
            a, b = which * 8, which * 8 + 8
            if lo <= a and b <= hi and which % 3 == 1:
                self.ts(self.mod[:, a:b], self.mod[:, a:b], 1.0, None, ALU.add, None)
            if lo <= a and b <= hi and which % 3 == 2:
                w = 1.0 if which == 5 else 0.5
                self.ts(self.mod[:, a:b], self.mod[:, a:b], 1.0, w, ALU.add, ALU.mult)
        yield

    def swiglu(self, u, u_marks, gate, up, down, h0, evacuate):
        tmp_read = [None, None]
        h_marks = [None] * KF
        for j in range(KF):
            n, gbank = self.lin.take()
            gm = self.product(gbank, gate[0], gate[1] + j, u, u_marks, KD)
            n2, ubank = self.lin.take()
            um = self.product(ubank, up[0], up[1] + j, u, u_marks, KD)
            tmp = self.scratch[:, j % 2, :]
            a = self.act(tmp, gbank, ACT.Silu, gm, tmp_read[j % 2])
            self.lin.free[n] = a
            h_marks[j] = tmp_read[j % 2] = self.tt(self.t(h0 + j), tmp, ubank, ALU.mult, a, um)
            self.lin.free[n2] = h_marks[j]
            yield
        yield from self.linear(down, range(KD), lambda k: self.t(h0 + k), h_marks, KF, evacuate)

    def modulated(self, which, x_marks):
        sh, sc = 24 * which, 24 * which + 8
        return [self.ts(self.t(8 + k), self.t(k), self.mod[:, sc + k:sc + k + 1], self.mod[:, sh + k:sh + k + 1],
                        ALU.mult, ALU.add, x_marks[k]) for k in range(KD)]

    def residual(self, which, pre, base):
        marks = [None] * KD

        def evacuate(f, bank, m):
            c = 24 * which + 16 + f
            marks[f] = self.stt(pre(f), bank, self.mod[:, c:c + 1], pre(f), ALU.mult, ALU.add, m, base[f])
            return marks[f]
        return evacuate, marks

    def scaled_x(self, pre, x_marks):
        return [self.ts(pre(k), self.t(k), ALPHA, None, ALU.mult, None, x_marks[k], lane=self.GP) for k in range(KD)]

    def block1(self):
        t = self.t
        cb = t(52, 2).rearrange("p a t -> p (a t)")
        cl = self.load(cb, self.dram["c_rows"])
        self.c_act = cb
        self.c_ready = self.act(cb, cb, ACT.Silu, cl)
        drain(self.modulation(0, 16))
        x_marks = [None] * KD
        pre = lambda k: t(16 + k)
        u_marks = self.modulated(0, x_marks)
        base = self.scaled_x(pre, x_marks)
        evac, pm = self.residual(0, pre, base)
        rest = self.modulation(16, 72)
        for n, _ in enumerate(self.swiglu(lambda k: t(8 + k), u_marks, ("ffn1_w_gate", 0), ("ffn1_w_up", 0),
                                          "ffn1_w_down", 24, evac)):
            for _ in range(3):
                next(rest, None)
        drain(rest)
        x_marks = self.layer_norm(pre, pm, lambda k: t(k), ACT.Identity, "ln1_g", "ln1_b")
        self.meet()
        x_marks = self.mixer1(x_marks)
        self.meet()
        u_marks = self.modulated(2, x_marks)
        base = self.scaled_x(pre, x_marks)
        evac, pm = self.residual(2, pre, base)
        drain(self.swiglu(lambda k: t(8 + k), u_marks, ("ffn2_w_gate", 0), ("ffn2_w_up", 0), "ffn2_w_down", 24, evac))
        x_marks = self.layer_norm(pre, pm, lambda k: t(k), ACT.Identity, "ln3_g", "ln3_b")
        self.meet()
        return x_marks

    def taps(self, out, x, w, b, n_taps, *marks):
        if b is None:
            m = self.ts(out, x, w(n_taps - 1), None, ALU.mult, None, *marks)
        else:
            m = self.ts(out, x, w(n_taps - 1), b, ALU.mult, ALU.add, *marks)
        yield m
        for back in range(1, n_taps):
            m = self.stt(out[:, back:T], x[:, 0:T - back], w(n_taps - 1 - back), out[:, back:T], ALU.mult, ALU.add)
            yield m

    def mixer1(self, x_marks):
        t, S = self.t, self.scratch
        U, GLU, HB, XR, XC, GR, GA, GB = (lambda k, o=o: t(o + k) for o in (8, 16, 24, 32, 40, 48, 56, 64))
        u_marks = self.modulated(1, x_marks)
        glu_marks, hb_marks = [None] * KD, [None] * KD

        def conf_conv():
            for k in range(KD):
                for m in self.taps(HB(k), GLU(k), lambda j, k=k: self.v("conf_dw_w", j * 8 + k),
                                   self.v("conf_dw_b", k), CONF_TAPS, glu_marks[k]):
                    yield
                hb_marks[k] = m
        conv = conf_conv()

        def glu():
            tmp_read = [None, None]
            for k in range(KD):
                n, gate = self.lin.take()
                gm = self.product(gate, "w_in", 24 + k, U, u_marks, KD)
                n2, val = self.lin.take()
                vm = self.product(val, "w_in", 16 + k, U, u_marks, KD)
                a = self.act(S[:, k % 2, :], gate, ACT.Sigmoid, gm, tmp_read[k % 2])
                self.lin.free[n] = a
                glu_marks[k] = tmp_read[k % 2] = self.lin.free[n2] = self.tt(GLU(k), S[:, k % 2, :], val, ALU.mult,
                                                                             a, vm)
                yield
        for k, _ in enumerate(glu()):
            for _ in range(14 if k else 0):
                next(conv)

        xr_marks = [None] * KD

        def raw(dst, marks):
            def evacuate(f, bank, m):
                k = f % KD
                marks[k] = self.act(dst(k), bank, ACT.Copy, m)
                return marks[k]
            return evacuate
        xc_marks = [None] * KD
        for f, _ in enumerate(self.linear("w_in", range(0, 8), U, u_marks, KD, raw(XR, xr_marks))):
            for m in self.taps(XC(f), XR(f), lambda j, f=f: self.v("rnn_conv_w", j * 8 + f), self.v("rnn_conv_b", f), 4,
                               xr_marks[f]):
                xc_marks[f] = m
            for _ in range(6):
                next(conv, None)

        for k0, name, dst, bias in ((0, "rglru_w_r", XR, "rglru_b_r"), (0, "rglru_w_i", GB, "rglru_b_i")):
            w, loaded, slot = self.unit([(name, k, 0) for k in range(KD)])
            self.PE.wait(loaded)
            for k in range(KD):
                n, bank = self.mat.take()
                m = self.mm(bank, w[:, k * P:(k + 1) * P], XC(k), True, True, xc_marks[k], step=True)
                self.mat.free[n] = self.act(dst(k), bank, ACT.Sigmoid, m, xc_marks[k], bias=self.v(bias, k))
            self.release(slot, m)

        lam = self.vec[:, VCOL["rglru_lambda"]:VCOL["rglru_lambda"] + 8]
        rate = self.small[:, 8:16]
        neg_rate = self.small[:, 16:24]
        self.softplus(rate, lam, -1.0, self.small[:, 24:64], 8, P)
        self.ts(rate, rate, 8.0, None, ALU.mult, None)
        rate_mark = self.ts(neg_rate, rate, -1.0, None, ALU.mult, None)

        gr_marks = [None] * KD
        hr_marks = [None] * KD

        def lru():
            for k in range(KD):
                self.act(GA(k), XR(k), ACT.Exp, rate_mark, scale=neg_rate[:, k:k + 1])
                a = self.act(XR(k), XR(k), ACT.Tanh, scale=rate[:, k:k + 1])
                q = self.tt(S[:, 2, :], GA(k), GA(k), ALU.mult, a)
                self.stt(XR(k), S[:, 2, :], 1.0, XR(k), ALU.add, ALU.mult)
                yield
            q = self.VE.last()
            for k in range(KD):
                a = self.act(XR(k), XR(k), ACT.Sqrt, q)
                self.tt(GB(k), GB(k), XC(k), ALU.mult)
                self.tt(GB(k), GB(k), XR(k), ALU.mult, a)
                hr_marks[k] = self.scan(XC(k), GA(k), GB(k))
                yield
        scan = lru()
        for _ in self.linear("w_in", range(8, 16), U, u_marks, KD, raw(GR, gr_marks)):
            for _ in range(2):
                next(scan, None)
            for _ in range(5):
                next(conv, None)
        drain(scan)
        scan_done = self.VE.last()

        def gate(dst):
            def evacuate(f, bank, m):
                return self.act(dst(f % KD), bank, ACT.Sigmoid, m, scan_done)
            return evacuate
        for _ in self.linear("w_in", range(32, 40), U, u_marks, KD, gate(GA)):
            for _ in range(6):
                next(conv, None)
        for _ in self.linear("w_in", range(40, 48), U, u_marks, KD, gate(GB)):
            for _ in range(6):
                next(conv, None)
        for k in range(KD):
            a = self.act(GR(k), GR(k), ACT.Gelu_apprx_tanh)
            gr_marks[k] = self.tt(GR(k), GR(k), XC(k), ALU.mult, a)
        drain(conv)

        ya_marks, yb_marks, mix_marks = [None] * KD, [None] * KD, [None] * KD

        def scale_by(dst, marks):
            def evacuate(f, bank, m):
                marks[f] = self.tt(dst(f), dst(f), bank, ALU.mult, m)
                return marks[f]
            return evacuate
        hb_marks = self.layer_norm(HB, hb_marks, HB, ACT.Silu, "conf_ln_g", "conf_ln_b")
        drain(self.linear("rnn_w_proj", range(8), GR, gr_marks, KD, scale_by(GA, ya_marks)))
        base = [self.ts(GLU(k), self.t(k), ALPHA, None, ALU.mult, None, hb_marks[k], lane=self.GP) for k in range(KD)]
        for f, _ in enumerate(self.linear("conf_w_proj", range(8), HB, hb_marks, KD, scale_by(GB, yb_marks))):
            mix_marks[f] = self.tt(U(f), GA(f), GB(f), ALU.add, yb_marks[f], lane=self.GP)
        evac, pm = self.residual(1, GLU, base)
        drain(self.linear("mix_w_out", range(8), U, mix_marks, KD, evac))
        return self.layer_norm(GLU, pm, lambda k: self.t(k), ACT.Identity, "ln2_g", "ln2_b")

    def softplus(self, out, x, sign, tmp, n, rows, *marks):
        R = slice(0, rows)
        e, u, d, z = (tmp[R, i * n:(i + 1) * n] for i in range(4))
        a = self.act(e, x, ACT.Abs, *marks, self.VE.last())
        a = self.act(e, e, ACT.Exp, scale=-1.0)
        m = self.ts(u, e, 1.0, None, ALU.add, None, a)
        a = self.act(out, u, ACT.Ln, m)
        self.ts(d, u, 1.0, None, ALU.subtract, None)
        self.ts(z, d, 0.0, None, ALU.is_equal, None)
        self.tt(d, d, z, ALU.add)
        self.tt(out, out, z, ALU.add, a)
        self.tt(out, out, e, ALU.mult)
        m = self.VE.step(lambda e_: e_.reciprocal(d, d))
        self.tt(out, out, d, ALU.mult)
        self.ts(u, x, sign, 0.0, ALU.mult, ALU.max)
        return self.tt(out, out, u, ALU.add)

    def block2(self, x_marks):
        t, S = self.t, self.scratch
        U = lambda k: t(8 + k)
        self.U = U
        self.um = um = self.rms_norm(lambda k: t(k), x_marks, U, "mix_norm_g_2")
        n_in = "w_in_2"
        GQ, GK, GV, GRR, AQ, AK, AV, DQ, DKk, DV, DZ, MERGE = 0, 4, 8, 12, 16, 20, 24, 28, 32, 36, 40, 44

        def evac_to(dst, marks, func=ACT.Copy, scale=1.0):
            def evacuate(f, bank, m):
                k = f % 4
                marks[k] = self.act(dst(k), bank, func, m, scale=scale)
                return marks[k]
            return evacuate
        Q, K, V, R = (lambda k, o=o: t(o + k) for o in (28, 32, 36, 40))
        qm, km, vm, rm = ([None] * 4 for _ in range(4))
        lr = S[0:16, 4, :]
        lr_mark = self.narrow(lr, 0, 16, U, um, ACT.Copy)
        drain(self.linear(n_in, range(GQ, GQ + 4), U, um, KD, evac_to(Q, qm, scale=DK ** -0.5)),
              self.linear(n_in, range(GK, GK + 4), U, um, KD, evac_to(K, km)),
              self.token_major(n_in, GV, U, um, V, vm),
              self.linear(n_in, range(GRR, GRR + 4), U, um, KD, evac_to(R, rm, ACT.Silu)))
        AQt, AKt, AVt = (lambda k, o=o: t(o + k) for o in (57, 61, 65))
        aqm, akm, avm = ([None] * 4 for _ in range(3))

        def att_inputs():
            yield from self.linear(n_in, range(AQ, AQ + 4), U, um, KD, evac_to(AQt, aqm))
            yield from self.linear(n_in, range(AK, AK + 4), U, um, KD, evac_to(AKt, akm))
            yield from self.token_major(n_in, AV, U, um, AVt, avm)
        fill = att_inputs()
        pump(self.gla(Q, K, V, R, qm, km, vm, rm, lr, lr_mark), fill, 3)
        drain(fill)
        met = self.meet()
        toep = self.load(t(28, 8), self.dram["rel_rows"].rearrange("p (h m) -> p h m", m=T), *met)
        for lane in (self.VE, self.GP):
            lane.wait(toep)
        GD = [36, 37, 38, 39, 40, 41, 42, 43, 52, 53, 54, 55, 56, 69, 70, 71]
        Dt = lambda k: t(GD[k])
        dm = [None] * 16

        def gdn_inputs():
            def evacuate(f, bank, m):
                k = f - DQ
                dm[k] = self.act(Dt(k), bank, ACT.Copy, m)
                return dm[k]
            yield from self.linear(n_in, range(DQ, DQ + 16), U, um, KD, evacuate)
        fill = gdn_inputs()
        pump(self.attention(AQt, AKt, AVt, aqm, akm, avm), fill, 2)
        drain(fill)
        self.meet()
        self.Ym = [None] * KD
        Yt = lambda k: t(64 + k)
        fill = self.merge(Yt, [(0, 16), (1, 20)], MERGE)
        mv = [self.ts(t(b), t(a), 1.0, None, ALU.mult, None, lane=self.GP) for a, b in ((69, 28), (70, 29), (71, 30))]
        for i, b in zip((13, 14, 15), (28, 29, 30)):
            GD[i] = b
        self.PE.wait(mv[-1]); self.AC.wait(mv[-1]); self.VE.wait(mv[-1])
        pump(self.gdn(Dt), fill, 2)
        drain(fill)
        self.meet()
        drain(self.merge(Yt, [(2, 24)], MERGE))
        ym = self.Ym
        xm = [None] * KD

        def add_x(f, bank, m):
            xm[f] = self.tt(t(f), t(f), bank, ALU.add, m)
            return xm[f]
        drain(self.linear("w_out_2", range(8), Yt, ym, KD, add_x))
        um = self.rms_norm(lambda k: t(k), xm, U, "ffn_norm_g_2")
        x2 = [None] * KD

        def add_x2(f, bank, m):
            x2[f] = self.tt(t(f), t(f), bank, ALU.add, m)
            return x2[f]
        self.meet()
        drain(self.swiglu(U, um, ("w_ffn_in_2", 0), ("w_ffn_in_2", KF), "w_ffn_out_2", 24, add_x2))
        xm = self.rms_norm(lambda k: t(k), x2, lambda k: t(k), "final_norm_g_2")
        self.meet()
        return xm

    def narrow(self, out, c0, width, U, um, func, scale=1.0):
        n, bank = self.mat.take()
        for k in range(KD):
            m = self.mm(bank[0:width, :], self.small_w[:, k, c0:c0 + width], U(k), k == 0, k == KD - 1, um[k],
                        step=(k == KD - 1))
        a = self.act(out, bank[0:width, :], func, m, self.VE.last(), scale=scale)
        self.mat.free[n] = a
        return a

    def merge(self, Yt, branches, merge0):
        tmp = self.scratch[:, 3, :]
        names = ("w_branch_gla_2", "w_branch_att_2", "w_branch_gdn_2")
        for f in range(KD):
            for br, o in branches:
                n, gbank = self.lin.take()
                gm = self.product(gbank, "w_in_2", merge0 + br * 8 + f, self.U, self.um, KD)
                n2, bank = self.lin.take()
                bm = self.product(bank, names[br], f, lambda k, o=o: self.t(o + k), None, 4)
                a = self.act(tmp, gbank, ACT.Sigmoid, gm, self.VE.last())
                self.lin.free[n] = a
                if br == 0:
                    b = self.tt(Yt(f), tmp, bank, ALU.mult, a, bm)
                    self.lin.free[n2] = b
                else:
                    b = self.tt(tmp, tmp, bank, ALU.mult, a, bm)
                    self.lin.free[n2] = b
                    b = self.tt(Yt(f), Yt(f), tmp, ALU.add)
                self.Ym[f] = b
                yield

    def head_norm(self, O, gate, out, g, sq, std, sq_free, *marks):
        a = self.act(sq, O, ACT.Square, *marks, sq_free)
        n, bank = self.mat.take()
        m = self.mm(bank, self.c("mean_head"), sq, True, True, a, step=True)
        r = self.inverse_std(bank, n, m, 1e-6, std, self.mat)
        self.stt(O, O, self.v(g), std, ALU.mult, ALU.mult, r)
        return self.tt(out, O, gate, ALU.mult)

    def gla(self, Q, K, V, R, qm, km, vm, rm, lr, lr_mark):
        t, S = self.t, self.scratch
        vw = self.VE
        G, A1, KDT, QG, KDc, O = t(44), t(45), t(52), t(55), t(56), t(51)
        E = [t(46), t(47)]
        QE = [t(48), t(49)]
        KE = [S[:, 0, :], S[:, 1, :]]
        ST = t(50)
        states = t(53, 2).rearrange("p a (c v) -> p (a c) v", v=P)
        pair = lambda x, p: x[:, p * P:(p + 1) * P]
        TMP = S[:, 2, :]
        for h in range(HEADS):
            n, bank = self.mat.take()
            m = self.mm(bank, self.gate_up[:, h * P:(h + 1) * P], lr, True, True, lr_mark, step=True)
            a = self.act(A1, bank, ACT.Abs, m, vw.last(), bias=self.v("gla_b_gate_2", h))
            b = self.ts(G, bank, self.v("gla_b_gate_2", h), 0.0, ALU.add, ALU.min, a)
            a = self.act(A1, A1, ACT.Exp, scale=-1.0)
            a = self.act(A1, A1, ACT.Ln, bias=self.unit_bias)
            self.mat.free[n] = b
            self.tt(A1, G, A1, ALU.subtract, a)
            self.scan(G, self.c("start64"), A1)
            gm = self.ts(G, G, 1.0 / 16.0, None, ALU.mult, None)
            yield
            n, bank = self.mat.take()
            for p in range(BLK):
                m = self.mm(pair(bank, p), pair(K(h), p), pair(Q(h), p), True, True, qm[h], km[h], step=(p == BLK - 1))
            diag = self.c("ident").unsqueeze(1).to_broadcast([P, BLK, P])
            wide = lambda x: x.rearrange("p (b i) -> p b i", i=P)
            sm = self.tt(wide(ST), wide(bank), diag, ALU.mult, m)
            self.mat.free[n] = sm
            yield
            mms = [None, None]
            for li, s in enumerate(LEVELS):
                i = li % 2
                g3 = G.rearrange("p (b s) -> p b s", s=2 * s)
                ref = g3[:, :, s - 1:s].to_broadcast([P, T // (2 * s), 2 * s])
                d3 = E[i].rearrange("p (b s) -> p b s", s=2 * s)
                b = self.tt(d3, g3, ref, ALU.subtract, mms[i])
                a = self.act(E[i], E[i], ACT.Abs, b)
                a = self.act(E[i], E[i], ACT.Exp, scale=-1.0)
                kb = self.tt(KE[i], K(h), E[i], ALU.mult, a, mms[i], lane=self.GP)
                qb = self.tt(QE[i], Q(h), E[i], ALU.mult, a)
                n, bank = self.mat.take()
                for p in range(BLK):
                    m = self.mm(pair(bank, p), pair(KE[i], p), pair(QE[i], p), True, True, kb, qb,
                                step=(p == BLK - 1))
                mms[i] = m
                mask = self.c(f"level{s}").unsqueeze(1).to_broadcast([P, BLK, P])
                b = self.tt(wide(TMP), wide(bank), mask, ALU.mult, m)
                self.mat.free[n] = b
                vw.wait(kb)
                sm = self.tt(ST, ST, TMP, ALU.add)
                yield
            a = self.act(QG, G, ACT.Exp, gm, self.PE.last())
            el = self.small[:, 64 + h * 8:64 + h * 8 + 8]
            self.copy(el, QG[:, CH - 1::CH], a)
            qg = self.tt(QG, Q(h), QG, ALU.mult)
            g3 = G.rearrange("p (c i) -> p c i", i=CH)
            k3 = KDc.rearrange("p (c i) -> p c i", i=CH)
            b = self.tt(k3, g3[:, :, CH - 1:CH].to_broadcast([P, NCH, CH]), g3, ALU.subtract, self.PE.last())
            a = self.act(KDc, KDc, ACT.Exp, b)
            b = self.tt(KDc, K(h), KDc, ALU.mult, a)
            n, bank = self.mat.take()
            for p in range(BLK):
                m = self.tr(pair(bank, p), pair(KDc, p), P, b, step=(p == BLK - 1))
            a = self.act(KDT, bank, ACT.Copy, m)
            self.mat.free[n] = a
            yield
            us = []
            for half in range(2):
                n, bank = self.mat.take()
                r = half * CH
                for c in range(half, NCH - 1, 2):
                    p = c // 2
                    m = self.mm(pair(bank, p), KDT[r:r + CH, p * P:(p + 1) * P], V(p)[r:r + CH, h * P:(h + 1) * P],
                                True, True, a, vm[p], step=(c + 2 >= NCH - 1))
                us.append((n, bank, m))
            for c in range(NCH - 1):
                n, bank, m = us[c % 2]
                u = pair(bank, c // 2)
                if c == 0:
                    b = self.copy(states[:, 1, :], u, m)
                else:
                    b = self.stt(states[:, c + 1, :], states[:, c, :], el[:, c:c + 1], u, ALU.mult, ALU.add, m)
                self.mat.free[n] = b
            yield
            n, bank = self.mat.take()
            for p in range(BLK):
                m = self.mm(pair(bank, p), V(p)[:, h * P:(h + 1) * P], pair(ST, p), True, False, sm, b)
                for c in (2 * p, 2 * p + 1):
                    if c:
                        m = self.mm(bank[:, c * CH:(c + 1) * CH], states[:, c, :], QG[:, c * CH:(c + 1) * CH], False,
                                    c % 2 == 1, qg, step=(c == NCH - 1))
            a = self.act(O, bank, ACT.Copy, m)
            self.mat.free[n] = a
            self.head_norm(O, R(h), t(16 + h), "gla_norm_g_2", A1, E[0], None, rm[h], a, self.VE.last())
            yield

    def attention(self, Q, K, V, qm, km, vm):
        t = self.t
        T8 = t(28, 8)
        SC = [t(44), t(45)]
        PT = [t(46), t(47)]
        stat = self.small[:, 96:256]
        self.VE.step(lambda e: e.memset(T8[0:CH, :, T - CH:T], NEG))
        self.PE.wait(*self.mat.free)
        obank, rotate, out_read = self.mat.aps[0], Banks(self.PE, []), None
        rotate.aps, rotate.free = self.mat.aps[1:], [None] * 3
        use = [None, None]
        ptm = [None, None]
        step = 0
        for h in range(ATT_HEADS):
            r0, tile = (h % 2) * ATT_HD, h // 2
            if h % 2 == 0:
                self.PE.wait(out_read)
            for it in range(BLK):
                n_keys = (it + 1) * P
                i = step % 2
                n, bank = rotate.take()
                m = self.mm(bank[:, 0:n_keys], Q(tile)[r0:r0 + ATT_HD, it * P:(it + 1) * P],
                            K(tile)[r0:r0 + ATT_HD, 0:n_keys], True, True, qm[tile], km[tile], step=True)
                sc = SC[i][:, 0:n_keys]
                self.stt(sc, bank[:, 0:n_keys], ATT_HD ** -0.5, T8[:, h, T - n_keys:T], ALU.mult, ALU.add, m, use[i])
                rotate.free[n] = self.VE.last()
                mx, tot = stat[:, 4 * step:4 * step + 1], stat[:, 4 * step + 1:4 * step + 2]
                self.VE.step(lambda e, mx=mx, sc=sc: e.tensor_reduce(mx, sc, AX.X, ALU.max))
                b = self.ts(mx, mx, -1.0, None, ALU.mult, None)
                a = self.act(sc, sc, ACT.Exp, b, bias=mx, total=tot)
                self.VE.step(lambda e, tot=tot: e.reciprocal(tot, tot), a)
                b = self.ts(sc, sc, tot, None, ALU.mult, None)
                n, bank = rotate.take()
                for j in range(it + 1):
                    m = self.tr(bank[:, j * P:(j + 1) * P], sc[:, j * P:(j + 1) * P], P, b, step=(j == it))
                use[i] = m
                a = self.act(PT[i][:, 0:n_keys], bank[:, 0:n_keys], ACT.Copy, m, ptm[i])
                rotate.free[n] = a
                for j in range(it + 1):
                    m = self.mm(obank[r0:r0 + ATT_HD, it * P:(it + 1) * P], V(j)[:, h * ATT_HD:(h + 1) * ATT_HD],
                                PT[i][:, j * P:(j + 1) * P], j == 0, j == it, a, vm[j], step=(j == it))
                ptm[i] = m
                step += 1
                yield
            if h % 2 == 1:
                out_read = self.act(t(20 + tile), obank, ACT.Copy, m)
        self.mat.free = [out_read] + rotate.free

    def gdn(self, Dt):
        t, S, VE = self.t, self.scratch, self.VE
        small = self.small
        pair = lambda x, p: x[:, p * P:(p + 1) * P]
        wide = lambda x: x.rearrange("p (b i) -> p b i", i=P)
        rows = t(31)[0:HEADS, :], t(32)[0:HEADS, :], t(33)[0:HEADS, :], t(34)[0:HEADS, :]
        g_row, beta_row, eg_row, ed_row = rows
        tmp = t(44, 4).rearrange("p a t -> p (a t)")
        am = self.narrow(S[0:4, 0, :], 16, 4, self.U, self.um, ACT.Copy)
        bm = self.narrow(beta_row, 20, 4, self.U, self.um, ACT.Sigmoid)
        self.ts(S[0:4, 0, :], S[0:4, 0, :], self.v("gdn_dt_bias_2", rows=4), None, ALU.add, None, am)
        self.softplus(g_row, S[0:4, 0, :], 1.0, tmp, T, 4)
        ea = small[0:4, 4:5]
        a = self.act(ea, self.v("gdn_a_log_2", rows=4), ACT.Exp, VE.last())
        self.ts(g_row, g_row, ea, -1.0, ALU.mult, ALU.mult, a)
        self.scan(S[0:4, 0, :], self.c("start64")[0:4, :], g_row)
        b = self.copy(g_row, S[0:4, 0, :])
        a = self.act(eg_row, g_row, ACT.Exp, b)
        g3 = g_row.rearrange("p (c i) -> p c i", i=CH)
        b = self.tt(ed_row.rearrange("p (c i) -> p c i", i=CH), g3[:, :, CH - 1:CH].to_broadcast([HEADS, NCH, CH]), g3,
                    ALU.subtract)
        a = self.act(ed_row, ed_row, ACT.Exp, b)
        n, bank = self.mat.take()
        for q in range(4):
            for p in range(BLK):
                c = (q * BLK + p) * HEADS
                m = self.tr(bank[:, c:c + HEADS], pair(rows[q], p), HEADS, a, b, bm, step=(q == 3 and p == BLK - 1))
        cols = small[:, 96:160].rearrange("p (q b h) -> p q b h", q=4, h=HEADS)
        b = self.copy(small[:, 96:160], bank[:, 0:64], m)
        self.mat.free[n] = b
        bg = small[:, 160:176].rearrange("p (b h) -> p b h", h=HEADS)
        cm = self.tt(bg, cols[:, 1], cols[:, 2], ALU.mult)
        yield
        for k in range(12):
            tm = [S[:, 0, :], S[:, 1, :]][k % 2]
            for _ in self.taps(tm, Dt(k), lambda j, k=k: self.v("gdn_conv_w_2", j * 12 + k), None, 4, self.AC.last(),
                               self.PE.last()):
                pass
            a = self.act(Dt(k), tm, ACT.Silu, VE.last())
            if k % 3 == 2:
                yield
        for k in range(12, 16):
            self.act(Dt(k), Dt(k), ACT.Silu)
        for k in range(8):
            a = self.act(S[:, k % 2, :], Dt(k), ACT.Square, self.PE.last())
            n, bank = self.mat.take()
            m = self.mm(bank, self.c("one"), S[:, k % 2, :], True, True, a, step=True)
            r = self.inverse_std(bank, n, m, 1e-6, S[:, 2, :], self.mat)
            b = self.stt(Dt(k), Dt(k), DK ** -0.5 if k < 4 else 1.0, S[:, 2, :], ALU.mult, ALU.mult)
            if k % 4 == 3:
                yield
        WT = lambda h: t(44 + h)
        AT_N = lambda h: t(48 + h)
        UV = t(57, 4)
        KDT = t(35), t(61), t(62), t(63)
        TT, TI, PM = S[:, 0, :], S[:, 1, :], S[:, 2, :]
        elast = small[:, 176:208].rearrange("p (h c) -> p h c", h=HEADS)
        AMAT, KB, GAM = t(24), t(25), t(26)
        AM = [t(27), S[:, 4, :]]
        for h in range(HEADS):
            q, k, v = Dt(h), Dt(4 + h), Dt(8 + h)
            sel = self.c("ident")[0:HEADS, h:h + 1].to_broadcast([HEADS, P])

            def row(x):
                n, bank = self.mat.take()
                return n, bank, self.mm(bank, sel, x, True, True, cm, step=True)
            n, bank, m = row(beta_row)
            kb = self.tt(KB, k, bank, ALU.mult, m)
            self.mat.free[n] = kb
            n, bank, m = row(g_row)
            for p in range(BLK):
                b = self.ts(pair(GAM, p), pair(bank, p), cols[:, 0, p, h:h + 1], 0.0, ALU.subtract, ALU.min, m)
            self.mat.free[n] = b
            a = self.act(GAM, GAM, ACT.Exp, b)
            incl = self.c("incl64").unsqueeze(1).to_broadcast([P, BLK, P])
            strict = self.c("strict64").unsqueeze(1).to_broadcast([P, BLK, P])
            self.tt(wide(GAM), wide(GAM), incl, ALU.mult, a)
            n, bank = self.mat.take()
            for p in range(BLK):
                m = self.mm(pair(bank, p), pair(k, p), pair(KB, p), True, True, kb, step=(p == BLK - 1))
            self.tt(AMAT, bank, GAM, ALU.mult, m)
            self.mat.free[n] = self.VE.last()
            am = self.tt(wide(AMAT), wide(AMAT), strict, ALU.mult)
            n, bank = self.mat.take()
            for p in range(BLK):
                m = self.mm(pair(bank, p), pair(k, p), pair(q, p), True, True, step=(p == BLK - 1))
            at = self.tt(AT_N(h), bank, GAM, ALU.mult, m)
            self.mat.free[n] = at
            ident = self.c("ident").unsqueeze(1).to_broadcast([P, BLK, P])
            self.copy(wide(TI), ident, self.PE.last(), self.AC.last())
            tm = self.copy(wide(TT), ident)
            a_read = [None, None]
            yield
            for li, s in enumerate(reversed(LEVELS)):
                i = li % 2
                mask = self.c(f"level{s}").unsqueeze(1).to_broadcast([P, BLK, P])
                g = self.tt(wide(AM[i]), wide(AMAT), mask, ALU.mult, am, a_read[i], lane=self.GP)
                n, bank = self.mat.take()
                for p in range(BLK):
                    m = self.mm(pair(bank, p), pair(AM[i], p), pair(TI, p), True, True, g, tm, step=(p == BLK - 1))
                a_read[i] = m
                a = self.act(PM, bank, ACT.Copy, m, self.PE.last())
                self.mat.free[n] = a
                n, bank = self.mat.take()
                n2, bank2 = self.mat.take()
                for p in range(BLK):
                    self.mm(pair(bank, p), pair(TT, p), pair(PM, p), True, True, a)
                for p in range(BLK):
                    m = self.mm(pair(bank2, p), pair(PM, p), pair(TT, p), True, True, step=(p == BLK - 1))
                self.mat.free[n] = self.tt(TI, TI, bank, ALU.subtract, m)
                self.mat.free[n2] = tm = self.tt(TT, TT, bank2, ALU.subtract)
                yield
            n, bank = self.mat.take()
            for p in range(BLK):
                m = self.tr(pair(bank, p), pair(k, p), P, step=(p == BLK - 1))
            col = lambda x: x[:, :, h:h + 1].to_broadcast([P, BLK, P])
            kbe = self.tt(wide(KB), wide(bank), col(bg), ALU.mult, m)
            kd = self.tt(wide(KDT[h]), wide(bank), col(cols[:, 3]), ALU.mult)
            self.mat.free[n] = kd
            n, bank = self.mat.take()
            for p in range(BLK):
                m = self.tr(pair(bank, p), pair(v, p), P, step=(p == BLK - 1))
            vb = self.tt(wide(GAM), wide(bank), col(cols[:, 1]), ALU.mult, m)
            self.mat.free[n] = vb
            n, bank = self.mat.take()
            for p in range(BLK):
                m = self.mm(pair(bank, p), pair(TT, p), pair(GAM, p), True, True, vb, tm, step=(p == BLK - 1))
            self.mat.free[n] = self.act(UV[:, h, :], bank, ACT.Copy, m)
            n, bank = self.mat.take()
            for p in range(BLK):
                m = self.mm(pair(bank, p), pair(KB, p), pair(TT, p), True, True, step=(p == BLK - 1))
            self.mat.free[n] = self.act(WT(h), bank, ACT.Copy, m)
            n, bank, m = row(eg_row)
            self.copy(elast[:, h, :], bank[:, CH - 1::CH], m)
            self.mat.free[n] = self.tt(q, q, bank, ALU.mult)
            yield
        states = [AMAT, KB, GAM, AM[0]]
        st = lambda c: states[c % 4]
        O = [Dt(8 + h) for h in range(HEADS)]
        O4 = t(52, 4)
        UV5 = UV.rearrange("p h (b v) -> p h b v", v=P)
        b = self.VE.last()
        for c in range(NCH):
            r, p = (c % 2) * CH, c // 2
            if c:
                n, bank = self.mat.take()
                for h in range(HEADS):
                    m = self.mm(bank[r:r + CH, h * P:(h + 1) * P], WT(h)[:, p * P + r:p * P + r + CH],
                                st(c)[:, h * P:(h + 1) * P], True, True, b, self.AC.last(), step=(h == HEADS - 1))
                b = self.tt(UV5[r:r + CH, :, p, :], UV5[r:r + CH, :, p, :], wide(bank)[r:r + CH], ALU.subtract, m)
                self.mat.free[n] = b
            else:
                b = self.AC.last()
            if c < NCH - 1:
                n, bank = self.mat.take()
                for h in range(HEADS):
                    m = self.mm(bank[:, h * P:(h + 1) * P], KDT[h][r:r + CH, p * P:(p + 1) * P],
                                UV[r:r + CH, h, p * P:(p + 1) * P], True, True, b, step=(h == HEADS - 1))
                if c == 0:
                    b = self.copy(st(c + 1), bank, m)
                else:
                    e4 = elast[:, :, c:c + 1].to_broadcast([P, HEADS, P])
                    self.tt(wide(st(c + 1)), wide(st(c)), e4, ALU.mult, self.PE.last())
                    b = self.tt(st(c + 1), st(c + 1), bank, ALU.add, m)
                self.mat.free[n] = b
            if c % 2 == 1:
                n, bank = self.mat.take()
                for h in range(HEADS):
                    self.mm(pair(bank, h), UV[:, h, p * P:(p + 1) * P], pair(AT_N(h), p), True, False, b)
                    for cc in (c - 1, c):
                        if cc:
                            m = self.mm(bank[:, h * P + (cc % 2) * CH:h * P + (cc % 2 + 1) * CH],
                                        st(cc)[:, h * P:(h + 1) * P], Dt(h)[:, cc * CH:(cc + 1) * CH], False,
                                        cc == c, step=(h == HEADS - 1 and cc == c))
                a = self.act(O4[:, :, p * P:(p + 1) * P], wide(bank), ACT.Copy, m)
                self.mat.free[n] = a
            yield
        for h in range(HEADS):
            self.head_norm(O[h], Dt(12 + h), t(24 + h), "gdn_norm_g_2", S[:, 0, :], S[:, 1, :], None,
                           self.VE.last(), self.PE.last())
        yield

    def block3(self, x_marks):
        t, S, VE = self.t, self.scratch, self.VE
        small = self.small
        U = lambda k: t(8 + k)
        um = self.rms_norm(lambda k: t(k), x_marks, U, "norm_mix_g_3")
        name = "w_in_3"
        UU, VV, ZZ, XS, BM, CM, GATE = 0, 8, 16, 32, 48, 56, 64
        YA = lambda k: t(16 + k)
        VN = lambda k: t(24 + k)
        YB = lambda k: t(32 + k)
        sp = self.load(t(48, 2).rearrange("p a (g i) -> p (a g) i", i=P), self.dram["w_spatial_T"]
                       .rearrange("p (g i) -> p g i", i=P), self.met)
        bs = self.load(t(50, 2).rearrange("p a t -> p (a t)"), self.dram["b_spatial_rows"], self.met)
        vmk, umk = [None] * KD, [None] * KD

        def gelu_to(dst, marks):
            def evacuate(f, bank, m):
                marks[f % KD] = self.act(dst(f % KD), bank, ACT.Gelu, m)
                return marks[f % KD]
            return evacuate
        drain(self.linear(name, range(VV, VV + 8), U, um, KD, gelu_to(VN, vmk)))
        vm = self.layer_norm(VN, vmk, VN, ACT.Identity, "v_norm_g_3", "v_norm_b_3")
        drain(self.linear(name, range(UU, UU + 8), U, um, KD, gelu_to(YA, umk)))

        def spatial():
            WS = t(48, 2).rearrange("p a (g i) -> p (a g) i", i=P)
            BS = t(50, 2).rearrange("p a (g i) -> p (a g) i", i=P)
            causal = self.c("causal").unsqueeze(1).to_broadcast([P, KD, P])
            wm = self.tt(WS, WS, causal, ALU.mult, sp, bs)
            for g in range(KD):
                n, bank = self.mat.take()
                for c in range(BLK):
                    m = self.tr(bank[:, c * P:(c + 1) * P], VN(g)[:, c * P:(c + 1) * P], P, vm[g], step=(c == BLK - 1))
                vt = S[:, 3 + g % 2, :]
                a = self.act(vt, bank, ACT.Copy, m, self.PE.last())
                self.mat.free[n] = a
                n, bank = self.mat.take()
                for c in range(BLK):
                    m = self.mm(bank[:, c * P:(c + 1) * P], vt[:, c * P:(c + 1) * P], WS[:, g, :], True, True, a, wm,
                                step=(c == BLK - 1))
                w3 = lambda x: x.rearrange("p (b i) -> p b i", i=P)
                b = self.tt(w3(VN(g)), w3(bank), BS[:, g:g + 1, :].to_broadcast([P, BLK, P]), ALU.add, m)
                self.mat.free[n] = b
                self.tt(YA(g), YA(g), VN(g), ALU.mult, umk[g])
                yield
        drain(spatial())
        self.meet()
        DT, CS, DD = t(24)[0:MH, :], t(25)[0:MH, :], t(26)[0:MH, :]
        raw = t(27)[0:MH, :]
        a = self.narrow(raw, 24, MH, U, um, ACT.Copy)
        self.ts(raw, raw, self.v("dt_bias_3", rows=MH), None, ALU.add, None, a)
        self.softplus(DT, raw, 1.0, t(28, 4).rearrange("p a t -> p (a t)"), T, MH)
        ea = small[0:MH, 4:5]
        a = self.act(ea, self.v("a_log_3", rows=MH), ACT.Exp, VE.last())
        self.ts(raw, DT, ea, -1.0, ALU.mult, ALU.mult, a)
        self.scan(CS, self.c("start128")[0:MH, :], raw)
        c3 = CS.rearrange("p (c i) -> p c i", i=P)
        b = self.tt(DD.rearrange("p (c i) -> p c i", i=P), c3[:, :, P - 1:P].to_broadcast([MH, BLK, P]), c3,
                    ALU.subtract)
        a = self.act(DD, DD, ACT.Exp, b)
        b = self.tt(DD, DD, DT, ALU.mult, a)
        n, bank = self.mat.take()
        for q, x in enumerate((DT, CS, DD)):
            for c in range(BLK):
                o = (q * BLK + c) * MH
                m = self.tr(bank[:, o:o + MH], x[:, c * P:(c + 1) * P], MH, b, step=(q == 2 and c == BLK - 1))
        b = self.copy(t(27)[:, 0:384], bank[:, 0:384], m)
        self.mat.free[n] = b
        self.mcols = t(27)[:, 0:384].rearrange("p (q c h) -> p q c h", q=3, h=MH)
        self.cs_rows = CS
        self.PE.wait(b); self.AC.wait(b); self.GP.wait(b)

        ins = [[t(48 + 12 * i + j) for j in range(6)] for i in range(2)]
        free = [None, None]

        def inputs(g):
            x0, x1, bb, cc, z0, z1 = ins[g % 2]
            tiles = [(XS + 2 * g, x0, 2 * g), (XS + 2 * g + 1, x1, 2 * g + 1), (BM + g, bb, 16 + g),
                     (CM + g, cc, 24 + g), (ZZ + 2 * g, z0, None), (ZZ + 2 * g + 1, z1, None)]
            for f, dst, ch in tiles:
                n, bank = self.lin.take()
                m = self.product(bank, name, f, U, um, KD)
                if ch is None:
                    self.lin.free[n] = self.act(dst, bank, ACT.Silu, m, free[g % 2])
                else:
                    tm = S[:, ch % 2, :]
                    tm2 = dst
                    a = self.act(tm, bank, ACT.Copy, m, self.VE.last())
                    self.lin.free[n] = a
                    for _ in self.taps(tm2, tm, lambda j, ch=ch: self.v("conv_w_3", j * 32 + ch),
                                       self.v("conv_b_3", ch), 4, a, free[g % 2]):
                        pass
                    self.act(dst, dst, ACT.Silu, self.VE.last())
                yield
        drain(inputs(0))
        for g in range(MG):
            nxt = inputs(g + 1) if g + 1 < MG else iter(())
            ready = [self.AC.last(), self.VE.last()]
            pump(self.ssd_group(g, ins[g % 2], YB, ready), nxt, 2)
            free[g % 2] = [self.PE.last(), self.VE.last(), self.AC.last(), self.GP.last()]
            drain(nxt)
        self.meet()
        M = lambda k: t(48 + k)
        mm = [None] * KD
        for f in range(KD):
            parts = []
            for br, (pname, src, kts) in enumerate((("w_proj_a_3", YA, KD), ("w_proj_b_3", YB, 2 * KD))):
                n, gbank = self.lin.take()
                gm = self.product(gbank, name, GATE + br * 8 + f, U, um, KD)
                n2, bank = self.lin.take()
                bm = self.product(bank, pname, f, src, None, kts)
                tmp = S[:, 3 + br, :]
                a = self.act(tmp, gbank, ACT.Sigmoid, gm, self.VE.last(), bias=self.v("b_gates_3", br * 8 + f))
                self.lin.free[n] = a
                dst = M(f) if br == 0 else tmp
                self.lin.free[n2] = self.tt(dst, tmp, bank, ALU.mult, a, bm)
            mm[f] = self.tt(M(f), M(f), S[:, 4, :], ALU.add)
        xm = [None] * KD

        def add_x(f, bank, m):
            xm[f] = self.tt(t(f), t(f), bank, ALU.add, m)
            return xm[f]
        drain(self.linear("w_out_3", range(8), M, mm, KD, add_x))
        um = self.rms_norm(lambda k: t(k), xm, U, "norm_mlp_g_3")
        hm = [None] * 32
        self.meet()

        def relu2(f, bank, m):
            a = self.act(S[:, f % 2, :], bank, ACT.Relu, m, hm[f - 2] if f > 1 else None)
            hm[f] = self.tt(t(24 + f), S[:, f % 2, :], bank, ALU.mult, a)
            return hm[f]
        drain(self.linear("w_mlp_up_3", range(32), U, um, KD, relu2))
        x2 = [None] * KD

        def add_x2(f, bank, m):
            x2[f] = self.tt(t(f), t(f), bank, ALU.add, m)
            return x2[f]
        drain(self.linear("w_mlp_down_3", range(8), lambda k: t(24 + k), hm, 32, add_x2))
        return self.rms_norm(lambda k: t(k), x2, lambda k: t(8 + k), "norm_final_g_3")

    def ssd_group(self, g, tiles, YB, ready):
        t, S, VE = self.t, self.scratch, self.VE
        x0, x1, BMt, CMt, z0, z1 = tiles
        cols = self.mcols
        blk = lambda x, c: x[:, c * P:(c + 1) * P]
        wide = lambda x: x.rearrange("p (b i) -> p b i", i=P)
        CB, BT = t(54), t(55)
        XD = t(56, 2).rearrange("p a (c f) -> p (a c) f", f=256)
        XE = t(58, 2).rearrange("p a (c f) -> p (a c) f", f=256)
        L = [t(66), t(67)]
        CE = [t(68), t(69)]
        HS = t(70, 2).rearrange("p a (c f) -> p (a c) f", f=256)
        dec = self.small[:, 208:224].rearrange("p (h c) -> p h c", h=MHG)
        n, bank = self.mat.take()
        for c in range(BLK):
            m = self.mm(blk(bank, c), blk(BMt, c), blk(CMt, c), True, True, *ready, step=(c == BLK - 1))
        causal = self.c("causal").unsqueeze(1).to_broadcast([P, BLK, P])
        cb = self.tt(wide(CB), wide(bank), causal, ALU.mult, m)
        self.mat.free[n] = cb
        n, bank = self.mat.take()
        for c in range(BLK):
            m = self.tr(blk(bank, c), blk(BMt, c), P, step=(c == BLK - 1))
        bt = self.act(BT, bank, ACT.Copy, m)
        self.mat.free[n] = bt
        yield
        for i, x in enumerate((x0, x1)):
            n, bank = self.mat.take()
            for c in range(BLK):
                m = self.tr(blk(bank, c), blk(x, c), P, step=(c == BLK - 1))
            x4 = bank.rearrange("p (c e f) -> p c e f", c=BLK, e=2)
            h0 = 4 * g + 2 * i
            for q, dst in ((0, XD), (2, XE)):
                col = cols[:, q, :, h0:h0 + 2].unsqueeze(3).to_broadcast([P, BLK, 2, MP])
                d4 = dst[:, :, i * P:(i + 1) * P].rearrange("p c (e f) -> p c e f", e=2)
                xe = self.tt(d4, x4, col, ALU.mult, m)
            self.mat.free[n] = xe
        yield
        sts = []
        for c in range(BLK - 1):
            if c % 2 == 0:
                n, bank = self.mat.take()
            m = self.mm(bank[:, (c % 2) * 256:(c % 2 + 1) * 256], blk(BT, c), XE[:, c, :], True, True, xe, bt,
                        step=True)
            sts.append((n, bank, m))
        rows_bank = {}
        ms = {}
        for hh in range(MHG):
            head = 4 * g + hh
            i = hh % 2
            n, bank = self.lin.take()
            sel = self.c("ident")[0:MH, head:head + 1].to_broadcast([MH, P])
            m = self.mm(bank, sel, self.cs_rows, True, True, step=True)
            a = self.act(CE[i], bank, ACT.Exp, m, ms.get(hh - 2))
            b = self.copy(dec[:, hh, :], CE[i][:, P - 1::P], a)
            for c in range(BLK):
                b = self.ts(blk(L[i], c), blk(bank, c), cols[:, 1, c, head:head + 1], 0.0, ALU.subtract, ALU.min, m,
                            ms.get(hh - 2))
            self.lin.free[n] = b
            a = self.act(L[i], L[i], ACT.Exp, b)
            ce = self.tt(CE[i], CE[i], CMt, ALU.mult, b, lane=self.GP)
            lm = self.tt(L[i], L[i], CB, ALU.mult, a)
            hsl = slice(hh * MP, (hh + 1) * MP)
            for c in range(BLK - 1):
                ns, sbank, sm = sts[c]
                s = sbank[:, (c % 2) * 256 + hh * MP:(c % 2) * 256 + (hh + 1) * MP]
                if c == 0:
                    hb = self.copy(HS[:, 1, hsl], s, sm)
                else:
                    hb = self.stt(HS[:, c + 1, hsl], HS[:, c, hsl], dec[:, hh, c:c + 1], s, ALU.mult, ALU.add, sm)
                self.mat.free[ns] = hb
            if i == 0:
                yn, ybank = self.mat.take()
            r = i * MP
            for c in range(BLK):
                m = self.mm(blk(ybank, c)[r:r + MP], XD[:, c, hsl], blk(L[i], c), True, c == 0, lm, ce, hb)
                if c:
                    m = self.mm(blk(ybank, c)[r:r + MP], HS[:, c, hsl], blk(CE[i], c), False, True,
                                step=(c == BLK - 1))
            ms[hh] = m
            if i == 1:
                k = hh // 2
                y = YB(2 * g + k)
                x, z = (x0, x1)[k], (z0, z1)[k]
                b = self.stt(y, x, self.v("d_skip_3", 2 * g + k), ybank, ALU.mult, ALU.add, m)
                self.mat.free[yn] = b
                self.tt(y, y, z, ALU.mult)
            yield
        n, bank = self.mat.take()
        for k in range(2):
            a = self.act(S[:, 3 + k, :], YB(2 * g + k), ACT.Square, VE.last(), self.PE.last())
            m = self.mm(bank, self.c("mean_group"), S[:, 3 + k, :], k == 0, k == 1, a, step=True)
        r = self.inverse_std(bank, n, m, 1e-6, S[:, 2, :], self.mat)
        for k in range(2):
            self.stt(YB(2 * g + k), YB(2 * g + k), self.v("ssm_norm_g_3", 2 * g + k), S[:, 2, :], ALU.mult, ALU.mult, r)
        yield

    def build(self):
        nc = self.nc
        self.setup()
        x_marks = self.block1()
        self.dbg(x_marks, 0)
        x_marks = self.block2(x_marks)
        self.dbg(x_marks, 1)
        self.met = self.meet()
        om = self.block3(x_marks)
        out_sem = nc.alloc_semaphore("stored")
        o = self.dram["out"].rearrange("p (k t) -> p k t", k=KD)
        self.SP.issue(lambda e: e.dma_start(o, self.t(8, 8)).then_inc(out_sem, 16), *om)
        self.SP.wait(("stored", out_sem, 16))
        with nc.Block() as block:
            @block.tensor
            def _(e):
                self.PE.run(e)

            @block.scalar
            def _(e):
                self.AC.run(e)

            @block.vector
            def _(e):
                self.VE.run(e)

            @block.gpsimd
            def _(e):
                self.GP.run(e)

            @block.sync
            def _(e):
                self.SP.run(e)
        return self.plan

    def dbg(self, marks, i):
        pass


INPUTS = [("x", (P, KD * T)), ("c", (1, D)), ("vectors", (P, NVEC)), ("constants", (P, NCONST)),
          ("small_weights", (P, KD * 64)), ("gla_w_gate_up", (16, T)), ("rel_rows", (P, ATT_HEADS * T)),
          ("w_spatial_T", (P, KD * P)), ("b_spatial", (1, KD * P))]


def build_program(nc, out_shape=(P, KD * T)):
    dram = {name: nc.dram_tensor(name, shape, F32, kind="ExternalInput").ap() for name, shape in INPUTS}
    n_blocks = weight_blocks()
    dram["weights"] = nc.dram_tensor("weights", (n_blocks * P * P,), F32, kind="ExternalInput").ap()
    dram["out"] = nc.dram_tensor("out", out_shape, F32, kind="ExternalOutput").ap()
    dram["c_rows"] = bass.AP(dram["c"].tensor, 0, [[0, P], [1, D]])
    dram["b_spatial_rows"] = bass.AP(dram["b_spatial"].tensor, 0, [[0, P], [1, KD * P]])
    plan = Program(nc, dram).build()
    assert sum(map(len, plan)) == n_blocks
    return plan


def weight_blocks():
    swiglu = 3 * KD * KF
    one = 72 * KD + 2 * swiglu + KD * 48 + 2 * KD + 3 * KD * KD
    two = KD * 68 + 3 * 4 * KD + KD * KD + swiglu
    three = KD * 80 + KD * KD + 2 * KD * KD + KD * KD + 2 * KD * 32
    return one + two + three


def lay_out(inputs, plan):
    a = {k: np.asarray(v) for k, v in inputs.items()}
    a = {k: (v[0] if k.endswith(("_2", "_3")) and k not in ("final_norm_g_2", "norm_final_g_3") else v)
         for k, v in a.items()}
    columns = lambda v: np.ascontiguousarray(v).reshape(-1, P).T
    a["d_skip_3"] = np.repeat(a["d_skip_3"], MP)
    vectors = np.zeros((P, NVEC), np.float32)
    for name, w in VECTORS:
        c = VCOL[name]
        if name in ("gdn_a_log_2", "gdn_dt_bias_2", "dt_bias_3", "a_log_3"):
            vectors[:a[name].size, c] = a[name]
        else:
            vectors[:, c:c + w] = columns(a[name])
    w2, w3 = a["w_in_2"], a["w_in_3"]
    a["w_in_2"] = np.concatenate([w2[:, :2048], w2[:, 2064:5648], w2[:, 5656:]], axis=1)
    a["w_in_3"] = np.concatenate([w3[:, :8192], w3[:, 8224:]], axis=1)
    small = np.zeros((D, 64), np.float32)
    small[:, 0:16], small[:, 16:24], small[:, 24:56] = w2[:, 2048:2064], w2[:, 5648:5656], w3[:, 8192:8224]
    small = small.reshape(KD, P, 64).transpose(1, 0, 2).reshape(P, KD * 64)
    rel = a["att_rel_bias_2"][:, ::-1]
    padded = np.zeros((ATT_HEADS, 640), np.float32)
    padded[:, :255] = rel[:, :1]
    padded[:, 255:255 + REL] = rel
    rows = np.stack([padded[:, P - 1 - p:P - 1 - p + T] for p in range(P)]).reshape(P, ATT_HEADS * T)
    for name in ("rglru_w_r", "rglru_w_i"):
        a[name] = a[name].reshape(D, P)
    stream = np.empty((weight_blocks() * P * P,), np.float32)
    at = 0
    for blocks in plan:
        n = len(blocks)
        part = stream[at:at + n * P * P].reshape(P, n, P)
        for i, (name, k, f) in enumerate(blocks):
            w = a["ada_w"] if name == "ada_w_T" else a[name]
            b = w[k * P:(k + 1) * P, f * P:(f + 1) * P]
            part[:, i, :] = b.T if name == "ada_w_T" else b
        at += n * P * P
    spatial = a["w_spatial_3"].transpose(2, 0, 1).reshape(P, KD * P)
    x = a["x"].reshape(T, KD, P).transpose(2, 1, 0).reshape(P, KD * T)
    return {"x": np.ascontiguousarray(x), "c": a["c"].reshape(1, D), "vectors": vectors, "constants": constants(),
            "small_weights": np.ascontiguousarray(small), "gla_w_gate_up": np.ascontiguousarray(a["gla_w_gate_up_2"]),
            "rel_rows": rows, "w_spatial_T": np.ascontiguousarray(spatial),
            "b_spatial": np.ascontiguousarray(a["b_spatial_3"]).reshape(1, KD * P), "weights": stream}


def kernel(**inputs):
    import concourse.bacc as bacc
    from concourse.bass_utils import run_bass_kernel_spmd

    nc = bacc.Bacc("TRN2", target_bir_lowering=False, num_devices=1)
    plan = build_program(nc)
    result = run_bass_kernel_spmd(nc, [lay_out(inputs, plan)], core_ids=[0])
    out = result.results[0]["out"]
    return np.ascontiguousarray(out.reshape(P, KD, T).transpose(2, 1, 0)).reshape(1, T, D)
```

```python
import itertools

import numpy as np
import concourse.bass as bass
from concourse import mybir

F32 = mybir.dt.float32
F32R = mybir.dt.float32r
ALU = mybir.AluOpType
ACT = mybir.ActivationFunctionType
AX = mybir.AxisListType

P = 128
T = 512
D = 1024
KD = D // P
BLK = T // P
FF = 2816
KF = FF // P
UNIT = 8
RING = 5
HIGH_RING = 3
SBUF_START = 16512
AHEAD = 2
WORK = 73
ALPHA = 2.0 ** 0.25
CH = 64
NCH = T // CH
LEVELS = (32, 16, 8, 4, 2, 1)
HEADS = 4
DK = 128
ATT_HEADS, ATT_HD = 8, 64
REL = 320
MH, MG, MP = 32, 8, 64
MHG = MH // MG
CONF_TAPS = 31
NEG = -1.0e30

VECTORS = [
    ("ada_b", 72), ("ln1_g", 8), ("ln1_b", 8), ("rnn_conv_w", 32), ("rnn_conv_b", 8), ("rglru_b_r", 8),
    ("rglru_b_i", 8), ("rglru_lambda", 8), ("conf_dw_w", 8 * CONF_TAPS), ("conf_dw_b", 8), ("conf_ln_g", 8),
    ("conf_ln_b", 8), ("ln2_g", 8), ("ln2_b", 8), ("ln3_g", 8), ("ln3_b", 8),
    ("mix_norm_g_2", 8), ("gla_b_gate_2", 4), ("gla_norm_g_2", 1), ("gdn_conv_w_2", 48), ("gdn_norm_g_2", 1),
    ("ffn_norm_g_2", 8), ("final_norm_g_2", 8),
    ("norm_mix_g_3", 8), ("conv_w_3", 128), ("conv_b_3", 32), ("ssm_norm_g_3", 16), ("v_norm_g_3", 8),
    ("v_norm_b_3", 8), ("b_gates_3", 16), ("norm_mlp_g_3", 8), ("norm_final_g_3", 8), ("d_skip_3", 16),
    ("gdn_a_log_2", 1), ("gdn_dt_bias_2", 1), ("dt_bias_3", 1), ("a_log_3", 1),
]
VCOL = {}
_n = 0
for _name, _w in VECTORS:
    VCOL[_name] = _n
    _n += _w
NVEC = _n

CONSTS = [("ident", P), ("one", P), ("mean_model", P), ("mean_head", P), ("mean_group", P),
          ("incl64", P), ("strict64", P), ("causal", P)] + [(f"level{s}", P) for s in LEVELS] + [
          ("start64", T), ("start128", T)]
CCOL = {}
_n = 0
for _name, _w in CONSTS:
    CCOL[_name] = (_n, _w)
    _n += _w
NCONST = _n


def constants():
    j, i = np.meshgrid(np.arange(P), np.arange(P), indexing="ij")
    same = j // CH == i // CH
    made = {
        "ident": j == i, "one": np.ones((P, P)), "mean_model": np.full((P, P), 1.0 / D),
        "mean_head": np.full((P, P), 1.0 / DK), "mean_group": np.full((P, P), 1.0 / 256),
        "incl64": same & (j <= i), "strict64": same & (j < i), "causal": j <= i,
        "start64": np.broadcast_to(np.arange(T) % CH != 0, (P, T)),
        "start128": np.broadcast_to(np.arange(T) % P != 0, (P, T)),
    }
    for s in LEVELS:
        made[f"level{s}"] = (j // (2 * s) == i // (2 * s)) & (j % (2 * s) < s) & (i % (2 * s) >= s)
    return np.concatenate([made[n].astype(np.float32) for n, _ in CONSTS], axis=1)


SPLIT = {"ffn1_w_gate", "ffn1_w_up", "ffn1_w_down", "ffn2_w_gate", "ffn2_w_up", "ffn2_w_down", "w_ffn_in_2",
         "w_ffn_out_2", "w_in_3", "w_proj_a_3", "w_proj_b_3", "w_out_3", "w_mlp_up_3",
         "w_mlp_down_3"}


class Lane:

    def __init__(self, sem, name, chained):
        self.sem, self.name, self.chained = sem, name, chained
        self.count, self.queue, self.seen = 0, [], {}

    def last(self):
        return (self.name, self.sem, self.count) if self.count else None

    def wait(self, *marks):
        for m in marks:
            if m is None:
                continue
            if isinstance(m, list):
                self.wait(*m)
                continue
            name, sem, value = m
            if self.seen.get(name, 0) < value:
                self.seen[name] = value
                self.queue.append(lambda e, s=sem, v=value: e.wait_ge(s, v))

    def issue(self, make, *marks):
        self.wait(*marks)
        self.queue.append(make)

    def step(self, make, *marks):
        if self.chained:
            self.wait(self.last())
        self.wait(*marks)
        self.count += 1
        self.queue.append(lambda e: make(e).then_inc(self.sem, 1))
        return self.last()

    def run(self, engine):
        for make in self.queue:
            make(engine)


class Banks:

    def __init__(self, pe, tensors):
        self.pe, self.aps, self.free, self.at = pe, [t[:, :] for t in tensors], [None] * len(tensors), 0

    def take(self):
        n = self.at
        self.at = (n + 1) % len(self.aps)
        self.pe.wait(self.free[n])
        return n, self.aps[n]


def pump(main, filler, per):
    due = 0.0
    while True:
        try:
            next(main)
        except StopIteration as end:
            return end.value
        due += per
        while due >= 1.0:
            due -= 1.0
            next(filler, None)


def in_step(*gens):
    live = list(gens)
    while live:
        for g in list(live):
            if next(g, live) is live:
                live.remove(g)
        yield


def drain(*gens):
    for g in gens:
        for _ in g:
            pass


class Memory:

    def __init__(self, nc):
        self.nc, self.at = nc, SBUF_START
        self.work = self.place("work", [P, WORK, T], F32)
        self.work_r = [self.place(f"work_split{i}", [P, min(8, WORK - i), T], F32R, over=self.work_at + i * T * 4)
                       for i in range(0, WORK, 8)]
        self.ring = self.place("weight_ring", [P, RING, UNIT * P], F32)
        self.ring_r = self.place("weight_ring_low", [P, RING, UNIT * P], F32R, over=self.weight_ring_at)
        self.high = self.place("weight_ring_high", [P, HIGH_RING, UNIT * P], F32R)
        self.scratch = self.place("scratch", [P, 5, T], F32)
        self.vec = self.place("vector_columns", [P, NVEC], F32)
        self.con = self.place("constant_columns", [P, NCONST], F32)
        self.mod = self.place("modulation", [P, 72], F32)
        self.small = self.place("small", [P, 344], F32)
        self.small_w = self.place("narrow_weights", [P, KD, 64], F32)
        self.rows = self.place("rows", [P, T], F32)
        self.banks = [nc.alloc_psum_tensor(f"bank{i}", [P, T], F32) for i in range(8)]

    def place(self, name, shape, dtype, over=None):
        offset = self.at if over is None else over
        if name == "work":
            self.work_at = offset
        if name == "weight_ring":
            self.weight_ring_at = offset
        if over is None:
            self.at += -(-int(np.prod(shape[1:])) * 4 // 32) * 32
        return self.nc.alloc_sbuf_tensor_at(name, shape, dtype, offset=offset)


class Program:

    def __init__(self, nc, dram, memory, order=None):
        self.nc, self.dram, self.order = nc, dram, order
        self.plan, self.plan_cols = [], 0
        self.PE = Lane(self.semaphore("pe_steps"), "pe_steps", False)
        self.AC = Lane(self.semaphore("act_steps"), "act_steps", True)
        self.VE = Lane(self.semaphore("dve_steps"), "dve_steps", True)
        self.GP = Lane(self.semaphore("pool_steps"), "pool_steps", True)
        self.SP = Lane(self.semaphore("sp_steps"), "sp_steps", False)

        self.ring, self.ring_r, self.high = memory.ring, memory.ring_r, memory.high
        self.ring_sem = [self.semaphore(f"ring_loaded{i}") for i in range(RING)]
        self.ring_loads = [0] * RING
        self.ring_free, self.high_free = [None] * RING, [None] * HIGH_RING
        self.ring_at = self.high_at = 0
        self.prepared = []
        self.low_lane = self.VE
        self.work, self.work_r, self.scratch, self.vec = memory.work, memory.work_r, memory.scratch, memory.vec
        self.con, self.mod, self.small, self.small_w = memory.con, memory.mod, memory.small, memory.small_w
        self.rows = memory.rows
        self.gate_up = self.rows[0:16, :]
        self.lin = Banks(self.PE, memory.banks[:4])
        self.mat = Banks(self.PE, memory.banks[4:])
        self.load_count = 0

    def semaphore(self, name):
        return self.nc.alloc_semaphore(name) if self.order is not None else None

    def t(self, i, n=None):
        return self.work[:, i, :] if n is None else self.work[:, i:i + n, :]

    def r(self, i):
        return self.work_r[i // 8][:, i % 8, :]

    def v(self, name, j=0, rows=P):
        c = VCOL[name] + j
        return self.vec[0:rows, c:c + 1]

    def c(self, name):
        a, w = CCOL[name]
        return self.con[:, a:a + w]

    def load(self, out, src, *marks):
        self.load_count += 1
        name = f"load{self.load_count}"
        sem = self.semaphore(name)
        self.SP.issue(lambda e: e.dma_start(out, src).then_inc(sem, 16), *marks)
        return name, sem, 16

    def unit(self, blocks):
        self.plan.append(blocks)
        if self.order is None:
            self.prepare(blocks)
        else:
            done = len(self.plan) - 1
            for n in range(done + len(self.prepared), min(done + AHEAD + 1, len(self.order))):
                self.prepare(self.order[n])
        return self.prepared.pop(0)

    def prepare(self, blocks):
        slot = self.ring_at
        self.ring_at = (slot + 1) % RING
        cols = len(blocks) * P
        src = self.dram["weights"][self.plan_cols * P:(self.plan_cols + cols) * P].rearrange("(p c) -> p c", p=P)
        self.plan_cols += cols
        self.ring_loads[slot] += 1
        dst = self.ring[:, slot, 0:cols]
        sem = self.ring_sem[slot]
        self.SP.issue(lambda e: e.dma_start(dst, src).then_inc(sem, 16), self.ring_free[slot])
        loaded = (f"ring{slot}", sem, 16 * self.ring_loads[slot])
        if blocks[0][0] not in SPLIT:
            self.prepared.append((dst, loaded, (slot, None)))
            return
        high_slot = self.high_at
        self.high_at = (high_slot + 1) % HIGH_RING
        high, low = self.high[:, high_slot, 0:cols], self.ring_r[:, slot, 0:cols]
        mark = self.split(high, low, dst, loaded, self.high_free[high_slot], lane=self.low_lane)
        self.prepared.append(((high, low), mark, (slot, high_slot)))

    def release(self, slots, mark):
        self.ring_free[slots[0]] = mark
        if slots[1] is not None:
            self.high_free[slots[1]] = mark

    def split(self, high, low, x, *marks, lane=None, after=None):
        a = self.act(high, x, ACT.Copy, *marks)
        return self.tt(low, x, high, ALU.subtract, a, after, lane=lane)

    def split_tiles(self, first, high, marks, after=(None,) * KD):
        marks = [self.split(self.r(high + k), self.r(first + k), self.t(first + k), marks[k], after=after[k])
                 for k in range(KD)]
        return (lambda k: (self.r(high + k), self.r(first + k))), marks

    def act(self, out, x, func, *marks, scale=1.0, bias=0.0, total=None):
        kw = {} if total is None else {"accum_out": total}
        if func == ACT.Copy:
            return self.AC.step(lambda e: e.activation(out, x, func, scale=scale), *marks)
        return self.AC.step(lambda e: e.activation(out, x, func, scale=scale, bias=bias, **kw), *marks)

    def tt(self, out, a, b, op, *marks, lane=None):
        return (lane or self.VE).step(lambda e: e.tensor_tensor(out, a, b, op), *marks)

    def ts(self, out, a, s1, s2, op0, op1, *marks, lane=None):
        if op1 is None:
            return (lane or self.VE).step(lambda e: e.tensor_scalar(out, a, s1, None, op0), *marks)
        return (lane or self.VE).step(lambda e: e.tensor_scalar(out, a, s1, s2, op0, op1), *marks)

    def stt(self, out, a, s, b, op0, op1, *marks):
        return self.VE.step(lambda e: e.scalar_tensor_tensor(out=out, in0=a, scalar=s, in1=b, op0=op0, op1=op1),
                            *marks)

    def copy(self, out, x, *marks):
        return self.VE.step(lambda e: e.tensor_copy(out, x), *marks)

    def scan(self, out, keep, x, *marks):
        return self.VE.step(lambda e: e.tensor_tensor_scan(out, keep, x, 0.0, ALU.mult, ALU.add), *marks)

    def mm(self, out, lhsT, rhs, start, stop, *marks, step=False):
        make = lambda e: e.matmul(out, lhsT, rhs, start=start, stop=stop, skip_group_check=True)
        return self.PE.step(make, *marks) if step else self.PE.issue(make, *marks)

    def tr(self, out, x, rows, *marks, step=False):
        ident = self.c("ident")[0:rows, 0:rows]
        make = lambda e: e.transpose(out, x, ident)
        return self.PE.step(make, *marks) if step else self.PE.issue(make, *marks)

    def meet(self):
        lanes = [self.PE, self.AC, self.VE, self.GP]
        marks = [x.last() for x in lanes]
        for x in lanes:
            x.wait(*[m for y, m in zip(lanes, marks) if y is not x])
        return marks

    def product_parts(self, bank, name, f, src, marks, kts):
        kts = range(kts) if isinstance(kts, int) else kts
        last = None
        for k0 in range(kts[0], kts[-1] + 1, UNIT):
            ks = range(k0, min(k0 + UNIT, kts[-1] + 1))
            w, loaded, slot = self.unit([(name, k, f) for k in ks])
            self.PE.wait(loaded)
            for k in ks:
                block = slice((k - k0) * P, (k - k0 + 1) * P)
                first, end, mark = k == kts[0], k == kts[-1], marks[k] if marks else None
                if isinstance(w, tuple):
                    high, low = src(k)
                    self.mm(bank, w[0][:, block], high, first, False, mark)
                    self.mm(bank, w[0][:, block], low, False, False)
                    last = self.mm(bank, w[1][:, block], high, False, end, step=(k == ks[-1]))
                else:
                    last = self.mm(bank, w[:, block], src(k), first, end, mark, step=(k == ks[-1]))
                if k == ks[-1]:
                    self.release(slot, last)
                if k % 4 == 3 and not end:
                    yield
        return last

    def product(self, *args):
        parts = self.product_parts(*args)
        while True:
            try:
                next(parts)
            except StopIteration as end:
                return end.value

    def linear(self, name, fs, src, marks, kts, evacuate, fine=False):
        for f in fs:
            n, bank = self.lin.take()
            if fine:
                m = yield from self.product_parts(bank, name, f, src, marks, kts)
            else:
                m = self.product(bank, name, f, src, marks, kts)
            self.lin.free[n] = evacuate(f, bank, m)
            yield

    def token_major(self, name, f0, src, marks, out, done):
        banks = [self.lin.take() for _ in range(BLK)]
        for k0 in range(0, KD, 2):
            w, loaded, slot = self.unit([(name, k, f0 + f) for k in (k0, k0 + 1) for f in range(4)])
            self.PE.wait(loaded)
            for k in (k0, k0 + 1):
                for b in range(BLK):
                    m = self.mm(banks[b][1], src(k)[:, b * P:(b + 1) * P], w[:, (k - k0) * T:(k - k0 + 1) * T],
                                k == 0, k == KD - 1, marks[k] if marks else None, step=(k % 2 == 1 and b == BLK - 1))
                if k % 2 == 1:
                    self.release(slot, m)
                yield
        for b in range(BLK):
            done[b] = self.act(out(b), banks[b][1], ACT.Copy, m)
            self.lin.free[banks[b][0]] = done[b]
        yield

    def inverse_std(self, bank, n, mark, eps, std, pool):
        a = self.act(std, bank, ACT.Sqrt, mark, self.VE.last(), bias=self.eps[eps])
        pool.free[n] = a
        return self.VE.step(lambda e: e.reciprocal(std, std), a)

    def norm_sum(self, square):
        n, bank = self.mat.take()
        S, read, held = self.scratch, [None, None], []

        def flush():
            for k, x, m in held:
                read[k % 2] = self.mm(bank, self.c("mean_model"), x, k == 0, k == KD - 1, m, step=True)
            held.clear()
            return read[(KD - 1) % 2]

        def add(k, x, mark):
            flush()
            if square:
                mark = self.act(S[:, k % 2, :], x, ACT.Square, mark, read[k % 2])
                x = S[:, k % 2, :]
            held.append((k, x, mark))
        return n, bank, add, flush

    def layer_norm(self, pre, total, out, evacuate_func, g, b):
        S = self.scratch
        n, bank, _, flush = total
        m = flush()
        n2, bank2, add, flush2 = self.norm_sum(True)
        for k in range(KD):
            cen = self.tt(pre(k), pre(k), bank, ALU.subtract, m)
            add(k, pre(k), cen)
        self.mat.free[n] = cen
        r = self.inverse_std(bank2, n2, flush2(), 1e-5, S[:, 2, :], self.mat)
        marks = []
        for k in range(KD):
            y = self.tt(pre(k), pre(k), S[:, 2, :], ALU.mult, r)
            marks.append(self.act(out(k), pre(k), evacuate_func, y, scale=self.v(g, k), bias=self.v(b, k)))
        return marks

    def rms_norm(self, x, total, out, g):
        S = self.scratch
        n, bank, _, flush = total
        r = self.inverse_std(bank, n, flush(), 1e-6, S[:, 2, :], self.mat)
        return [self.stt(out(k), x(k), self.v(g, k), S[:, 2, :], ALU.mult, ALU.mult, r) for k in range(KD)]

    def summed(self, marks, x, total):
        for k in range(KD):
            total[2](k, x(k), marks[k])
        return total

    def setup(self):
        d = self.dram
        self.c_row = self.t(52, 2).rearrange("p a t -> p (a t)")
        crl = self.load(self.c_row, d["c_rows"])
        cvl = self.load(self.small[:, 336:344], d["c_columns"])
        vl = self.load(self.vec[:, :], d["vectors"])
        self.late_loads = lambda: [
            self.load(self.t(0, 8), d["x"].rearrange("p (k t) -> p k t", k=KD)),
            self.load(self.con[:, :], d["constants"]),
            self.load(self.small_w[:, :, :], d["small_weights"].rearrange("p (k m) -> p k m", k=KD)),
            self.load(self.gate_up, d["gla_w_gate_up"])]
        for lane in (self.PE, self.AC, self.VE, self.GP):
            lane.wait(crl, cvl, vl)
        self.eps = {1e-5: self.small[:, 0:1], 1e-6: self.small[:, 1:2]}
        self.unit_bias = self.small[:, 2:3]
        self.zero_bias = self.small[:, 3:4]
        for i, val in enumerate((1e-5, 1e-6, 1.0, 0.0)):
            self.VE.step(lambda e, i=i, val=val: e.memset(self.small[:, i:i + 1], val))
        self.AC.wait(self.VE.last())

    def modulation(self, lo, hi, on_pe=False):
        if on_pe:
            n, bank = self.mat.take()
            for j in range(lo, hi):
                w, loaded, slot = self.unit([("ada_w", k, j) for k in range(KD)])
                self.PE.wait(loaded)
                for k in range(KD):
                    m = self.mm(bank[:, j - lo:j - lo + 1], w[:, k * P:(k + 1) * P], self.c_col[:, k:k + 1], k == 0,
                                k == KD - 1, self.c_ready, step=(k == KD - 1))
                self.release(slot, m)
            self.mat.free[n] = self.copy(self.mod[:, lo:hi], bank[:, 0:hi - lo], m)
        for j in [] if on_pe else range(lo, hi):
            w, loaded, slot = self.unit([("ada_w_T", k, j) for k in range(KD)])
            junk = self.scratch[:, 3:5, :].rearrange("p a t -> p (a t)")
            m = self.VE.step(lambda e, w=w, j=j: e.tensor_tensor_reduce(
                out=junk, in0=w, in1=self.c_act, scale=1.0, scalar=0.0, op0=ALU.mult, op1=ALU.add,
                accum_out=self.mod[:, j:j + 1]), loaded, self.c_ready)
            self.release(slot, m)
            yield
        self.tt(self.mod[:, lo:hi], self.mod[:, lo:hi], self.vec[:, VCOL["ada_b"] + lo:VCOL["ada_b"] + hi], ALU.add)
        for which in range(9):
            a, b = which * 8, which * 8 + 8
            if lo <= a and b <= hi and which % 3 == 1:
                self.ts(self.mod[:, a:b], self.mod[:, a:b], 1.0, None, ALU.add, None)
            if lo <= a and b <= hi and which % 3 == 2:
                w = 1.0 if which == 5 else 0.5
                self.ts(self.mod[:, a:b], self.mod[:, a:b], 1.0, w, ALU.add, ALU.mult)
        yield

    def feed_forward(self, hidden, n_hidden, down, evacuate):
        for first in range(0, n_hidden, 8):
            ks = range(first, min(first + 8, n_hidden))
            marks = {}
            for j in ks:
                i = j % 8
                mark = hidden(j, self.t(24 + i))
                marks[j] = self.split(self.r(32 + i), self.r(24 + i), self.t(24 + i), mark)
                yield
            for f in range(KD):
                n, bank = self.lin.take()
                m = self.product(bank, down, f, lambda k: (self.r(32 + k % 8), self.r(24 + k % 8)), marks, ks)
                self.lin.free[n] = evacuate(f, bank, m, ks[-1] == n_hidden - 1)
                yield

    def swiglu(self, u, u_marks, gate, up, down, evacuate):
        tmp_read = [None, None]

        def hidden(j, out):
            n, gbank = self.lin.take()
            gm = self.product(gbank, gate[0], gate[1] + j, u, u_marks, KD)
            tmp = self.scratch[:, j % 2, :]
            a = self.act(tmp, gbank, ACT.Silu, gm, tmp_read[j % 2])
            self.lin.free[n] = a
            n2, ubank = self.lin.take()
            um = self.product(ubank, up[0], up[1] + j, u, u_marks, KD)
            self.lin.free[n2] = tmp_read[j % 2] = self.tt(out, tmp, ubank, ALU.mult, a, um)
            return tmp_read[j % 2]
        return self.feed_forward(hidden, KF, down, evacuate)

    def modulated(self, which, x_marks):
        sh, sc = 24 * which, 24 * which + 8
        return [self.ts(self.t(8 + k), self.t(k), self.mod[:, sc + k:sc + k + 1], self.mod[:, sh + k:sh + k + 1],
                        ALU.mult, ALU.add, x_marks[k]) for k in range(KD)]

    def residual(self, which, pre, base):
        total = self.norm_sum(False)

        def evacuate(f, bank, m, last=True):
            c = 24 * which + 16 + f
            mark = self.stt(pre(f), bank, self.mod[:, c:c + 1], pre(f), ALU.mult, ALU.add, m, base[f])
            if last:
                total[2](f, pre(f), mark)
            return mark
        return evacuate, total

    def add_to_x(self):
        total = self.norm_sum(True)

        def evacuate(f, bank, m, last=True):
            mark = self.tt(self.t(f), self.t(f), bank, ALU.add, m)
            if last:
                total[2](f, self.t(f), mark)
            return mark
        return evacuate, total

    def scaled_x(self, pre, x_marks):
        return [self.ts(pre(k), self.t(k), ALPHA, None, ALU.mult, None, x_marks[k], lane=self.GP) for k in range(KD)]

    def block1(self):
        t = self.t
        self.c_act, self.c_col = self.c_row, self.small[:, 336:344]
        self.act(self.c_col, self.c_col, ACT.Silu)
        self.c_ready = self.act(self.c_act, self.c_row, ACT.Silu)
        drain(self.modulation(0, 16, on_pe=True))
        late = self.late_loads()
        for lane in (self.PE, self.AC, self.VE, self.GP):
            lane.wait(*late)
        x_marks = [None] * KD
        pre = lambda k: t(16 + k)
        u_marks = self.modulated(0, x_marks)
        base = self.scaled_x(pre, x_marks)
        evac, pm = self.residual(0, pre, base)
        u, u_marks = self.split_tiles(8, 40, u_marks)
        rest = itertools.chain(self.modulation(16, 24), self.modulation(24, 72))
        pump(self.swiglu(u, u_marks, ("ffn1_w_gate", 0), ("ffn1_w_up", 0), "ffn1_w_down", evac), rest, 1.3)
        drain(rest)
        x_marks = self.layer_norm(pre, pm, lambda k: t(k), ACT.Identity, "ln1_g", "ln1_b")
        x_marks = self.mixer1(x_marks)
        u_marks = self.modulated(2, x_marks)
        base = self.scaled_x(pre, x_marks)
        evac, pm = self.residual(2, pre, base)
        u, u_marks = self.split_tiles(8, 40, u_marks)
        drain(self.swiglu(u, u_marks, ("ffn2_w_gate", 0), ("ffn2_w_up", 0), "ffn2_w_down", evac))
        return self.layer_norm(pre, pm, lambda k: t(k), ACT.Identity, "ln3_g", "ln3_b")

    def taps(self, out, x, w, b, n_taps, *marks):
        if b is None:
            m = self.ts(out, x, w(n_taps - 1), None, ALU.mult, None, *marks)
        else:
            m = self.ts(out, x, w(n_taps - 1), b, ALU.mult, ALU.add, *marks)
        yield m
        for back in range(1, n_taps):
            m = self.stt(out[:, back:T], x[:, 0:T - back], w(n_taps - 1 - back), out[:, back:T], ALU.mult, ALU.add)
            yield m

    def mixer1(self, x_marks):
        t, S = self.t, self.scratch
        U, GLU, HB, XR, XC, GR, GA, GB = (lambda k, o=o: t(o + k) for o in (8, 16, 24, 32, 40, 48, 56, 64))
        u_marks = self.modulated(1, x_marks)
        glu_marks, hb_marks = [None] * KD, [None] * KD

        def conf_conv():
            for k in range(KD):
                for m in self.taps(HB(k), GLU(k), lambda j, k=k: self.v("conf_dw_w", j * 8 + k),
                                   self.v("conf_dw_b", k), CONF_TAPS, glu_marks[k]):
                    yield
                hb_marks[k] = m
        conv = conf_conv()

        def glu():
            tmp_read = [None, None]
            for k in range(KD):
                n, gate = self.lin.take()
                gm = self.product(gate, "w_in", 24 + k, U, u_marks, KD)
                n2, val = self.lin.take()
                vm = self.product(val, "w_in", 16 + k, U, u_marks, KD)
                a = self.act(S[:, k % 2, :], gate, ACT.Sigmoid, gm, tmp_read[k % 2])
                self.lin.free[n] = a
                glu_marks[k] = tmp_read[k % 2] = self.lin.free[n2] = self.tt(GLU(k), S[:, k % 2, :], val, ALU.mult,
                                                                             a, vm)
                yield
        for k, _ in enumerate(glu()):
            for _ in range(14 if k else 0):
                next(conv)

        xr_marks = [None] * KD

        def raw(dst, marks):
            def evacuate(f, bank, m):
                k = f % KD
                marks[k] = self.act(dst(k), bank, ACT.Copy, m)
                return marks[k]
            return evacuate
        xc_marks = [None] * KD
        for f, _ in enumerate(self.linear("w_in", range(0, 8), U, u_marks, KD, raw(XR, xr_marks))):
            for m in self.taps(XC(f), XR(f), lambda j, f=f: self.v("rnn_conv_w", j * 8 + f), self.v("rnn_conv_b", f), 4,
                               xr_marks[f]):
                xc_marks[f] = m
            for _ in range(6):
                next(conv, None)

        for k0, name, dst, bias in ((0, "rglru_w_r", XR, "rglru_b_r"), (0, "rglru_w_i", GB, "rglru_b_i")):
            w, loaded, slot = self.unit([(name, k, 0) for k in range(KD)])
            self.PE.wait(loaded)
            for k in range(KD):
                n, bank = self.mat.take()
                m = self.mm(bank, w[:, k * P:(k + 1) * P], XC(k), True, True, xc_marks[k], step=True)
                self.mat.free[n] = self.act(dst(k), bank, ACT.Sigmoid, m, xc_marks[k], bias=self.v(bias, k))
            self.release(slot, m)

        lam = self.vec[:, VCOL["rglru_lambda"]:VCOL["rglru_lambda"] + 8]
        rate = self.small[:, 8:16]
        neg_rate = self.small[:, 16:24]
        self.softplus(rate, lam, -1.0, self.small[:, 24:64], 8, P)
        self.ts(rate, rate, 8.0, None, ALU.mult, None)
        rate_mark = self.ts(neg_rate, rate, -1.0, None, ALU.mult, None)

        gr_marks = [None] * KD
        hr_marks = [None] * KD

        def lru():
            for k in range(KD):
                self.act(GA(k), XR(k), ACT.Exp, rate_mark, scale=neg_rate[:, k:k + 1])
                a = self.act(XR(k), XR(k), ACT.Tanh, scale=rate[:, k:k + 1])
                q = self.tt(S[:, 2, :], GA(k), GA(k), ALU.mult, a)
                self.stt(XR(k), S[:, 2, :], 1.0, XR(k), ALU.add, ALU.mult)
                yield
            q = self.VE.last()
            for k in range(KD):
                a = self.act(XR(k), XR(k), ACT.Sqrt, q)
                self.tt(GB(k), GB(k), XC(k), ALU.mult)
                self.tt(GB(k), GB(k), XR(k), ALU.mult, a)
                hr_marks[k] = self.scan(XC(k), GA(k), GB(k))
                yield
        scan = lru()
        for _ in self.linear("w_in", range(8, 16), U, u_marks, KD, raw(GR, gr_marks)):
            for _ in range(2):
                next(scan, None)
            for _ in range(5):
                next(conv, None)
        drain(scan)
        scan_done = self.VE.last()

        def gate(dst):
            def evacuate(f, bank, m):
                return self.act(dst(f % KD), bank, ACT.Sigmoid, m, scan_done)
            return evacuate
        for _ in self.linear("w_in", range(32, 40), U, u_marks, KD, gate(GA)):
            for _ in range(6):
                next(conv, None)
        for _ in self.linear("w_in", range(40, 48), U, u_marks, KD, gate(GB)):
            for _ in range(6):
                next(conv, None)
        for k in range(KD):
            a = self.act(GR(k), GR(k), ACT.Gelu_apprx_tanh)
            gr_marks[k] = self.tt(GR(k), GR(k), XC(k), ALU.mult, a)
        drain(conv)

        ya_marks, yb_marks, mix_marks = [None] * KD, [None] * KD, [None] * KD

        def scale_by(dst, marks):
            def evacuate(f, bank, m):
                marks[f] = self.tt(dst(f), dst(f), bank, ALU.mult, m)
                return marks[f]
            return evacuate
        ya = self.linear("rnn_w_proj", range(8), GR, gr_marks, KD, scale_by(GA, ya_marks))
        next(ya)
        total = self.summed(hb_marks, HB, self.norm_sum(False))
        hb_marks = self.layer_norm(HB, total, HB, ACT.Silu, "conf_ln_g", "conf_ln_b")
        drain(ya)
        base = [self.ts(GLU(k), self.t(k), ALPHA, None, ALU.mult, None, hb_marks[k], lane=self.GP) for k in range(KD)]
        for f, _ in enumerate(self.linear("conf_w_proj", range(8), HB, hb_marks, KD, scale_by(GB, yb_marks))):
            mix_marks[f] = self.tt(U(f), GA(f), GB(f), ALU.add, yb_marks[f], lane=self.GP)
        evac, pm = self.residual(1, GLU, base)
        drain(self.linear("mix_w_out", range(8), U, mix_marks, KD, evac))
        return self.layer_norm(GLU, pm, lambda k: self.t(k), ACT.Identity, "ln2_g", "ln2_b")

    def softplus(self, out, x, sign, tmp, n, rows, *marks):
        R = slice(0, rows)
        e, u, d, z = (tmp[R, i * n:(i + 1) * n] for i in range(4))
        a = self.act(e, x, ACT.Abs, *marks, self.VE.last())
        a = self.act(e, e, ACT.Exp, scale=-1.0)
        m = self.ts(u, e, 1.0, None, ALU.add, None, a)
        a = self.act(out, u, ACT.Ln, m)
        self.ts(d, u, 1.0, None, ALU.subtract, None)
        self.ts(z, d, 0.0, None, ALU.is_equal, None)
        self.tt(d, d, z, ALU.add)
        self.tt(out, out, z, ALU.add, a)
        self.tt(out, out, e, ALU.mult)
        m = self.VE.step(lambda e_: e_.reciprocal(d, d))
        self.tt(out, out, d, ALU.mult)
        self.ts(u, x, sign, 0.0, ALU.mult, ALU.max)
        return self.tt(out, out, u, ALU.add)

    def block2(self, x_marks):
        t, S = self.t, self.scratch
        U = lambda k: t(8 + k)
        self.U = U
        self.meet()
        total = self.summed(x_marks, t, self.norm_sum(True))
        self.um = um = self.rms_norm(t, total, U, "mix_norm_g_2")
        n_in = "w_in_2"
        GQ, GK, GV, GR, AQ, AK, AV, DQ, MERGE = 0, 4, 8, 12, 16, 20, 24, 28, 44

        def evac_to(dst, marks, func=ACT.Copy, scale=1.0):
            def evacuate(f, bank, m):
                k = f % 4
                marks[k] = self.act(dst(k), bank, func, m, scale=scale)
                return marks[k]
            return evacuate
        Q, K, V, R = (lambda k, o=o: t(o + k) for o in (28, 32, 36, 40))
        qm, km, vm, rm = ([None] * 4 for _ in range(4))
        lr = S[0:16, 4, :]
        rows = self.gdn_rows()
        pump(self.linear(n_in, range(GQ, GQ + 4), U, um, KD, evac_to(Q, qm, scale=DK ** -0.5)), rows, 1)
        lr_mark, _ = self.narrow(lr, 0, 16, U, um, ACT.Copy)
        pump(self.linear(n_in, range(GK, GK + 4), U, um, KD, evac_to(K, km)), rows, 1)
        pump(self.token_major(n_in, GV, U, um, V, vm), rows, 1)
        drain(rows)
        drain(self.linear(n_in, range(GR, GR + 4), U, um, KD, evac_to(R, rm, ACT.Silu)))
        AQt, AKt, AVt = (lambda k, o=o: t(o + k) for o in (57, 61, 65))
        aqm, akm, avm = ([None] * 4 for _ in range(3))

        def att_inputs():
            yield from self.linear(n_in, range(AQ, AQ + 4), U, um, KD, evac_to(AQt, aqm), fine=True)
            yield from self.linear(n_in, range(AK, AK + 4), U, um, KD, evac_to(AKt, akm), fine=True)
            yield from self.token_major(n_in, AV, U, um, AVt, avm)
        fill = att_inputs()
        pump(self.gla(Q, K, V, R, qm, km, vm, rm, lr, lr_mark), fill, 0.6)
        drain(fill)
        self.meet()
        self.GD = [36, 37, 38, 39, 40, 41, 42, 43, 52, 53, 54, 55, 56, 69, 28, 29]
        fill = self.gdn_inputs(n_in, DQ, U, um)
        pump(self.attention(AQt, AKt, AVt, aqm, akm, avm), fill, 1.1)
        drain(fill)
        self.meet()
        self.Ym = ym = [None] * KD
        Yt = lambda k: t([30, 31, 32, 33, 34, 35, 57, 58][k])
        fill = self.merge(Yt, [(0, 16), (1, 20)], MERGE)
        pump(self.gdn(), fill, 1.0)
        drain(fill)
        self.meet()
        drain(self.merge(Yt, [(2, 24)], MERGE))
        evac, total = self.add_to_x()
        drain(self.linear("w_out_2", range(8), Yt, ym, KD, evac))
        um = self.rms_norm(t, total, U, "ffn_norm_g_2")
        evac, total = self.add_to_x()
        u, um = self.split_tiles(8, 40, um)
        drain(self.swiglu(u, um, ("w_ffn_in_2", 0), ("w_ffn_in_2", KF), "w_ffn_out_2", evac))
        return self.rms_norm(t, total, t, "final_norm_g_2")

    def gdn_inputs(self, name, f0, U, um):
        S, Dt = self.scratch, lambda k: self.t(self.GD[k])
        RAW, SQ, STD = S[:, 0, :], S[:, 1, :], S[:, 2, :]

        def l2_norm(k):
            a = self.act(SQ, Dt(k), ACT.Square, self.PE.last())
            n, bank = self.lin.take()
            m = self.mm(bank, self.c("one"), SQ, True, True, a, step=True)
            r = self.inverse_std(bank, n, m, 1e-6, STD, self.lin)
            self.stt(Dt(k), Dt(k), DK ** -0.5 if k < 4 else 1.0, STD, ALU.mult, ALU.mult, r)
        for k in range(16):
            n, bank = self.lin.take()
            m = yield from self.product_parts(bank, name, f0 + k, U, um, KD)
            if k >= 12:
                self.lin.free[n] = self.act(Dt(k), bank, ACT.Silu, m)
            else:
                a = self.act(RAW, bank, ACT.Copy, m, self.VE.last())
                self.lin.free[n] = a
                drain(self.taps(Dt(k), RAW, lambda j, k=k: self.v("gdn_conv_w_2", j * 12 + k), None, 4, a))
                self.act(Dt(k), Dt(k), ACT.Silu, self.VE.last())
            if 1 <= k <= 8:
                l2_norm(k - 1)
            yield

    def gdn_rows(self):
        t, S, small = self.t, self.scratch, self.small
        G, B, EG, ED, X = (t(i)[0:HEADS, :] for i in (44, 45, 46, 47, 48))
        tmp = t(49, 4).rearrange("p a t -> p (a t)")
        am, _ = self.narrow(X, 16, HEADS, self.U, self.um, ACT.Copy)
        yield
        bm, _ = self.narrow(B, 20, HEADS, self.U, self.um, ACT.Sigmoid)
        yield
        self.ts(X, X, self.v("gdn_dt_bias_2", rows=4), None, ALU.add, None, am)
        self.softplus(G, X, 1.0, tmp, T, 4)
        yield
        ea = small[0:4, 4:5]
        a = self.act(ea, self.v("gdn_a_log_2", rows=4), ACT.Exp, self.VE.last())
        self.ts(X, G, ea, -1.0, ALU.mult, ALU.mult, a)
        b = self.scan(G, self.c("start64")[0:4, :], X)
        a = self.act(EG, G, ACT.Exp, b)
        g3 = G.rearrange("p (c i) -> p c i", i=CH)
        b = self.tt(ED.rearrange("p (c i) -> p c i", i=CH), g3[:, :, CH - 1:CH].to_broadcast([HEADS, NCH, CH]), g3,
                    ALU.subtract)
        a = self.act(ED, ED, ACT.Exp, b)
        yield
        n, bank = self.mat.take()
        for q, x in enumerate((G, B, EG, ED)):
            for p in range(BLK):
                c = (q * BLK + p) * HEADS
                m = self.tr(bank[:, c:c + HEADS], x[:, p * P:(p + 1) * P], HEADS, a, b, bm,
                            step=(q == 3 and p == BLK - 1))
        self.gcols = small[:, 224:288].rearrange("p (q b h) -> p q b h", q=4, h=HEADS)
        self.mat.free[n] = self.copy(small[:, 224:288], bank[:, 0:64], m)
        self.gcol_bg = small[:, 288:304].rearrange("p (b h) -> p b h", h=HEADS)
        self.tt(self.gcol_bg, self.gcols[:, 1], self.gcols[:, 2], ALU.mult)
        self.grow_marks = [self.act(S[r:r + HEADS, 4, :], x, ACT.Copy) for r, x in ((32, G), (64, B), (96, EG))][-1]
        yield

    def narrow(self, out, c0, width, U, um, func, scale=1.0):
        n, bank = self.mat.take()
        steps = []
        for k in range(KD):
            m = self.mm(bank[0:width, :], self.small_w[:, k, c0:c0 + width], U(k), k == 0, k == KD - 1, um[k],
                        step=True)
            steps.append(m)
        a = self.act(out, bank[0:width, :], func, m, self.VE.last(), scale=scale)
        self.mat.free[n] = a
        return a, steps

    def merge(self, Yt, branches, merge0):
        tmp = self.scratch[:, 3, :]
        names = ("w_branch_gla_2", "w_branch_att_2", "w_branch_gdn_2")
        for f in range(KD):
            for br, o in branches:
                n, gbank = self.lin.take()
                gm = yield from self.product_parts(gbank, "w_in_2", merge0 + br * 8 + f, self.U, self.um, KD)
                a = self.act(tmp, gbank, ACT.Sigmoid, gm, self.VE.last())
                self.lin.free[n] = a
                yield
                n2, bank = self.lin.take()
                bm = yield from self.product_parts(bank, names[br], f, lambda k, o=o: self.t(o + k), None, 4)
                if br == 0:
                    b = self.tt(Yt(f), tmp, bank, ALU.mult, a, bm)
                    self.lin.free[n2] = b
                else:
                    b = self.tt(tmp, tmp, bank, ALU.mult, a, bm)
                    self.lin.free[n2] = b
                    b = self.tt(Yt(f), Yt(f), tmp, ALU.add)
                self.Ym[f] = b
                yield

    def head_norm(self, O, gate, out, g, sq, std, sq_free, *marks):
        a = self.act(sq, O, ACT.Square, *marks, sq_free)
        n, bank = self.mat.take()
        m = self.mm(bank, self.c("mean_head"), sq, True, True, a, step=True)
        r = self.inverse_std(bank, n, m, 1e-6, std, self.mat)
        self.stt(O, O, self.v(g), std, ALU.mult, ALU.mult, r)
        return self.tt(out, O, gate, ALU.mult)

    def gla(self, Q, K, V, R, qm, km, vm, rm, lr, lr_mark):
        t, S, VE, small = self.t, self.scratch, self.VE, self.small
        G, A1 = [t(44), t(69)], t(45)
        E, QE, KE = [t(46), t(47)], [t(48), t(49)], [S[:, 0, :], S[:, 1, :]]
        SC, O, KDT, QG, KDC, TMP, A2 = t(50), t(51), t(52), t(55), t(56), S[:, 2, :], S[:, 3, :]
        states = t(53, 2).rearrange("p a (c v) -> p (a c) v", v=P)
        pair = lambda x, p: x[:, p * P:(p + 1) * P]
        wide = lambda x: x.rearrange("p (b i) -> p b i", i=P)
        masked = lambda name: self.c(name).unsqueeze(1).to_broadcast([P, BLK, P])
        g_marks = [None] * HEADS

        def decay(h):
            g, bias = G[h % 2], self.v("gla_b_gate_2", h)
            n, bank = self.mat.take()
            m = self.mm(bank, self.gate_up[:, h * P:(h + 1) * P], lr, True, True, lr_mark, step=True)
            a = self.act(A2, bank, ACT.Abs, m, VE.last(), bias=bias)
            self.mat.free[n] = self.ts(g, bank, bias, 0.0, ALU.add, ALU.min, a)
            self.act(A2, A2, ACT.Exp, scale=-1.0)
            a = self.act(A2, A2, ACT.Ln, bias=self.unit_bias)
            self.tt(A2, g, A2, ALU.subtract, a)
            self.scan(g, self.c("start64"), A2)
            g_marks[h] = self.ts(g, g, 1.0 / 16.0, None, ALU.mult, None)

        mms = [None, None]

        def front(h, li):
            s, i, g = LEVELS[li], li % 2, G[h % 2]
            g3 = g.rearrange("p (b s) -> p b s", s=2 * s)
            ref = g3[:, :, s - 1:s].to_broadcast([P, T // (2 * s), 2 * s])
            b = self.tt(E[i].rearrange("p (b s) -> p b s", s=2 * s), g3, ref, ALU.subtract, mms[i])
            self.act(E[i], E[i], ACT.Abs, b)
            a = self.act(E[i], E[i], ACT.Exp, scale=-1.0)
            kb = self.tt(KE[i], K(h), E[i], ALU.mult, a, mms[i], lane=self.GP)
            qb = self.tt(QE[i], Q(h), E[i], ALU.mult, a)
            return kb, qb

        def back(li, kb, qb):
            i = li % 2
            n, bank = self.mat.take()
            for p in range(BLK):
                m = self.mm(pair(bank, p), pair(KE[i], p), pair(QE[i], p), True, True, kb, qb, step=(p == BLK - 1))
            mms[i] = m
            self.mat.free[n] = self.tt(wide(TMP), wide(bank), masked(f"level{LEVELS[li]}"), ALU.mult, m)
            VE.wait(kb)
            return self.tt(SC, SC, TMP, ALU.add)

        decay(0)
        for h in range(HEADS):
            ready = front(h, 0)
            yield
            n, bank = self.mat.take()
            for p in range(BLK):
                m = self.mm(pair(bank, p), pair(K(h), p), pair(Q(h), p), True, True, qm[h], km[h], step=(p == BLK - 1))
            sm = self.tt(wide(SC), wide(bank), masked("ident"), ALU.mult, m)
            self.mat.free[n] = sm
            for li in range(len(LEVELS)):
                ahead = front(h, li + 1) if li + 1 < len(LEVELS) else None
                yield
                sm = back(li, *ready)
                ready = ahead
                yield
            g = G[h % 2]
            a = self.act(QG, g, ACT.Exp, g_marks[h], self.PE.last())
            el = small[:, 64 + h * 8:64 + h * 8 + 8]
            self.copy(el, QG[:, CH - 1::CH], a)
            qg = self.tt(QG, Q(h), QG, ALU.mult)
            g3 = g.rearrange("p (c i) -> p c i", i=CH)
            b = self.tt(KDC.rearrange("p (c i) -> p c i", i=CH), g3[:, :, CH - 1:CH].to_broadcast([P, NCH, CH]), g3,
                        ALU.subtract, self.PE.last())
            a = self.act(KDC, KDC, ACT.Exp, b)
            kd = self.tt(KDC, K(h), KDC, ALU.mult, a)
            if h + 1 < HEADS:
                decay(h + 1)
            yield
            n, bank = self.mat.take()
            for p in range(BLK):
                m = self.tr(pair(bank, p), pair(KDC, p), P, kd, step=(p == BLK - 1))
            a = self.act(KDT, bank, ACT.Copy, m)
            self.mat.free[n] = a
            yield
            us = []
            for half in range(2):
                n, bank = self.mat.take()
                r = half * CH
                for c in range(half, NCH - 1, 2):
                    p = c // 2
                    m = self.mm(pair(bank, p), KDT[r:r + CH, p * P:(p + 1) * P], V(p)[r:r + CH, h * P:(h + 1) * P],
                                True, True, a, vm[p], step=(c + 2 >= NCH - 1))
                us.append((n, bank, m))
            for c in range(NCH - 1):
                n, bank, m = us[c % 2]
                u = pair(bank, c // 2)
                if c == 0:
                    b = self.copy(states[:, 1, :], u, m)
                else:
                    b = self.stt(states[:, c + 1, :], states[:, c, :], el[:, c:c + 1], u, ALU.mult, ALU.add, m)
                self.mat.free[n] = b
            yield
            yield
            n, bank = self.mat.take()
            for p in range(BLK):
                m = self.mm(pair(bank, p), V(p)[:, h * P:(h + 1) * P], pair(SC, p), True, False, sm, b)
                for c in (2 * p, 2 * p + 1):
                    if c:
                        m = self.mm(bank[:, c * CH:(c + 1) * CH], states[:, c, :], QG[:, c * CH:(c + 1) * CH], False,
                                    c % 2 == 1, qg, step=(c == NCH - 1))
            a = self.act(O, bank, ACT.Copy, m, VE.last())
            self.mat.free[n] = a
            self.head_norm(O, R(h), t(16 + h), "gla_norm_g_2", A1, QE[0], None, rm[h], a, VE.last())
            yield

    def attention(self, Q, K, V, qm, km, vm):
        t = self.t
        rel = self.dram["rel_rows"].rearrange("p (h m) -> p h m", m=T)
        bias, bias_read = [t(70), t(71)], [self.VE.last(), self.VE.last()]
        SC, PT = [t(44), t(45)], [t(46), t(47)]
        stat = self.small[:, 96:224]
        bias_loaded = {}

        def load_bias(h):
            bias_loaded[h] = self.load(bias[h % 2], rel[:, h, :], bias_read[h % 2])
        load_bias(0)
        load_bias(1)
        self.PE.wait(*self.mat.free)
        obank, rotate = self.mat.aps[0], Banks(self.PE, [])
        rotate.aps, rotate.free = self.mat.aps[1:], [None] * 3
        out_read = [None]
        scores_read, pt_read = [None, None], [None, None]
        steps = [(h, it) for h in range(ATT_HEADS) for it in range(BLK)]

        def softmax(n_step):
            h, it = steps[n_step]
            r0, tile, i = (h % 2) * ATT_HD, h // 2, n_step % 2
            n_keys = (it + 1) * P
            n, bank = rotate.take()
            m = self.mm(bank[:, 0:n_keys], Q(tile)[r0:r0 + ATT_HD, it * P:(it + 1) * P],
                        K(tile)[r0:r0 + ATT_HD, 0:n_keys], True, True, qm[tile], km[tile], step=True)
            sc = SC[i][:, 0:n_keys]
            tile_bias = bias[h % 2]
            if it == 0:
                self.VE.step(lambda e: e.memset(tile_bias[0:CH, T - CH:T], NEG), bias_loaded[h])
            rotate.free[n] = self.stt(sc, bank[:, 0:n_keys], ATT_HD ** -0.5, tile_bias[:, T - n_keys:T], ALU.mult,
                                      ALU.add, m, scores_read[i])
            bias_read[h % 2] = rotate.free[n]
            if it == BLK - 1 and h + 2 < ATT_HEADS:
                load_bias(h + 2)
            mx, tot = stat[:, 4 * n_step:4 * n_step + 1], stat[:, 4 * n_step + 1:4 * n_step + 2]
            self.VE.step(lambda e: e.tensor_reduce(mx, sc, AX.X, ALU.max))
            b = self.ts(mx, mx, -1.0, None, ALU.mult, None)
            a = self.act(sc, sc, ACT.Exp, b, bias=mx, total=tot)
            self.VE.step(lambda e: e.reciprocal(tot, tot), a)
            return self.ts(sc, sc, tot, None, ALU.mult, None)

        def values(n_step, ready):
            h, it = steps[n_step]
            r0, i = (h % 2) * ATT_HD, n_step % 2
            n_keys = (it + 1) * P
            n, bank = rotate.take()
            for j in range(it + 1):
                m = self.tr(bank[:, j * P:(j + 1) * P], SC[i][:, j * P:(j + 1) * P], P, ready, step=(j == it))
            scores_read[i] = m
            a = self.act(PT[i][:, 0:n_keys], bank[:, 0:n_keys], ACT.Copy, m, pt_read[i])
            rotate.free[n] = a
            yield
            if h % 2 == 0 and it == 0:
                self.PE.wait(out_read[0])
            for j in range(it + 1):
                m = self.mm(obank[r0:r0 + ATT_HD, it * P:(it + 1) * P], V(j)[:, h * ATT_HD:(h + 1) * ATT_HD],
                            PT[i][:, j * P:(j + 1) * P], j == 0, j == it, a, vm[j], step=(j == it))
            pt_read[i] = m
            if h % 2 == 1 and it == BLK - 1:
                out_read[0] = self.act(t(20 + h // 2), obank, ACT.Copy, m)

        ready = softmax(0)
        for n_step in range(len(steps)):
            ahead = softmax(n_step + 1) if n_step + 1 < len(steps) else None
            yield from values(n_step, ready)
            ready = ahead
        self.mat.free = [out_read[0]] + rotate.free

    def gdn(self):
        t, S, VE = self.t, self.scratch, self.VE
        small, cols = self.small, self.gcols
        Dt = lambda k: t(self.GD[k])
        pair = lambda x, p: x[:, p * P:(p + 1) * P]
        wide = lambda x: x.rearrange("p (b i) -> p b i", i=P)
        masked = lambda name: self.c(name).unsqueeze(1).to_broadcast([P, BLK, P])
        WT = lambda h: t(44 + h)
        ATN = lambda h: t(48 + h)
        KDT = lambda h: t(63 + h)
        UV = t(59, 4)
        elast = small[:, 304:336].rearrange("p (h c) -> p h c", h=HEADS)

        def head(h, KB, GAM, AMAT, AM, TI, TT, PM):
            q, k, v = Dt(h), Dt(4 + h), Dt(8 + h)

            def row(r):
                n, bank = self.mat.take()
                sel = self.c("ident")[r:r + HEADS, r + h:r + h + 1].to_broadcast([HEADS, P])
                return n, bank, self.mm(bank, sel, S[r:r + HEADS, 4, :], True, True, self.grow_marks, step=True)
            n, bank, m = row(64)
            kb = self.tt(KB, k, bank, ALU.mult, m)
            self.mat.free[n] = kb
            yield
            n, bank, m = row(32)
            for p in range(BLK):
                b = self.ts(pair(GAM, p), pair(bank, p), cols[:, 0, p, h:h + 1], 0.0, ALU.subtract, ALU.min, m)
            self.mat.free[n] = b
            a = self.act(GAM, GAM, ACT.Exp, b)
            self.tt(wide(GAM), wide(GAM), masked("incl64"), ALU.mult, a)
            yield
            n, bank = self.mat.take()
            for p in range(BLK):
                m = self.mm(pair(bank, p), pair(k, p), pair(KB, p), True, True, kb, step=(p == BLK - 1))
            self.mat.free[n] = self.tt(AMAT, bank, GAM, ALU.mult, m)
            am = self.tt(wide(AMAT), wide(AMAT), masked("strict64"), ALU.mult)
            n, bank = self.mat.take()
            for p in range(BLK):
                m = self.mm(pair(bank, p), pair(k, p), pair(q, p), True, True, step=(p == BLK - 1))
            self.mat.free[n] = self.tt(ATN(h), bank, GAM, ALU.mult, m)
            self.copy(wide(TI), masked("ident"), self.PE.last(), self.AC.last())
            tm = self.copy(wide(TT), masked("ident"))
            m = None
            for s in reversed(LEVELS):
                g = self.tt(wide(AM), wide(AMAT), masked(f"level{s}"), ALU.mult, am, m, lane=self.GP)
                yield
                n, bank = self.mat.take()
                for p in range(BLK):
                    m = self.mm(pair(bank, p), pair(AM, p), pair(TI, p), True, True, g, tm, step=(p == BLK - 1))
                a = self.act(PM, bank, ACT.Copy, m, self.PE.last())
                self.mat.free[n] = a
                yield
                n, bank = self.mat.take()
                for p in range(BLK):
                    mi = self.mm(pair(bank, p), pair(TT, p), pair(PM, p), True, True, a, step=(p == BLK - 1))
                n2, bank2 = self.mat.take()
                for p in range(BLK):
                    mt = self.mm(pair(bank2, p), pair(PM, p), pair(TT, p), True, True, step=(p == BLK - 1))
                self.mat.free[n] = self.tt(TI, TI, bank, ALU.subtract, mi)
                self.mat.free[n2] = tm = self.tt(TT, TT, bank2, ALU.subtract, mt)
            yield
            n, bank = self.mat.take()
            for p in range(BLK):
                m = self.tr(pair(bank, p), pair(k, p), P, step=(p == BLK - 1))
            col = lambda x: x[:, :, h:h + 1].to_broadcast([P, BLK, P])
            self.tt(wide(KB), wide(bank), col(self.gcol_bg), ALU.mult, m)
            self.mat.free[n] = self.tt(wide(KDT(h)), wide(bank), col(cols[:, 3]), ALU.mult)
            n, bank = self.mat.take()
            for p in range(BLK):
                m = self.tr(pair(bank, p), pair(v, p), P, step=(p == BLK - 1))
            vb = self.tt(wide(GAM), wide(bank), col(cols[:, 1]), ALU.mult, m)
            self.mat.free[n] = vb
            yield
            n, bank = self.mat.take()
            for p in range(BLK):
                m = self.mm(pair(bank, p), pair(TT, p), pair(GAM, p), True, True, vb, tm, step=(p == BLK - 1))
            self.mat.free[n] = self.act(UV[:, h, :], bank, ACT.Copy, m)
            n, bank = self.mat.take()
            for p in range(BLK):
                m = self.mm(pair(bank, p), pair(KB, p), pair(TT, p), True, True, step=(p == BLK - 1))
            self.mat.free[n] = self.act(WT(h), bank, ACT.Copy, m)
            n, bank, m = row(96)
            self.copy(elast[:, h, :], bank[:, CH - 1::CH], m)
            self.mat.free[n] = self.tt(q, q, bank, ALU.mult)
            yield

        sets = [[t(24), t(25), t(26), t(27), S[:, 0, :], S[:, 1, :], S[:, 2, :]], [t(i) for i in (67, 68, 70, 62, 72, 71, 66)]]
        for h in range(0, HEADS, 2):
            yield from in_step(head(h, *sets[0]), head(h + 1, *sets[1]))
        st = lambda c: t(24 + c % 4)
        O = [Dt(8 + h) for h in range(HEADS)]
        O4 = t(52, 4)
        UV5 = UV.rearrange("p h (b v) -> p h b v", v=P)
        b = VE.last()
        for c in range(NCH):
            r, p = (c % 2) * CH, c // 2
            if c:
                n, bank = self.mat.take()
                for h in range(HEADS):
                    m = self.mm(bank[r:r + CH, h * P:(h + 1) * P], WT(h)[:, p * P + r:p * P + r + CH],
                                st(c)[:, h * P:(h + 1) * P], True, True, b, self.AC.last(), step=(h == HEADS - 1))
                b = self.tt(UV5[r:r + CH, :, p, :], UV5[r:r + CH, :, p, :], wide(bank)[r:r + CH], ALU.subtract, m)
                self.mat.free[n] = b
                yield
            else:
                b = self.AC.last()
            if c < NCH - 1:
                n, bank = self.mat.take()
                for h in range(HEADS):
                    m = self.mm(bank[:, h * P:(h + 1) * P], KDT(h)[r:r + CH, p * P:(p + 1) * P],
                                UV[r:r + CH, h, p * P:(p + 1) * P], True, True, b, step=(h == HEADS - 1))
                if c == 0:
                    b = self.copy(st(c + 1), bank, m)
                else:
                    e4 = elast[:, :, c:c + 1].to_broadcast([P, HEADS, P])
                    self.tt(wide(st(c + 1)), wide(st(c)), e4, ALU.mult, self.PE.last())
                    b = self.tt(st(c + 1), st(c + 1), bank, ALU.add, m)
                self.mat.free[n] = b
                yield
            if c % 2 == 1:
                n, bank = self.mat.take()
                for h in range(HEADS):
                    self.mm(pair(bank, h), UV[:, h, p * P:(p + 1) * P], pair(ATN(h), p), True, False, b)
                    for cc in (c - 1, c):
                        if cc:
                            m = self.mm(bank[:, h * P + (cc % 2) * CH:h * P + (cc % 2 + 1) * CH],
                                        st(cc)[:, h * P:(h + 1) * P], Dt(h)[:, cc * CH:(cc + 1) * CH], False,
                                        cc == c, step=(h == HEADS - 1 and cc == c))
                self.mat.free[n] = self.act(O4[:, :, p * P:(p + 1) * P], wide(bank), ACT.Copy, m)
        for h in range(HEADS):
            self.head_norm(O[h], Dt(12 + h), t(24 + h), "gdn_norm_g_2", S[:, h % 2, :], S[:, 2, :], None,
                           VE.last(), self.PE.last())
            yield

    def block3(self, x_marks):
        t, S, VE = self.t, self.scratch, self.VE
        name = "w_in_3"
        UU, VV, ZZ, XS, BM, CM, GATE = 0, 8, 16, 32, 48, 56, 64
        YA, YB, M, VN = (lambda k, o=o: t(o + k) for o in (32, 32, 24, 24))
        sp = self.load(t(66, 2).rearrange("p a (g i) -> p (a g) i", i=P), self.dram["w_spatial_T"]
                       .rearrange("p (g i) -> p g i", i=P), self.met)
        bs = self.load(t(68, 2).rearrange("p a t -> p (a t)"), self.dram["b_spatial_rows"], self.met)
        total = self.summed(x_marks, t, self.norm_sum(True))
        um = self.rms_norm(t, total, lambda k: t(8 + k), "norm_mix_g_3")
        raw = t(57)[0:MH, :]
        raw_mark, steps = self.narrow(raw, 24, MH, lambda k: t(8 + k), um, ACT.Copy)
        U, um = self.split_tiles(8, 16, um, steps)
        self.low_lane = self.GP
        vmk, umk = [None] * KD, [None] * KD

        def gelu_to(dst, marks):
            def evacuate(f, bank, m):
                marks[f % KD] = self.act(dst(f % KD), bank, ACT.Gelu, m)
                return marks[f % KD]
            return evacuate
        pump(self.linear(name, range(VV, VV + 8), U, um, KD, gelu_to(VN, vmk)), self.ssd_rates(raw, raw_mark), 0.5)
        uu = self.linear(name, range(UU, UU + 8), U, um, KD, gelu_to(YA, umk))
        next(uu)
        total = self.summed(vmk, VN, self.norm_sum(False))
        vm = self.layer_norm(VN, total, VN, ACT.Identity, "v_norm_g_3", "v_norm_b_3")
        for _ in range(4):
            next(uu)

        ya_marks = [None] * KD

        def spatial():
            WS = t(66, 2).rearrange("p a (g i) -> p (a g) i", i=P)
            BS = t(68, 2).rearrange("p a (g i) -> p (a g) i", i=P)
            causal = self.c("causal").unsqueeze(1).to_broadcast([P, KD, P])
            w3 = lambda x: x.rearrange("p (b i) -> p b i", i=P)
            wm = self.tt(WS, WS, causal, ALU.mult, sp, bs)
            read = [None, None]
            for g in range(KD):
                n, bank = self.mat.take()
                for c in range(BLK):
                    m = self.tr(bank[:, c * P:(c + 1) * P], VN(g)[:, c * P:(c + 1) * P], P, vm[g], step=(c == BLK - 1))
                vt = S[:, 3 + g % 2, :]
                a = self.act(vt, bank, ACT.Copy, m, read[g % 2])
                self.mat.free[n] = a
                yield
                n, bank = self.mat.take()
                for c in range(BLK):
                    m = self.mm(bank[:, c * P:(c + 1) * P], vt[:, c * P:(c + 1) * P], WS[:, g, :], True, True, a, wm,
                                step=(c == BLK - 1))
                read[g % 2] = m
                b = self.tt(w3(VN(g)), w3(bank), BS[:, g:g + 1, :].to_broadcast([P, BLK, P]), ALU.add, m)
                self.mat.free[n] = b
                b = self.tt(YA(g), YA(g), VN(g), ALU.mult, umk[g])
                ya_marks[g] = self.split(self.r(40 + g), self.r(32 + g), YA(g), b)
                yield
        mixing = spatial()
        pump(uu, mixing, 2)

        ins = [[t(48 + 12 * i + j) for j in range(6)] for i in range(2)]
        free = [None, None]
        in_marks = {}

        def inputs(g):
            x0, x1, bb, cc, z0, z1 = ins[g % 2]
            tiles = [(XS + 2 * g, x0, 2 * g), (XS + 2 * g + 1, x1, 2 * g + 1), (BM + g, bb, 16 + g),
                     (CM + g, cc, 24 + g), (ZZ + 2 * g, z0, None), (ZZ + 2 * g + 1, z1, None)]
            for j, (f, dst, ch) in enumerate(tiles):
                n, bank = self.lin.take()
                m = yield from self.product_parts(bank, name, f, U, um, KD)
                if ch is None:
                    self.lin.free[n] = in_marks[g, j] = self.act(dst, bank, ACT.Silu, m, free[g % 2])
                else:
                    raw = S[:, ch % 2, :]
                    a = self.act(raw, bank, ACT.Copy, m, in_marks.get((g, j - 2)))
                    self.lin.free[n] = a
                    for b in self.taps(dst, raw, lambda i, ch=ch: self.v("conv_w_3", i * 32 + ch),
                                       self.v("conv_b_3", ch), 4, a, free[g % 2]):
                        pass
                    in_marks[g, j] = self.act(dst, dst, ACT.Silu, b)
                yield
        pump(inputs(0), mixing, 1)
        drain(mixing)

        def gated(f, branch, proj, src, marks, kts, out):
            n, gate_bank = self.lin.take()
            gm = self.product(gate_bank, name, GATE + branch * 8 + f, U, um, KD)
            tmp = S[:, 3, :]
            a = self.act(tmp, gate_bank, ACT.Sigmoid, gm, VE.last(), bias=self.v("b_gates_3", branch * 8 + f))
            self.lin.free[n] = a
            n, bank = self.lin.take()
            m = self.product(bank, proj, f, src, marks, kts)
            self.lin.free[n] = b = self.tt(out, tmp, bank, ALU.mult, a, m)
            return b
        merged = [gated(f, 0, "w_proj_a_3", lambda k: (self.r(40 + k), self.r(32 + k)), ya_marks, KD, M(f))
                  for f in range(KD)]
        group_done, squares_used = [self.PE.last(), self.GP.last()], [None]
        last_norm = iter(())
        for g in range(MG):
            following = inputs(g + 1) if g + 1 < MG else iter(())
            marks = [in_marks[g, j] for j in range(6)]
            group_done = pump(self.ssd_group(g, ins[g % 2], marks, YB, last_norm, group_done), following, 1.1)
            free[g % 2] = [self.PE.last(), VE.last(), self.AC.last(), self.GP.last()]
            drain(following)
            last_norm = self.group_norm(g, YB, squares_used)
        drain(last_norm)
        self.low_lane = self.VE
        groups_done = [self.PE.last(), self.GP.last()]
        yb_marks = [self.split(self.r(48 + k), self.r(32 + k), YB(k), VE.last(), groups_done) for k in range(2 * KD)]
        for f in range(KD):
            gated(f, 1, "w_proj_b_3", lambda k: (self.r(48 + k), self.r(32 + k)), yb_marks, 2 * KD, S[:, 4, :])
            b = self.tt(M(f), M(f), S[:, 4, :], ALU.add)
            merged[f] = self.split(self.r(64 + f), self.r(24 + f), M(f), b)
        evac, total = self.add_to_x()
        drain(self.linear("w_out_3", range(8), lambda k: (self.r(64 + k), self.r(24 + k)), merged, KD, evac))
        um = self.rms_norm(t, total, lambda k: t(8 + k), "norm_mlp_g_3")
        u, um = self.split_tiles(8, 40, um)

        def hidden(j, out):
            n, bank = self.lin.take()
            m = self.product(bank, "w_mlp_up_3", j, u, um, KD)
            relu = S[:, j % 2, :]
            a = self.act(relu, bank, ACT.Relu, m, VE.last())
            self.lin.free[n] = a
            return self.tt(out, relu, relu, ALU.mult, a)
        evac, total = self.add_to_x()
        drain(self.feed_forward(hidden, 32, "w_mlp_down_3", evac))
        return self.rms_norm(t, total, lambda k: t(8 + k), "norm_final_g_3")

    def ssd_rates(self, raw, raw_mark):
        t, VE, CS = self.t, self.VE, self.rows[0:MH, :]
        DT, DD = t(54)[0:MH, :], t(56)[0:MH, :]
        self.ts(raw, raw, self.v("dt_bias_3", rows=MH), None, ALU.add, None, raw_mark)
        self.softplus(DT, raw, 1.0, t(60, 4).rearrange("p a t -> p (a t)"), T, MH)
        yield
        ea = self.small[0:MH, 4:5]
        a = self.act(ea, self.v("a_log_3", rows=MH), ACT.Exp, VE.last())
        self.ts(raw, DT, ea, -1.0, ALU.mult, ALU.mult, a)
        self.scan(CS, self.c("start128")[0:MH, :], raw)
        c3 = CS.rearrange("p (c i) -> p c i", i=P)
        b = self.tt(DD.rearrange("p (c i) -> p c i", i=P), c3[:, :, P - 1:P].to_broadcast([MH, BLK, P]), c3,
                    ALU.subtract)
        a = self.act(DD, DD, ACT.Exp, b)
        b = self.tt(DD, DD, DT, ALU.mult, a)
        yield
        yield
        n, bank = self.mat.take()
        for q, x in enumerate((DT, CS, DD)):
            for c in range(BLK):
                o = (q * BLK + c) * MH
                m = self.tr(bank[:, o:o + MH], x[:, c * P:(c + 1) * P], MH, b, step=(q == 2 and c == BLK - 1))
        self.mat.free[n] = self.copy(t(72)[:, 0:384], bank[:, 0:384], m)
        self.rate_columns = t(72)[:, 0:384].rearrange("p (q c h) -> p q c h", q=3, h=MH)
        yield

    def ssd_group(self, g, tiles, marks, YB, last_norm, earlier):
        t, VE = self.t, self.VE
        x0, x1, BMt, CMt, z0, z1 = tiles
        xm, bm, cm, zm = marks[0:2], marks[2], marks[3], marks[4:6]
        cols = self.rate_columns
        blk = lambda x, c: x[:, c * P:(c + 1) * P]
        wide = lambda x: x.rearrange("p (b i) -> p b i", i=P)
        CB, BT = t(54), t(55)
        XD = t(56, 2).rearrange("p a (c f) -> p (a c) f", f=256)
        XE = t(58, 2).rearrange("p a (c f) -> p (a c) f", f=256)
        L = [t(66), t(67)]
        CE = [t(68), t(69)]
        HS = t(70, 2).rearrange("p a (c f) -> p (a c) f", f=256)
        dec = self.small[:, 208:224].rearrange("p (h c) -> p h c", h=MHG)
        sts, y_steps = [], {}

        def front(hh):
            head, i = 4 * g + hh, hh % 2
            n, bank = self.lin.take()
            sel = self.c("ident")[0:MH, head:head + 1].to_broadcast([MH, P])
            m = self.mm(bank, sel, self.rows[0:MH, :], True, True, step=True)
            a = self.act(CE[i], bank, ACT.Exp, m, y_steps.get(hh - 2, earlier))
            self.copy(dec[:, hh, :], CE[i][:, P - 1::P], a)
            for c in range(BLK):
                b = self.ts(blk(L[i], c), blk(bank, c), cols[:, 1, c, head:head + 1], 0.0, ALU.subtract, ALU.min, m,
                            y_steps.get(hh - 2, earlier))
            self.lin.free[n] = b
            a = self.act(L[i], L[i], ACT.Exp, b)
            ce = self.tt(CE[i], CE[i], CMt, ALU.mult, b, lane=self.GP)
            hsl = slice(hh * MP, (hh + 1) * MP)
            for c in range(BLK - 1):
                ns, sbank, sm = sts[c]
                s = sbank[:, (c % 2) * 256 + hh * MP:(c % 2) * 256 + (hh + 1) * MP]
                if c == 0:
                    hb = self.copy(HS[:, 1, hsl], s, sm)
                else:
                    hb = self.stt(HS[:, c + 1, hsl], HS[:, c, hsl], dec[:, hh, c:c + 1], s, ALU.mult, ALU.add, sm)
                self.mat.free[ns] = hb
            return self.tt(L[i], L[i], CB, ALU.mult, a), ce, hb

        n, bank = self.mat.take()
        for c in range(BLK):
            m = self.mm(blk(bank, c), blk(BMt, c), blk(CMt, c), True, True, bm, cm, step=(c == BLK - 1))
        causal = self.c("causal").unsqueeze(1).to_broadcast([P, BLK, P])
        self.mat.free[n] = self.tt(wide(CB), wide(bank), causal, ALU.mult, m)
        n, bank = self.mat.take()
        for c in range(BLK):
            m = self.tr(blk(bank, c), blk(BMt, c), P, step=(c == BLK - 1))
        self.mat.free[n] = bt = self.act(BT, bank, ACT.Copy, m, earlier)
        next(last_norm, None)
        yield
        for i, x in enumerate((x0, x1)):
            n, bank = self.mat.take()
            for c in range(BLK):
                m = self.tr(blk(bank, c), blk(x, c), P, xm[i], step=(c == BLK - 1))
            x4 = bank.rearrange("p (c e f) -> p c e f", c=BLK, e=2)
            h0 = 4 * g + 2 * i
            for q, dst in ((0, XD), (2, XE)):
                col = cols[:, q, :, h0:h0 + 2].unsqueeze(3).to_broadcast([P, BLK, 2, MP])
                d4 = dst[:, :, i * P:(i + 1) * P].rearrange("p c (e f) -> p c e f", e=2)
                xe = self.tt(d4, x4, col, ALU.mult, m, earlier)
            self.mat.free[n] = xe
        next(last_norm, None)
        yield
        next(last_norm, None)
        yield
        for c in range(BLK - 1):
            if c % 2 == 0:
                n, bank = self.mat.take()
            m = self.mm(bank[:, (c % 2) * 256:(c % 2 + 1) * 256], blk(BT, c), XE[:, c, :], True, True, xe, bt,
                        step=True)
            sts.append((n, bank, m))
        ready = front(0)
        yield
        for hh in range(MHG):
            i, hsl = hh % 2, slice(hh * MP, (hh + 1) * MP)
            ahead = front(hh + 1) if hh + 1 < MHG else None
            yield
            if i == 0:
                yn, ybank = self.mat.take()
            r = i * MP
            for c in range(BLK):
                m = self.mm(blk(ybank, c)[r:r + MP], XD[:, c, hsl], blk(L[i], c), True, c == 0, *ready)
                if c:
                    m = self.mm(blk(ybank, c)[r:r + MP], HS[:, c, hsl], blk(CE[i], c), False, True,
                                step=(c == BLK - 1))
            y_steps[hh] = m
            if i == 1:
                k = hh // 2
                y = YB(2 * g + k)
                self.mat.free[yn] = self.stt(y, (x0, x1)[k], self.v("d_skip_3", 2 * g + k), ybank, ALU.mult,
                                             ALU.add, m)
                self.tt(y, y, (z0, z1)[k], ALU.mult, zm[k])
            ready = ahead
            yield
        return m

    def group_norm(self, g, YB, squares_used):
        S, y_mark = self.scratch, self.VE.last()
        n, bank = self.mat.take()
        for k in range(2):
            a = self.act(S[:, 3 + k, :], YB(2 * g + k), ACT.Square, y_mark, squares_used[0])
            m = self.mm(bank, self.c("mean_group"), S[:, 3 + k, :], k == 0, k == 1, a, step=True)
        squares_used[0] = m
        yield
        r = self.inverse_std(bank, n, m, 1e-6, S[:, 2, :], self.mat)
        yield
        for k in range(2):
            self.stt(YB(2 * g + k), YB(2 * g + k), self.v("ssm_norm_g_3", 2 * g + k), S[:, 2, :], ALU.mult, ALU.mult, r)
        yield

    def build(self):
        self.setup()
        x_marks = self.block1()
        self.dbg(x_marks, 0)
        x_marks = self.block2(x_marks)
        self.dbg(x_marks, 1)
        self.met = self.meet()
        om = self.block3(x_marks)
        out_sem = self.semaphore("stored")
        o = self.dram["out"].rearrange("p (k t) -> p k t", k=KD)
        self.SP.issue(lambda e: e.dma_start(o, self.t(8, 8)).then_inc(out_sem, 16), *om)
        self.SP.wait(("stored", out_sem, 16))

    def run(self):
        with self.nc.Block() as block:
            @block.tensor
            def _(e):
                self.PE.run(e)

            @block.scalar
            def _(e):
                self.AC.run(e)

            @block.vector
            def _(e):
                self.VE.run(e)

            @block.gpsimd
            def _(e):
                self.GP.run(e)

            @block.sync
            def _(e):
                self.SP.run(e)

    def dbg(self, marks, i):
        pass


INPUTS = [("x", (P, KD * T)), ("c", (1, D)), ("c_columns", (P, KD)), ("vectors", (P, NVEC)), ("constants", (P, NCONST)),
          ("small_weights", (P, KD * 64)), ("gla_w_gate_up", (16, T)), ("rel_rows", (P, ATT_HEADS * T)),
          ("w_spatial_T", (P, KD * P)), ("b_spatial", (1, KD * P))]


def build_program(nc, out_shape=(P, KD * T)):
    dram = {name: nc.dram_tensor(name, shape, F32, kind="ExternalInput").ap() for name, shape in INPUTS}
    n_blocks = weight_blocks()
    dram["weights"] = nc.dram_tensor("weights", (n_blocks * P * P,), F32, kind="ExternalInput").ap()
    dram["out"] = nc.dram_tensor("out", out_shape, F32, kind="ExternalOutput").ap()
    dram["c_rows"] = bass.AP(dram["c"].tensor, 0, [[0, P], [1, D]])
    dram["b_spatial_rows"] = bass.AP(dram["b_spatial"].tensor, 0, [[0, P], [1, KD * P]])
    memory = Memory(nc)
    first = Program(nc, dram, memory)
    first.build()
    plan = first.plan
    program = Program(nc, dram, memory, plan)
    program.build()
    program.run()
    assert sum(map(len, plan)) == n_blocks
    return plan


def weight_blocks():
    swiglu = 3 * KD * KF
    one = 72 * KD + 2 * swiglu + KD * 48 + 2 * KD + 3 * KD * KD
    two = KD * 68 + 3 * 4 * KD + KD * KD + swiglu
    three = KD * 80 + KD * KD + 2 * KD * KD + KD * KD + 2 * KD * 32
    return one + two + three


def lay_out(inputs, plan):
    a = {k: np.asarray(v) for k, v in inputs.items()}
    a = {k: (v[0] if k.endswith(("_2", "_3")) and k not in ("final_norm_g_2", "norm_final_g_3") else v)
         for k, v in a.items()}
    columns = lambda v: np.ascontiguousarray(v).reshape(-1, P).T
    a["d_skip_3"] = np.repeat(a["d_skip_3"], MP)
    vectors = np.zeros((P, NVEC), np.float32)
    for name, w in VECTORS:
        c = VCOL[name]
        if name in ("gdn_a_log_2", "gdn_dt_bias_2", "dt_bias_3", "a_log_3"):
            vectors[:a[name].size, c] = a[name]
        else:
            vectors[:, c:c + w] = columns(a[name])
    w2, w3 = a["w_in_2"], a["w_in_3"]
    a["w_in_2"] = np.concatenate([w2[:, :2048], w2[:, 2064:5648], w2[:, 5656:]], axis=1)
    a["w_in_3"] = np.concatenate([w3[:, :8192], w3[:, 8224:]], axis=1)
    small = np.zeros((D, 64), np.float32)
    small[:, 0:16], small[:, 16:24], small[:, 24:56] = w2[:, 2048:2064], w2[:, 5648:5656], w3[:, 8192:8224]
    small = small.reshape(KD, P, 64).transpose(1, 0, 2).reshape(P, KD * 64)
    rel = a["att_rel_bias_2"][:, ::-1]
    padded = np.zeros((ATT_HEADS, 640), np.float32)
    padded[:, :255] = rel[:, :1]
    padded[:, 255:255 + REL] = rel
    rows = np.stack([padded[:, P - 1 - p:P - 1 - p + T] for p in range(P)]).reshape(P, ATT_HEADS * T)
    for name in ("rglru_w_r", "rglru_w_i"):
        a[name] = a[name].reshape(D, P)
    stream = np.empty((weight_blocks() * P * P,), np.float32)
    at = 0
    for blocks in plan:
        n = len(blocks)
        part = stream[at:at + n * P * P].reshape(P, n, P)
        for i, (name, k, f) in enumerate(blocks):
            w = a["ada_w"] if name == "ada_w_T" else a[name]
            b = w[k * P:(k + 1) * P, f * P:(f + 1) * P]
            part[:, i, :] = b.T if name == "ada_w_T" else b
        at += n * P * P
    spatial = a["w_spatial_3"].transpose(2, 0, 1).reshape(P, KD * P)
    x = a["x"].reshape(T, KD, P).transpose(2, 1, 0).reshape(P, KD * T)
    return {"x": np.ascontiguousarray(x), "c": a["c"].reshape(1, D), "c_columns": np.ascontiguousarray(columns(a["c"])), "vectors": vectors, "constants": constants(),
            "small_weights": np.ascontiguousarray(small), "gla_w_gate_up": np.ascontiguousarray(a["gla_w_gate_up_2"]),
            "rel_rows": rows, "w_spatial_T": np.ascontiguousarray(spatial),
            "b_spatial": np.ascontiguousarray(a["b_spatial_3"]).reshape(1, KD * P), "weights": stream}


def kernel(**inputs):
    import concourse.bacc as bacc
    from concourse.bass_utils import run_bass_kernel_spmd

    nc = bacc.Bacc("TRN2", target_bir_lowering=False, num_devices=1)
    plan = build_program(nc)
    result = run_bass_kernel_spmd(nc, [lay_out(inputs, plan)], core_ids=[0])
    out = result.results[0]["out"]
    return np.ascontiguousarray(out.reshape(P, KD, T).transpose(2, 1, 0)).reshape(1, T, D)
```

```python
import itertools

import numpy as np
import concourse.bass as bass
from concourse import mybir

F32 = mybir.dt.float32
F32R = mybir.dt.float32r
ALU = mybir.AluOpType
ACT = mybir.ActivationFunctionType
AX = mybir.AxisListType

P = 128
T = 512
D = 1024
KD = D // P
BLK = T // P
FF = 2816
KF = FF // P
UNIT = 8
RING = 5
HIGH_RING = 3
SBUF_START = 16512
AHEAD = 3
WORK = 73
ALPHA = 2.0 ** 0.25
CH = 64
NCH = T // CH
LEVELS = (32, 16, 8, 4, 2, 1)
HEADS = 4
DK = 128
ATT_HEADS, ATT_HD = 8, 64
REL = 320
MH, MG, MP = 32, 8, 64
MHG = MH // MG
CONF_TAPS = 31
NEG = -1.0e30

VECTORS = [
    ("ada_b", 72), ("ln1_g", 8), ("ln1_b", 8), ("rnn_conv_w", 32), ("rnn_conv_b", 8), ("rglru_b_r", 8),
    ("rglru_b_i", 8), ("rglru_lambda", 8), ("conf_dw_w", 8 * CONF_TAPS), ("conf_dw_b", 8), ("conf_ln_g", 8),
    ("conf_ln_b", 8), ("ln2_g", 8), ("ln2_b", 8), ("ln3_g", 8), ("ln3_b", 8),
    ("mix_norm_g_2", 8), ("gla_b_gate_2", 4), ("gla_norm_g_2", 1), ("gdn_conv_w_2", 48), ("gdn_norm_g_2", 1),
    ("ffn_norm_g_2", 8), ("final_norm_g_2", 8),
    ("norm_mix_g_3", 8), ("conv_w_3", 128), ("conv_b_3", 32), ("ssm_norm_g_3", 16), ("v_norm_g_3", 8),
    ("v_norm_b_3", 8), ("b_gates_3", 16), ("norm_mlp_g_3", 8), ("norm_final_g_3", 8), ("d_skip_3", 16),
    ("gdn_a_log_2", 1), ("gdn_dt_bias_2", 1), ("dt_bias_3", 1), ("a_log_3", 1),
]
VCOL = {}
_n = 0
for _name, _w in VECTORS:
    VCOL[_name] = _n
    _n += _w
NVEC = _n

CONSTS = [("ident", P), ("one", P), ("mean_model", P), ("mean_head", P), ("mean_group", P),
          ("incl64", P), ("strict64", P), ("causal", P)] + [(f"level{s}", P) for s in LEVELS] + [
          ("start64", T), ("start128", T)]
CCOL = {}
_n = 0
for _name, _w in CONSTS:
    CCOL[_name] = (_n, _w)
    _n += _w
NCONST = _n


def constants():
    j, i = np.meshgrid(np.arange(P), np.arange(P), indexing="ij")
    same = j // CH == i // CH
    made = {
        "ident": j == i, "one": np.ones((P, P)), "mean_model": np.full((P, P), 1.0 / D),
        "mean_head": np.full((P, P), 1.0 / DK), "mean_group": np.full((P, P), 1.0 / 256),
        "incl64": same & (j <= i), "strict64": same & (j < i), "causal": j <= i,
        "start64": np.broadcast_to(np.arange(T) % CH != 0, (P, T)),
        "start128": np.broadcast_to(np.arange(T) % P != 0, (P, T)),
    }
    for s in LEVELS:
        made[f"level{s}"] = (j // (2 * s) == i // (2 * s)) & (j % (2 * s) < s) & (i % (2 * s) >= s)
    return np.concatenate([made[n].astype(np.float32) for n, _ in CONSTS], axis=1)


SPLIT = {"w_in", "rnn_w_proj", "conf_w_proj", "mix_w_out", "ffn1_w_gate", "ffn1_w_up",
         "ffn1_w_down", "ffn2_w_gate", "ffn2_w_up", "ffn2_w_down", "w_out_2", "w_ffn_in_2",
         "w_ffn_out_2", "w_in_3", "w_proj_a_3", "w_proj_b_3", "w_out_3", "w_mlp_up_3",
         "w_mlp_down_3"}


class Lane:

    def __init__(self, sem, name, chained):
        self.sem, self.name, self.chained = sem, name, chained
        self.count, self.queue, self.seen = 0, [], {}

    def last(self):
        return (self.name, self.sem, self.count) if self.count else None

    def wait(self, *marks):
        for m in marks:
            if m is None:
                continue
            if isinstance(m, list):
                self.wait(*m)
                continue
            name, sem, value = m
            if self.seen.get(name, 0) < value:
                self.seen[name] = value
                self.queue.append(lambda e, s=sem, v=value: e.wait_ge(s, v))

    def issue(self, make, *marks):
        self.wait(*marks)
        self.queue.append(make)

    def step(self, make, *marks):
        if self.chained:
            self.wait(self.last())
        self.wait(*marks)
        self.count += 1
        self.queue.append(lambda e: make(e).then_inc(self.sem, 1))
        return self.last()

    def run(self, engine):
        for make in self.queue:
            make(engine)


class Banks:

    def __init__(self, pe, tensors):
        self.pe, self.aps, self.free, self.at = pe, [t[:, :] for t in tensors], [None] * len(tensors), 0

    def take(self):
        n = self.at
        self.at = (n + 1) % len(self.aps)
        self.pe.wait(self.free[n])
        return n, self.aps[n]


def pump(main, filler, per):
    due = 0.0
    while True:
        try:
            next(main)
        except StopIteration as end:
            return end.value
        due += per
        while due >= 1.0:
            due -= 1.0
            next(filler, None)


def in_step(*gens):
    live = list(gens)
    while live:
        for g in list(live):
            if next(g, live) is live:
                live.remove(g)
        yield


def drain(*gens):
    for g in gens:
        for _ in g:
            pass


class Memory:

    def __init__(self, nc):
        self.nc, self.at = nc, SBUF_START
        self.work = self.place("work", [P, WORK, T], F32)
        self.work_r = [self.place(f"work_split{i}", [P, min(8, WORK - i), T], F32R, over=self.work_at + i * T * 4)
                       for i in range(0, WORK, 8)]
        self.ring = self.place("weight_ring", [P, RING, UNIT * P], F32)
        self.ring_r = self.place("weight_ring_low", [P, RING, UNIT * P], F32R, over=self.weight_ring_at)
        self.high = self.place("weight_ring_high", [P, HIGH_RING, UNIT * P], F32R)
        self.scratch = self.place("scratch", [P, 5, T], F32)
        self.vec = self.place("vector_columns", [P, NVEC], F32)
        self.con = self.place("constant_columns", [P, NCONST], F32)
        self.mod = self.place("modulation", [P, 72], F32)
        self.small = self.place("small", [P, 344], F32)
        self.small_w = self.place("narrow_weights", [P, KD, 64], F32)
        self.rows = self.place("rows", [P, T], F32)
        self.banks = [nc.alloc_psum_tensor(f"bank{i}", [P, T], F32) for i in range(8)]

    def place(self, name, shape, dtype, over=None):
        offset = self.at if over is None else over
        if name == "work":
            self.work_at = offset
        if name == "weight_ring":
            self.weight_ring_at = offset
        if over is None:
            self.at += -(-int(np.prod(shape[1:])) * 4 // 32) * 32
        return self.nc.alloc_sbuf_tensor_at(name, shape, dtype, offset=offset)


class Program:

    def __init__(self, nc, dram, memory, order=None):
        self.nc, self.dram, self.order = nc, dram, order
        self.plan, self.plan_cols = [], 0
        self.PE = Lane(self.semaphore("pe_steps"), "pe_steps", False)
        self.AC = Lane(self.semaphore("act_steps"), "act_steps", True)
        self.VE = Lane(self.semaphore("dve_steps"), "dve_steps", True)
        self.GP = Lane(self.semaphore("pool_steps"), "pool_steps", True)
        self.SP = Lane(self.semaphore("sp_steps"), "sp_steps", False)

        self.ring, self.ring_r, self.high = memory.ring, memory.ring_r, memory.high
        self.ring_sem = [self.semaphore(f"ring_loaded{i}") for i in range(RING)]
        self.ring_loads = [0] * RING
        self.ring_free, self.high_free = [None] * RING, [None] * HIGH_RING
        self.ring_at = self.high_at = 0
        self.loaded, self.prepared, self.in_use = [], [], []
        self.low_lane = self.VE
        self.work, self.work_r, self.scratch, self.vec = memory.work, memory.work_r, memory.scratch, memory.vec
        self.con, self.mod, self.small, self.small_w = memory.con, memory.mod, memory.small, memory.small_w
        self.rows = memory.rows
        self.gate_up = self.rows[0:16, :]
        self.lin = Banks(self.PE, memory.banks[:4])
        self.mat = Banks(self.PE, memory.banks[4:])
        self.load_count = 0

    def semaphore(self, name):
        return self.nc.alloc_semaphore(name) if self.order is not None else None

    def t(self, i, n=None):
        return self.work[:, i, :] if n is None else self.work[:, i:i + n, :]

    def r(self, i):
        return self.work_r[i // 8][:, i % 8, :]

    def v(self, name, j=0, rows=P):
        c = VCOL[name] + j
        return self.vec[0:rows, c:c + 1]

    def c(self, name):
        a, w = CCOL[name]
        return self.con[:, a:a + w]

    def load(self, out, src, *marks):
        self.load_count += 1
        name = f"load{self.load_count}"
        sem = self.semaphore(name)
        self.SP.issue(lambda e: e.dma_start(out, src).then_inc(sem, 16), *marks)
        return name, sem, 16

    def unit(self, blocks):
        self.plan.append(blocks)
        if self.order is None:
            self.loaded.append(self.load_unit(blocks))
            self.prepared.append(self.split_unit(*self.loaded.pop()))
        else:
            next_load = len(self.plan) - 1 + len(self.prepared) + len(self.loaded)
            for blocks in self.order[next_load:next_load + RING]:
                if len(self.in_use) + len(self.prepared) + len(self.loaded) < RING:
                    self.loaded.append(self.load_unit(blocks))
            while self.loaded and len(self.prepared) <= AHEAD:
                highs = [slots for slots in self.in_use + [slots for _, _, slots in self.prepared]
                         if slots[1] is not None]
                if len(highs) == HIGH_RING:
                    break
                self.prepared.append(self.split_unit(*self.loaded.pop(0)))
        unit = self.prepared.pop(0)
        self.in_use.append(unit[2])
        return unit

    def load_unit(self, blocks):
        slot = self.ring_at
        self.ring_at = (slot + 1) % RING
        cols = len(blocks) * P
        src = self.dram["weights"][self.plan_cols * P:(self.plan_cols + cols) * P].rearrange("(p c) -> p c", p=P)
        self.plan_cols += cols
        self.ring_loads[slot] += 1
        dst = self.ring[:, slot, 0:cols]
        sem = self.ring_sem[slot]
        self.SP.issue(lambda e: e.dma_start(dst, src).then_inc(sem, 16), self.ring_free[slot])
        return blocks[0][0] in SPLIT, slot, cols, (f"ring{slot}", sem, 16 * self.ring_loads[slot])

    def split_unit(self, is_split, slot, cols, loaded):
        dst = self.ring[:, slot, 0:cols]
        if not is_split:
            return dst, loaded, (slot, None)
        high_slot = self.high_at
        self.high_at = (high_slot + 1) % HIGH_RING
        high, low = self.high[:, high_slot, 0:cols], self.ring_r[:, slot, 0:cols]
        mark = self.split(high, low, dst, loaded, self.high_free[high_slot], lane=self.low_lane)
        return (high, low), mark, (slot, high_slot)

    def release(self, slots, mark):
        self.in_use.remove(slots)
        self.ring_free[slots[0]] = mark
        if slots[1] is not None:
            self.high_free[slots[1]] = mark

    def split(self, high, low, x, *marks, lane=None, after=None):
        a = self.act(high, x, ACT.Copy, *marks)
        return self.tt(low, x, high, ALU.subtract, a, after, lane=lane)

    def split_tiles(self, first, high, marks, after=(None,) * KD):
        marks = [self.split(self.r(high + k), self.r(first + k), self.t(first + k), marks[k], after=after[k],
                            lane=self.GP if k % 2 else self.VE)
                 for k in range(KD)]
        return (lambda k: (self.r(high + k), self.r(first + k))), marks

    def act(self, out, x, func, *marks, scale=1.0, bias=0.0, total=None):
        kw = {} if total is None else {"accum_out": total}
        if func == ACT.Copy:
            return self.AC.step(lambda e: e.activation(out, x, func, scale=scale), *marks)
        return self.AC.step(lambda e: e.activation(out, x, func, scale=scale, bias=bias, **kw), *marks)

    def tt(self, out, a, b, op, *marks, lane=None):
        return (lane or self.VE).step(lambda e: e.tensor_tensor(out, a, b, op), *marks)

    def ts(self, out, a, s1, s2, op0, op1, *marks, lane=None):
        if op1 is None:
            return (lane or self.VE).step(lambda e: e.tensor_scalar(out, a, s1, None, op0), *marks)
        return (lane or self.VE).step(lambda e: e.tensor_scalar(out, a, s1, s2, op0, op1), *marks)

    def stt(self, out, a, s, b, op0, op1, *marks):
        return self.VE.step(lambda e: e.scalar_tensor_tensor(out=out, in0=a, scalar=s, in1=b, op0=op0, op1=op1),
                            *marks)

    def copy(self, out, x, *marks):
        return self.VE.step(lambda e: e.tensor_copy(out, x), *marks)

    def scan(self, out, keep, x, *marks):
        return self.VE.step(lambda e: e.tensor_tensor_scan(out, keep, x, 0.0, ALU.mult, ALU.add), *marks)

    def mm(self, out, lhsT, rhs, start, stop, *marks, step=False):
        make = lambda e: e.matmul(out, lhsT, rhs, start=start, stop=stop, skip_group_check=True)
        return self.PE.step(make, *marks) if step else self.PE.issue(make, *marks)

    def tr(self, out, x, rows, *marks, step=False):
        ident = self.c("ident")[0:rows, 0:rows]
        make = lambda e: e.transpose(out, x, ident)
        return self.PE.step(make, *marks) if step else self.PE.issue(make, *marks)

    def meet(self):
        lanes = [self.PE, self.AC, self.VE, self.GP]
        marks = [x.last() for x in lanes]
        for x in lanes:
            x.wait(*[m for y, m in zip(lanes, marks) if y is not x])
        return marks

    def product_parts(self, bank, name, f, src, marks, kts):
        kts = range(kts) if isinstance(kts, int) else kts
        last = None
        for k0 in range(kts[0], kts[-1] + 1, UNIT):
            ks = range(k0, min(k0 + UNIT, kts[-1] + 1))
            w, loaded, slot = self.unit([(name, k, f) for k in ks])
            self.PE.wait(loaded)
            for k in ks:
                block = slice((k - k0) * P, (k - k0 + 1) * P)
                first, end, mark = k == kts[0], k == kts[-1], marks[k] if marks else None
                if isinstance(w, tuple):
                    high, low = src(k)
                    self.mm(bank, w[0][:, block], high, first, False, mark)
                    self.mm(bank, w[0][:, block], low, False, False)
                    last = self.mm(bank, w[1][:, block], high, False, end, step=(k == ks[-1]))
                else:
                    last = self.mm(bank, w[:, block], src(k), first, end, mark, step=(k == ks[-1]))
                if k == ks[-1]:
                    self.release(slot, last)
                if k % 4 == 3 and not end:
                    yield
        return last

    def product(self, *args):
        parts = self.product_parts(*args)
        while True:
            try:
                next(parts)
            except StopIteration as end:
                return end.value

    def linear(self, name, fs, src, marks, kts, evacuate, fine=False):
        for f in fs:
            n, bank = self.lin.take()
            if fine:
                m = yield from self.product_parts(bank, name, f, src, marks, kts)
            else:
                m = self.product(bank, name, f, src, marks, kts)
            self.lin.free[n] = evacuate(f, bank, m)
            yield

    def token_major(self, name, f0, src, marks, out, done):
        banks = [self.lin.take() for _ in range(BLK)]
        for k0 in range(0, KD, 2):
            w, loaded, slot = self.unit([(name, k, f0 + f) for k in (k0, k0 + 1) for f in range(4)])
            self.PE.wait(loaded)
            for k in (k0, k0 + 1):
                for b in range(BLK):
                    m = self.mm(banks[b][1], src(k)[:, b * P:(b + 1) * P], w[:, (k - k0) * T:(k - k0 + 1) * T],
                                k == 0, k == KD - 1, marks[k] if marks else None, step=(k % 2 == 1 and b == BLK - 1))
                if k % 2 == 1:
                    self.release(slot, m)
                yield
        for b in range(BLK):
            done[b] = self.act(out(b), banks[b][1], ACT.Copy, m)
            self.lin.free[banks[b][0]] = done[b]
        yield

    def inverse_std(self, bank, n, mark, eps, std, pool):
        a = self.act(std, bank, ACT.Sqrt, mark, self.VE.last(), bias=self.eps[eps])
        pool.free[n] = a
        return self.VE.step(lambda e: e.reciprocal(std, std), a)

    def norm_sum(self, square):
        n, bank = self.mat.take()
        S, read, held = self.scratch, [None, None], []

        def flush():
            for k, x, m in held:
                read[k % 2] = self.mm(bank, self.c("mean_model"), x, k == 0, k == KD - 1, m, step=True)
            held.clear()
            return read[(KD - 1) % 2]

        def add(k, x, mark):
            flush()
            if square:
                mark = self.act(S[:, k % 2, :], x, ACT.Square, mark, read[k % 2])
                x = S[:, k % 2, :]
            held.append((k, x, mark))
        return n, bank, add, flush

    def layer_norm(self, pre, total, out, evacuate_func, g, b):
        S = self.scratch
        n, bank, _, flush = total
        m = flush()
        n2, bank2, add, flush2 = self.norm_sum(True)
        for k in range(KD):
            cen = self.tt(pre(k), pre(k), bank, ALU.subtract, m)
            add(k, pre(k), cen)
        self.mat.free[n] = cen
        r = self.inverse_std(bank2, n2, flush2(), 1e-5, S[:, 2, :], self.mat)
        marks = []
        for k in range(KD):
            y = self.tt(pre(k), pre(k), S[:, 2, :], ALU.mult, r)
            marks.append(self.act(out(k), pre(k), evacuate_func, y, scale=self.v(g, k), bias=self.v(b, k)))
        return marks

    def rms_norm(self, x, total, out, g):
        S = self.scratch
        n, bank, _, flush = total
        r = self.inverse_std(bank, n, flush(), 1e-6, S[:, 2, :], self.mat)
        return [self.stt(out(k), x(k), self.v(g, k), S[:, 2, :], ALU.mult, ALU.mult, r) for k in range(KD)]

    def summed(self, marks, x, total):
        for k in range(KD):
            total[2](k, x(k), marks[k])
        return total

    def setup(self):
        d = self.dram
        self.c_row = self.t(52, 2).rearrange("p a t -> p (a t)")
        crl = self.load(self.c_row, d["c_rows"])
        cvl = self.load(self.small[:, 336:344], d["c_columns"])
        vl = self.load(self.vec[:, :], d["vectors"])
        self.late_loads = lambda: [
            self.load(self.t(0, 8), d["x"].rearrange("p (k t) -> p k t", k=KD)),
            self.load(self.con[:, :], d["constants"]),
            self.load(self.small_w[:, :, :], d["small_weights"].rearrange("p (k m) -> p k m", k=KD)),
            self.load(self.gate_up, d["gla_w_gate_up"])]
        for lane in (self.PE, self.AC, self.VE, self.GP):
            lane.wait(crl, cvl, vl)
        self.eps = {1e-5: self.small[:, 0:1], 1e-6: self.small[:, 1:2]}
        self.unit_bias = self.small[:, 2:3]
        self.zero_bias = self.small[:, 3:4]
        for i, val in enumerate((1e-5, 1e-6, 1.0, 0.0)):
            self.VE.step(lambda e, i=i, val=val: e.memset(self.small[:, i:i + 1], val))
        self.AC.wait(self.VE.last())

    def modulation(self, lo, hi, on_pe=False):
        if on_pe:
            n, bank = self.mat.take()
            for j in range(lo, hi):
                w, loaded, slot = self.unit([("ada_w", k, j) for k in range(KD)])
                self.PE.wait(loaded)
                for k in range(KD):
                    m = self.mm(bank[:, j - lo:j - lo + 1], w[:, k * P:(k + 1) * P], self.c_col[:, k:k + 1], k == 0,
                                k == KD - 1, self.c_ready, step=(k == KD - 1))
                self.release(slot, m)
            self.mat.free[n] = self.copy(self.mod[:, lo:hi], bank[:, 0:hi - lo], m)
        for j in [] if on_pe else range(lo, hi):
            w, loaded, slot = self.unit([("ada_w_T", k, j) for k in range(KD)])
            junk = self.scratch[:, 3:5, :].rearrange("p a t -> p (a t)")
            m = self.VE.step(lambda e, w=w, j=j: e.tensor_tensor_reduce(
                out=junk, in0=w, in1=self.c_act, scale=1.0, scalar=0.0, op0=ALU.mult, op1=ALU.add,
                accum_out=self.mod[:, j:j + 1]), loaded, self.c_ready)
            self.release(slot, m)
            yield
        self.tt(self.mod[:, lo:hi], self.mod[:, lo:hi], self.vec[:, VCOL["ada_b"] + lo:VCOL["ada_b"] + hi], ALU.add)
        for which in range(9):
            a, b = which * 8, which * 8 + 8
            if lo <= a and b <= hi and which % 3 == 1:
                self.ts(self.mod[:, a:b], self.mod[:, a:b], 1.0, None, ALU.add, None)
            if lo <= a and b <= hi and which % 3 == 2:
                w = 1.0 if which == 5 else 0.5
                self.ts(self.mod[:, a:b], self.mod[:, a:b], 1.0, w, ALU.add, ALU.mult)
        yield

    def feed_forward(self, hidden, n_hidden, down, evacuate):
        for first in range(0, n_hidden, 8):
            ks = range(first, min(first + 8, n_hidden))
            marks = {}
            for j in ks:
                i = j % 8
                mark = hidden(j, self.t(24 + i))
                marks[j] = self.split(self.r(32 + i), self.r(24 + i), self.t(24 + i), mark)
                yield
            for f in range(KD):
                n, bank = self.lin.take()
                m = self.product(bank, down, f, lambda k: (self.r(32 + k % 8), self.r(24 + k % 8)), marks, ks)
                self.lin.free[n] = evacuate(f, bank, m, ks[-1] == n_hidden - 1)
                yield

    def swiglu(self, u, u_marks, gate, up, down, evacuate):
        tmp_read = [None, None]

        def hidden(j, out):
            n, gbank = self.lin.take()
            gm = self.product(gbank, gate[0], gate[1] + j, u, u_marks, KD)
            tmp = self.scratch[:, j % 2, :]
            a = self.act(tmp, gbank, ACT.Silu, gm, tmp_read[j % 2])
            self.lin.free[n] = a
            n2, ubank = self.lin.take()
            um = self.product(ubank, up[0], up[1] + j, u, u_marks, KD)
            self.lin.free[n2] = tmp_read[j % 2] = self.tt(out, tmp, ubank, ALU.mult, a, um)
            return tmp_read[j % 2]
        return self.feed_forward(hidden, KF, down, evacuate)

    def modulated(self, which, x_marks):
        sh, sc = 24 * which, 24 * which + 8
        return [self.ts(self.t(8 + k), self.t(k), self.mod[:, sc + k:sc + k + 1], self.mod[:, sh + k:sh + k + 1],
                        ALU.mult, ALU.add, x_marks[k]) for k in range(KD)]

    def residual(self, which, pre, base):
        total = self.norm_sum(False)

        def evacuate(f, bank, m, last=True):
            c = 24 * which + 16 + f
            mark = self.stt(pre(f), bank, self.mod[:, c:c + 1], pre(f), ALU.mult, ALU.add, m, base[f])
            if last:
                total[2](f, pre(f), mark)
            return mark
        return evacuate, total

    def add_to_x(self):
        total = self.norm_sum(True)

        def evacuate(f, bank, m, last=True):
            mark = self.tt(self.t(f), self.t(f), bank, ALU.add, m)
            if last:
                total[2](f, self.t(f), mark)
            return mark
        return evacuate, total

    def scaled_x(self, pre, x_marks):
        return [self.ts(pre(k), self.t(k), ALPHA, None, ALU.mult, None, x_marks[k], lane=self.GP) for k in range(KD)]

    def block1(self):
        t = self.t
        self.c_act, self.c_col = self.c_row, self.small[:, 336:344]
        self.act(self.c_col, self.c_col, ACT.Silu)
        self.c_ready = self.act(self.c_act, self.c_row, ACT.Silu)
        lam = self.vec[:, VCOL["rglru_lambda"]:VCOL["rglru_lambda"] + 8]
        rate = self.small[:, 8:16]
        neg_rate = self.small[:, 16:24]
        self.softplus(rate, lam, -1.0, self.small[:, 24:64], 8, P)
        self.ts(rate, rate, 8.0, None, ALU.mult, None)
        self.rate = rate, neg_rate, self.ts(neg_rate, rate, -1.0, None, ALU.mult, None)
        drain(self.modulation(0, 8, on_pe=True))
        late = self.late_loads()
        drain(self.modulation(8, 16, on_pe=True))
        for lane in (self.PE, self.AC, self.VE, self.GP):
            lane.wait(*late)
        x_marks = [None] * KD
        pre = lambda k: t(16 + k)
        u_marks = self.modulated(0, x_marks)
        base = self.scaled_x(pre, x_marks)
        evac, pm = self.residual(0, pre, base)
        u, u_marks = self.split_tiles(8, 40, u_marks)
        rest = itertools.chain(self.modulation(16, 24), self.modulation(24, 72))
        pump(self.swiglu(u, u_marks, ("ffn1_w_gate", 0), ("ffn1_w_up", 0), "ffn1_w_down", evac), rest, 1.3)
        drain(rest)
        x_marks = self.layer_norm(pre, pm, lambda k: t(k), ACT.Identity, "ln1_g", "ln1_b")
        x_marks = self.mixer1(x_marks)
        u_marks = self.modulated(2, x_marks)
        base = self.scaled_x(pre, x_marks)
        evac, pm = self.residual(2, pre, base)
        u, u_marks = self.split_tiles(8, 40, u_marks)
        drain(self.swiglu(u, u_marks, ("ffn2_w_gate", 0), ("ffn2_w_up", 0), "ffn2_w_down", evac))
        return self.layer_norm(pre, pm, lambda k: t(k), ACT.Identity, "ln3_g", "ln3_b")

    def taps(self, out, x, w, b, n_taps, *marks):
        if b is None:
            m = self.ts(out, x, w(n_taps - 1), None, ALU.mult, None, *marks)
        else:
            m = self.ts(out, x, w(n_taps - 1), b, ALU.mult, ALU.add, *marks)
        yield m
        for back in range(1, n_taps):
            m = self.stt(out[:, back:T], x[:, 0:T - back], w(n_taps - 1 - back), out[:, back:T], ALU.mult, ALU.add)
            yield m

    def mixer1(self, x_marks):
        t, r, S = self.t, self.r, self.scratch
        GLU, HB, XC, GR, GA, GB = (lambda k, o=o: t(o + k) for o in (24, 32, 40, 48, 56, 64))
        U, u_marks = self.split_tiles(8, 16, self.modulated(1, x_marks))
        self.low_lane = self.GP
        glu_marks, hb_marks = [None] * KD, [None] * KD

        def conf_conv():
            for k in range(KD):
                for m in self.taps(HB(k), GLU(k), lambda j, k=k: self.v("conf_dw_w", j * 8 + k),
                                   self.v("conf_dw_b", k), CONF_TAPS, glu_marks[k]):
                    yield
                hb_marks[k] = m
        conv = conf_conv()

        def glu():
            tmp_read = [None, None]
            for k in range(KD):
                n, gate = self.lin.take()
                gm = self.product(gate, "w_in", 24 + k, U, u_marks, KD)
                a = self.act(S[:, k % 2, :], gate, ACT.Sigmoid, gm, tmp_read[k % 2])
                self.lin.free[n] = a
                n, val = self.lin.take()
                vm = self.product(val, "w_in", 16 + k, U, u_marks, KD)
                glu_marks[k] = tmp_read[k % 2] = self.lin.free[n] = self.tt(GLU(k), S[:, k % 2, :], val, ALU.mult,
                                                                            a, vm)
                yield
        for k, _ in enumerate(glu()):
            for _ in range(14 if k else 0):
                next(conv)

        rate, neg_rate, rate_mark = self.rate
        xc_marks = [None] * KD

        def recurrence_input():
            conv_done = [None, None]
            for k in range(KD):
                raw = S[:, k % 2, :]
                n, bank = self.lin.take()
                m = yield from self.product_parts(bank, "w_in", k, U, u_marks, KD)
                self.lin.free[n] = a = self.act(raw, bank, ACT.Copy, m, conv_done[k % 2], glu_marks[KD - 1])
                yield
                for m in self.taps(XC(k), raw, lambda j, k=k: self.v("rnn_conv_w", j * 8 + k),
                                   self.v("rnn_conv_b", k), 4, a):
                    pass
                xc_marks[k] = conv_done[k % 2] = m
        pump(recurrence_input(), conv, 2)

        def recurrence():
            R, I, A, A2 = S[:, 0, :], S[:, 1, :], S[:, 4, :], S[:, 2, :]
            done = xc_marks[KD - 1]
            for k in range(KD):
                w, loaded, slot = self.unit([("rglru_w_r", k, 0), ("rglru_w_i", k, 0)])
                n, rbank = self.mat.take()
                rm = self.mm(rbank, w[:, 0:P], XC(k), True, True, loaded, xc_marks[k], step=True)
                n2, ibank = self.mat.take()
                im = self.mm(ibank, w[:, P:2 * P], XC(k), True, True, step=True)
                self.release(slot, im)
                self.mat.free[n] = self.act(R, rbank, ACT.Sigmoid, rm, done, bias=self.v("rglru_b_r", k))
                self.mat.free[n2] = a = self.act(I, ibank, ACT.Sigmoid, im, bias=self.v("rglru_b_i", k))
                yield
                self.tt(I, I, XC(k), ALU.mult, a)
                self.act(A, R, ACT.Exp, rate_mark, scale=neg_rate[:, k:k + 1])
                a = self.act(R, R, ACT.Tanh, scale=rate[:, k:k + 1])
                yield
                self.tt(A2, A, A, ALU.mult, a)
                b = self.stt(R, A2, 1.0, R, ALU.add, ALU.mult)
                a = self.act(R, R, ACT.Sqrt, b)
                yield
                self.tt(I, I, R, ALU.mult, a)
                done = xc_marks[k] = self.scan(XC(k), A, I)
                yield
        scan = recurrence()

        def gates():
            def evac(dst, marks, func):
                def evacuate(f, bank, m):
                    marks[f % KD] = self.act(dst(f % KD), bank, func, m)
                    return marks[f % KD]
                return evacuate
            yield from self.linear("w_in", range(8, 16), U, u_marks, KD, evac(GR, gr_marks, ACT.Copy), fine=True)
            yield from self.linear("w_in", range(32, 40), U, u_marks, KD, evac(GA, ga_marks, ACT.Sigmoid), fine=True)
            yield from self.linear("w_in", range(40, 48), U, u_marks, KD, evac(GB, gb_marks, ACT.Sigmoid), fine=True)
        gr_marks, ga_marks, gb_marks = [None] * KD, [None] * KD, [None] * KD

        def vector_work():
            live = True
            while live:
                live = next(scan, self) is not self
                yield
                for _ in range(3):
                    live = next(conv, self) is not self or live
                yield
        pump(gates(), vector_work(), 2.0)
        drain(scan)
        for k in range(KD):
            a = self.act(GR(k), GR(k), ACT.Gelu_apprx_tanh)
            b = self.tt(GR(k), GR(k), XC(k), ALU.mult, a, xc_marks[k])
            gr_marks[k] = self.split(r(40 + k), r(48 + k), GR(k), b)
        drain(conv)

        ya_marks, yb_marks, mix_marks = [None] * KD, [None] * KD, [None] * KD

        def scale_by(dst, marks):
            def evacuate(f, bank, m):
                marks[f] = self.tt(dst(f), dst(f), bank, ALU.mult, m)
                return marks[f]
            return evacuate
        ya = self.linear("rnn_w_proj", range(8), lambda k: (r(40 + k), r(48 + k)), gr_marks, KD,
                         scale_by(GA, ya_marks))
        next(ya)
        total = self.summed(hb_marks, HB, self.norm_sum(False))
        hb_marks = self.layer_norm(HB, total, HB, ACT.Silu, "conf_ln_g", "conf_ln_b")
        hb, hb_marks = self.split_tiles(32, 24, hb_marks)
        drain(ya)
        base = [self.ts(GR(k), self.t(k), ALPHA, None, ALU.mult, None, self.PE.last(), lane=self.GP)
                for k in range(KD)]
        for f, _ in enumerate(self.linear("conf_w_proj", range(8), hb, hb_marks, KD, scale_by(GB, yb_marks))):
            m = self.tt(t(8 + f), GA(f), GB(f), ALU.add, yb_marks[f])
            mix_marks[f] = self.split(r(16 + f), r(8 + f), t(8 + f), m)
        self.low_lane = self.VE
        evac, pm = self.residual(1, GR, base)
        drain(self.linear("mix_w_out", range(8), lambda k: (r(16 + k), r(8 + k)), mix_marks, KD, evac))
        return self.layer_norm(GR, pm, lambda k: self.t(k), ACT.Identity, "ln2_g", "ln2_b")

    def softplus(self, out, x, sign, tmp, n, rows, *marks):
        R = slice(0, rows)
        e, u, d, z = (tmp[R, i * n:(i + 1) * n] for i in range(4))
        a = self.act(e, x, ACT.Abs, *marks, self.VE.last())
        a = self.act(e, e, ACT.Exp, scale=-1.0)
        m = self.ts(u, e, 1.0, None, ALU.add, None, a)
        a = self.act(out, u, ACT.Ln, m)
        self.ts(d, u, 1.0, None, ALU.subtract, None)
        self.ts(z, d, 0.0, None, ALU.is_equal, None)
        self.tt(d, d, z, ALU.add)
        self.tt(out, out, z, ALU.add, a)
        self.tt(out, out, e, ALU.mult)
        m = self.VE.step(lambda e_: e_.reciprocal(d, d))
        self.tt(out, out, d, ALU.mult)
        self.ts(u, x, sign, 0.0, ALU.mult, ALU.max)
        return self.tt(out, out, u, ALU.add)

    def block2(self, x_marks):
        t, S = self.t, self.scratch
        U = lambda k: t(8 + k)
        self.U = U
        self.meet()
        total = self.summed(x_marks, t, self.norm_sum(True))
        self.um = um = self.rms_norm(t, total, U, "mix_norm_g_2")
        n_in = "w_in_2"
        GQ, GK, GV, GR, AQ, AK, AV, DQ, MERGE = 0, 4, 8, 12, 16, 20, 24, 28, 44

        def evac_to(dst, marks, func=ACT.Copy, scale=1.0):
            def evacuate(f, bank, m):
                k = f % 4
                marks[k] = self.act(dst(k), bank, func, m, scale=scale)
                return marks[k]
            return evacuate
        Q, K, V, R = (lambda k, o=o: t(o + k) for o in (28, 32, 36, 40))
        qm, km, vm, rm = ([None] * 4 for _ in range(4))
        lr = S[0:16, 4, :]
        rows = self.gdn_rows()
        pump(self.linear(n_in, range(GQ, GQ + 4), U, um, KD, evac_to(Q, qm, scale=DK ** -0.5)), rows, 1)
        lr_mark, _ = self.narrow(lr, 0, 16, U, um, ACT.Copy)
        pump(self.linear(n_in, range(GK, GK + 4), U, um, KD, evac_to(K, km)), rows, 1)
        pump(self.token_major(n_in, GV, U, um, V, vm), rows, 1)
        drain(rows)
        drain(self.linear(n_in, range(GR, GR + 4), U, um, KD, evac_to(R, rm, ACT.Silu)))
        AQt, AKt, AVt = (lambda k, o=o: t(o + k) for o in (57, 61, 65))
        aqm, akm, avm = ([None] * 4 for _ in range(3))

        def att_inputs():
            yield from self.linear(n_in, range(AQ, AQ + 4), U, um, KD, evac_to(AQt, aqm), fine=True)
            yield from self.linear(n_in, range(AK, AK + 4), U, um, KD, evac_to(AKt, akm), fine=True)
            yield from self.token_major(n_in, AV, U, um, AVt, avm)
        self.GD = list(range(20, 28)) + list(range(36, 44))
        fill = itertools.chain(att_inputs(), self.gdn_inputs(n_in, DQ, U, um, range(8), [t(70), t(71), t(70)]))
        pump(self.gla(Q, K, V, R, qm, km, vm, rm, lr, lr_mark), fill, 0.85)
        drain(fill)
        self.meet()
        fill = self.gdn_inputs(n_in, DQ, U, um, range(8, 16), [S[:, 0, :], S[:, 1, :], S[:, 2, :]])
        pump(self.attention(AQt, AKt, AVt, aqm, akm, avm), fill, 0.8)
        drain(fill)
        self.meet()
        self.Ym = ym = [None] * KD
        Y = [32, 33, 34, 35, 56, 69, 57, 58]
        Yt = lambda k: t(Y[k])
        fill = self.merge(Yt, [(0, 16), (1, 28)], MERGE)
        pump(self.gdn(), fill, 1.0)
        drain(fill)
        self.meet()
        before = list(ym)
        for _ in self.merge(Yt, [(2, 52)], MERGE):
            done = [f for f in range(KD) if ym[f] is not before[f]]
            for f in done:
                before[f] = ym[f] = self.split(self.r(44 + f), self.r(Y[f]), Yt(f), ym[f])
        evac, total = self.add_to_x()
        drain(self.linear("w_out_2", range(8), lambda k: (self.r(44 + k), self.r(Y[k])), ym, KD, evac))
        um = self.rms_norm(t, total, U, "ffn_norm_g_2")
        evac, total = self.add_to_x()
        u, um = self.split_tiles(8, 40, um)
        drain(self.swiglu(u, um, ("w_ffn_in_2", 0), ("w_ffn_in_2", KF), "w_ffn_out_2", evac))
        return self.rms_norm(t, total, t, "final_norm_g_2")

    def gdn_inputs(self, name, f0, U, um, tiles, scratch):
        Dt = lambda k: self.t(self.GD[k])
        RAW, SQ, STD = scratch

        def l2_norm(k):
            a = self.act(SQ, Dt(k), ACT.Square, self.PE.last())
            n, bank = self.lin.take()
            m = self.mm(bank, self.c("one"), SQ, True, True, a, step=True)
            r = self.inverse_std(bank, n, m, 1e-6, STD, self.lin)
            self.stt(Dt(k), Dt(k), DK ** -0.5 if k < 4 else 1.0, STD, ALU.mult, ALU.mult, r)
        for k in tiles:
            n, bank = self.lin.take()
            m = yield from self.product_parts(bank, name, f0 + k, U, um, KD)
            if k >= 12:
                self.lin.free[n] = self.act(Dt(k), bank, ACT.Silu, m)
            else:
                a = self.act(RAW, bank, ACT.Copy, m, self.VE.last())
                self.lin.free[n] = a
                drain(self.taps(Dt(k), RAW, lambda j, k=k: self.v("gdn_conv_w_2", j * 12 + k), None, 4, a))
                self.act(Dt(k), Dt(k), ACT.Silu, self.VE.last())
            if 1 <= k <= 7:
                l2_norm(k - 1)
            yield
            if k == 7:
                l2_norm(7)
                yield

    def gdn_rows(self):
        t, S, small = self.t, self.scratch, self.small
        G, B, EG, ED, X = (t(i)[0:HEADS, :] for i in (44, 45, 46, 47, 48))
        tmp = t(49, 4).rearrange("p a t -> p (a t)")
        am, _ = self.narrow(X, 16, HEADS, self.U, self.um, ACT.Copy)
        yield
        bm, _ = self.narrow(B, 20, HEADS, self.U, self.um, ACT.Sigmoid)
        yield
        self.ts(X, X, self.v("gdn_dt_bias_2", rows=4), None, ALU.add, None, am)
        self.softplus(G, X, 1.0, tmp, T, 4)
        yield
        ea = small[0:4, 4:5]
        a = self.act(ea, self.v("gdn_a_log_2", rows=4), ACT.Exp, self.VE.last())
        self.ts(X, G, ea, -1.0, ALU.mult, ALU.mult, a)
        b = self.scan(G, self.c("start64")[0:4, :], X)
        a = self.act(EG, G, ACT.Exp, b)
        g3 = G.rearrange("p (c i) -> p c i", i=CH)
        b = self.tt(ED.rearrange("p (c i) -> p c i", i=CH), g3[:, :, CH - 1:CH].to_broadcast([HEADS, NCH, CH]), g3,
                    ALU.subtract)
        a = self.act(ED, ED, ACT.Exp, b)
        yield
        n, bank = self.mat.take()
        for q, x in enumerate((G, B, EG, ED)):
            for p in range(BLK):
                c = (q * BLK + p) * HEADS
                m = self.tr(bank[:, c:c + HEADS], x[:, p * P:(p + 1) * P], HEADS, a, b, bm,
                            step=(q == 3 and p == BLK - 1))
        self.gcols = small[:, 224:288].rearrange("p (q b h) -> p q b h", q=4, h=HEADS)
        self.mat.free[n] = self.copy(small[:, 224:288], bank[:, 0:64], m)
        self.gcol_bg = small[:, 288:304].rearrange("p (b h) -> p b h", h=HEADS)
        self.tt(self.gcol_bg, self.gcols[:, 1], self.gcols[:, 2], ALU.mult)
        self.grow_marks = [self.act(S[r:r + HEADS, 4, :], x, ACT.Copy) for r, x in ((32, G), (64, B), (96, EG))][-1]
        yield

    def narrow(self, out, c0, width, U, um, func, scale=1.0):
        n, bank = self.mat.take()
        steps = []
        for k in range(KD):
            m = self.mm(bank[0:width, :], self.small_w[:, k, c0:c0 + width], U(k), k == 0, k == KD - 1, um[k],
                        step=True)
            steps.append(m)
        a = self.act(out, bank[0:width, :], func, m, self.VE.last(), scale=scale)
        self.mat.free[n] = a
        return a, steps

    def merge(self, Yt, branches, merge0):
        tmp = self.scratch[:, 3, :]
        names = ("w_branch_gla_2", "w_branch_att_2", "w_branch_gdn_2")
        for f in range(KD):
            for br, o in branches:
                n, gbank = self.lin.take()
                gm = yield from self.product_parts(gbank, "w_in_2", merge0 + br * 8 + f, self.U, self.um, KD)
                a = self.act(tmp, gbank, ACT.Sigmoid, gm, self.VE.last())
                self.lin.free[n] = a
                yield
                n2, bank = self.lin.take()
                bm = yield from self.product_parts(bank, names[br], f, lambda k, o=o: self.t(o + k), None, 4)
                if br == 0:
                    b = self.tt(Yt(f), tmp, bank, ALU.mult, a, bm)
                    self.lin.free[n2] = b
                else:
                    b = self.tt(tmp, tmp, bank, ALU.mult, a, bm)
                    self.lin.free[n2] = b
                    b = self.tt(Yt(f), Yt(f), tmp, ALU.add)
                self.Ym[f] = b
                yield

    def head_norm(self, O, gate, out, g, sq, std, sq_free, *marks):
        a = self.act(sq, O, ACT.Square, *marks, sq_free)
        n, bank = self.mat.take()
        m = self.mm(bank, self.c("mean_head"), sq, True, True, a, step=True)
        r = self.inverse_std(bank, n, m, 1e-6, std, self.mat)
        self.stt(O, O, self.v(g), std, ALU.mult, ALU.mult, r)
        return self.tt(out, O, gate, ALU.mult)

    def gla(self, Q, K, V, R, qm, km, vm, rm, lr, lr_mark):
        t, S, VE, small = self.t, self.scratch, self.VE, self.small
        G, A1 = [t(44), t(69)], t(45)
        E, QE, KE = [t(46), t(47)], [t(48), t(49)], [S[:, 0, :], S[:, 1, :]]
        SCORES = [t(50), t(72)]
        O, KDT, QG, KDC, TMP, A2 = t(51), t(52), t(55), t(56), S[:, 2, :], S[:, 3, :]
        states = t(53, 2).rearrange("p a (c v) -> p (a c) v", v=P)
        pair = lambda x, p: x[:, p * P:(p + 1) * P]
        wide = lambda x: x.rearrange("p (b i) -> p b i", i=P)
        masked = lambda name: self.c(name).unsqueeze(1).to_broadcast([P, BLK, P])
        g_marks = [None] * HEADS

        def decay(h):
            g, bias = G[h % 2], self.v("gla_b_gate_2", h)
            n, bank = self.mat.take()
            m = self.mm(bank, self.gate_up[:, h * P:(h + 1) * P], lr, True, True, lr_mark, step=True)
            a = self.act(A2, bank, ACT.Abs, m, VE.last(), bias=bias)
            self.mat.free[n] = self.ts(g, bank, bias, 0.0, ALU.add, ALU.min, a)
            self.act(A2, A2, ACT.Exp, scale=-1.0)
            a = self.act(A2, A2, ACT.Ln, bias=self.unit_bias)
            self.tt(A2, g, A2, ALU.subtract, a)
            self.scan(g, self.c("start64"), A2)
            g_marks[h] = self.ts(g, g, 1.0 / 16.0, None, ALU.mult, None)

        mms = [None, None]

        def front(h, li):
            s, i, g = LEVELS[li], li % 2, G[h % 2]
            g3 = g.rearrange("p (b s) -> p b s", s=2 * s)
            ref = g3[:, :, s - 1:s].to_broadcast([P, T // (2 * s), 2 * s])
            b = self.tt(E[i].rearrange("p (b s) -> p b s", s=2 * s), g3, ref, ALU.subtract, mms[i])
            self.act(E[i], E[i], ACT.Abs, b)
            a = self.act(E[i], E[i], ACT.Exp, scale=-1.0)
            kb = self.tt(KE[i], K(h), E[i], ALU.mult, a, mms[i], lane=self.GP)
            qb = self.tt(QE[i], Q(h), E[i], ALU.mult, a)
            return kb, qb

        def back(h, li, kb, qb):
            i = li % 2
            n, bank = self.mat.take()
            for p in range(BLK):
                m = self.mm(pair(bank, p), pair(KE[i], p), pair(QE[i], p), True, True, kb, qb, step=(p == BLK - 1))
            mms[i] = m
            self.mat.free[n] = self.tt(wide(TMP), wide(bank), masked(f"level{LEVELS[li]}"), ALU.mult, m)
            VE.wait(kb)
            SC = SCORES[h % 2]
            return self.tt(SC, SC, TMP, ALU.add)

        scored = [None] * HEADS

        def scores(h):
            ready = front(h, 0)
            yield
            n, bank = self.mat.take()
            for p in range(BLK):
                m = self.mm(pair(bank, p), pair(K(h), p), pair(Q(h), p), True, True, qm[h], km[h], step=(p == BLK - 1))
            self.mat.free[n] = self.tt(wide(SCORES[h % 2]), wide(bank), masked("ident"), ALU.mult, m, output_read[h])
            for li in range(len(LEVELS)):
                ahead = front(h, li + 1) if li + 1 < len(LEVELS) else None
                yield
                scored[h] = back(h, li, *ready)
                ready = ahead
                if li == 2 and h + 1 < HEADS:
                    decay(h + 1)
                yield

        output_read = [None] * (HEADS + 2)

        def output(h):
            g = G[h % 2]
            a = self.act(QG, g, ACT.Exp, g_marks[h], self.PE.last())
            el = small[:, 64 + h * 8:64 + h * 8 + 8]
            self.copy(el, QG[:, CH - 1::CH], a)
            qg = self.tt(QG, Q(h), QG, ALU.mult)
            g3 = g.rearrange("p (c i) -> p c i", i=CH)
            b = self.tt(KDC.rearrange("p (c i) -> p c i", i=CH), g3[:, :, CH - 1:CH].to_broadcast([P, NCH, CH]), g3,
                        ALU.subtract, self.PE.last())
            a = self.act(KDC, KDC, ACT.Exp, b)
            kd = self.tt(KDC, K(h), KDC, ALU.mult, a)
            yield
            n, bank = self.mat.take()
            for p in range(BLK):
                m = self.tr(pair(bank, p), pair(KDC, p), P, kd, step=(p == BLK - 1))
            a = self.act(KDT, bank, ACT.Copy, m)
            self.mat.free[n] = a
            yield
            us = []
            for half in range(2):
                n, bank = self.mat.take()
                r = half * CH
                for c in range(half, NCH - 1, 2):
                    p = c // 2
                    m = self.mm(pair(bank, p), KDT[r:r + CH, p * P:(p + 1) * P], V(p)[r:r + CH, h * P:(h + 1) * P],
                                True, True, a, vm[p], step=(c + 2 >= NCH - 1))
                us.append((n, bank, m))
            for c in range(NCH - 1):
                n, bank, m = us[c % 2]
                u = pair(bank, c // 2)
                if c == 0:
                    b = self.copy(states[:, 1, :], u, m)
                else:
                    b = self.stt(states[:, c + 1, :], states[:, c, :], el[:, c:c + 1], u, ALU.mult, ALU.add, m)
                self.mat.free[n] = b
            yield
            n, bank = self.mat.take()
            for p in range(BLK):
                m = self.mm(pair(bank, p), V(p)[:, h * P:(h + 1) * P], pair(SCORES[h % 2], p), True, False,
                            scored[h], b)
                for c in (2 * p, 2 * p + 1):
                    if c:
                        m = self.mm(bank[:, c * CH:(c + 1) * CH], states[:, c, :], QG[:, c * CH:(c + 1) * CH], False,
                                    c % 2 == 1, qg, step=(c == NCH - 1))
            output_read[h + 2] = m
            a = self.act(O, bank, ACT.Copy, m, VE.last())
            self.mat.free[n] = a
            self.head_norm(O, R(h), t(16 + h), "gla_norm_g_2", A1, KDC, None, rm[h], a, VE.last())
            yield

        decay(0)
        yield from scores(0)
        for h in range(1, HEADS):
            yield from in_step(scores(h), output(h - 1))
        yield from output(HEADS - 1)

    def attention(self, Q, K, V, qm, km, vm):
        t = self.t
        rel = self.dram["rel_rows"].rearrange("p (h m) -> p h m", m=T)
        bias, bias_read = [t(70), t(71)], [self.VE.last(), self.VE.last()]
        SC, PT = [t(44), t(45), t(72)], [t(46), t(47)]
        stat = self.small[:, 96:224]
        bias_loaded = {}

        def load_bias(h):
            bias_loaded[h] = self.load(bias[h % 2], rel[:, h, :], bias_read[h % 2])
        load_bias(0)
        load_bias(1)
        self.PE.wait(*self.mat.free)
        obank, rotate = self.mat.aps[0], Banks(self.PE, [])
        rotate.aps, rotate.free = self.mat.aps[1:], [None] * 3
        out_read = [None]
        scores_read, pt_read = [None] * 3, [None] * 2
        steps = [(h, it) for h in range(ATT_HEADS) for it in range(BLK)]

        def softmax(n_step):
            h, it = steps[n_step]
            r0, tile, i = (h % 2) * ATT_HD, h // 2, n_step % 3
            n_keys = (it + 1) * P
            n, bank = rotate.take()
            m = self.mm(bank[:, 0:n_keys], Q(tile)[r0:r0 + ATT_HD, it * P:(it + 1) * P],
                        K(tile)[r0:r0 + ATT_HD, 0:n_keys], True, True, qm[tile], km[tile], step=True)
            sc = SC[i][:, 0:n_keys]
            tile_bias = bias[h % 2]
            if it == 0:
                self.VE.step(lambda e: e.memset(tile_bias[0:CH, T - CH:T], NEG), bias_loaded[h])
            rotate.free[n] = self.stt(sc, bank[:, 0:n_keys], ATT_HD ** -0.5, tile_bias[:, T - n_keys:T], ALU.mult,
                                      ALU.add, m, scores_read[i])
            bias_read[h % 2] = rotate.free[n]
            if it == BLK - 1 and h + 2 < ATT_HEADS:
                load_bias(h + 2)
            mx, tot = stat[:, 4 * n_step:4 * n_step + 1], stat[:, 4 * n_step + 1:4 * n_step + 2]
            self.VE.step(lambda e: e.tensor_reduce(mx, sc, AX.X, ALU.max))
            b = self.ts(mx, mx, -1.0, None, ALU.mult, None)
            a = self.act(sc, sc, ACT.Exp, b, bias=mx, total=tot)
            self.VE.step(lambda e: e.reciprocal(tot, tot), a)
            return self.ts(sc, sc, tot, None, ALU.mult, None)

        def values(n_step, ready):
            h, it = steps[n_step]
            r0, sc, i = (h % 2) * ATT_HD, SC[n_step % 3], n_step % 2
            n_keys = (it + 1) * P
            n, bank = rotate.take()
            for j in range(it + 1):
                m = self.tr(bank[:, j * P:(j + 1) * P], sc[:, j * P:(j + 1) * P], P, ready, step=(j == it))
            scores_read[n_step % 3] = m
            a = self.act(PT[i][:, 0:n_keys], bank[:, 0:n_keys], ACT.Copy, m, pt_read[i])
            rotate.free[n] = a
            yield
            if h % 2 == 0 and it == 0:
                self.PE.wait(out_read[0])
            for j in range(it + 1):
                m = self.mm(obank[r0:r0 + ATT_HD, it * P:(it + 1) * P], V(j)[:, h * ATT_HD:(h + 1) * ATT_HD],
                            PT[i][:, j * P:(j + 1) * P], j == 0, j == it, a, vm[j], step=(j == it))
            pt_read[i] = m
            if h % 2 == 1 and it == BLK - 1:
                out_read[0] = self.act(t(28 + h // 2), obank, ACT.Copy, m)

        ready = {0: softmax(0), 1: softmax(1)}
        for n_step in range(len(steps)):
            if n_step + 2 < len(steps):
                ready[n_step + 2] = softmax(n_step + 2)
            yield from values(n_step, ready[n_step])
        self.mat.free = [out_read[0]] + rotate.free

    def gdn(self):
        t, S, VE = self.t, self.scratch, self.VE
        small, cols = self.small, self.gcols
        Dt = lambda k: t(self.GD[k])
        pair = lambda x, p: x[:, p * P:(p + 1) * P]
        wide = lambda x: x.rearrange("p (b i) -> p b i", i=P)
        masked = lambda name: self.c(name).unsqueeze(1).to_broadcast([P, BLK, P])
        WT = lambda h: t(44 + h)
        ATN = lambda h: t(48 + h)
        KDT = lambda h: t(63 + h)
        UV = t(59, 4)
        elast = small[:, 304:336].rearrange("p (h c) -> p h c", h=HEADS)

        def head(h, KB, GAM, AMAT, AM, TI, TT, PM):
            q, k, v = Dt(h), Dt(4 + h), Dt(8 + h)

            def row(r):
                n, bank = self.mat.take()
                sel = self.c("ident")[r:r + HEADS, r + h:r + h + 1].to_broadcast([HEADS, P])
                return n, bank, self.mm(bank, sel, S[r:r + HEADS, 4, :], True, True, self.grow_marks, step=True)
            n, bank, m = row(64)
            kb = self.tt(KB, k, bank, ALU.mult, m)
            self.mat.free[n] = kb
            yield
            n, bank, m = row(32)
            for p in range(BLK):
                b = self.ts(pair(GAM, p), pair(bank, p), cols[:, 0, p, h:h + 1], 0.0, ALU.subtract, ALU.min, m)
            self.mat.free[n] = b
            a = self.act(GAM, GAM, ACT.Exp, b)
            self.tt(wide(GAM), wide(GAM), masked("incl64"), ALU.mult, a)
            yield
            n, bank = self.mat.take()
            for p in range(BLK):
                m = self.mm(pair(bank, p), pair(k, p), pair(KB, p), True, True, kb, step=(p == BLK - 1))
            self.mat.free[n] = self.tt(AMAT, bank, GAM, ALU.mult, m)
            am = self.tt(wide(AMAT), wide(AMAT), masked("strict64"), ALU.mult)
            n, bank = self.mat.take()
            for p in range(BLK):
                m = self.mm(pair(bank, p), pair(k, p), pair(q, p), True, True, step=(p == BLK - 1))
            self.mat.free[n] = self.tt(ATN(h), bank, GAM, ALU.mult, m)
            self.copy(wide(TI), masked("ident"), self.PE.last(), self.AC.last())
            tm = self.copy(wide(TT), masked("ident"))
            m = None
            for s in reversed(LEVELS):
                g = self.tt(wide(AM), wide(AMAT), masked(f"level{s}"), ALU.mult, am, m, lane=self.GP)
                yield
                n, bank = self.mat.take()
                for p in range(BLK):
                    m = self.mm(pair(bank, p), pair(AM, p), pair(TI, p), True, True, g, tm, step=(p == BLK - 1))
                a = self.act(PM, bank, ACT.Copy, m, self.PE.last())
                self.mat.free[n] = a
                yield
                n, bank = self.mat.take()
                for p in range(BLK):
                    mi = self.mm(pair(bank, p), pair(TT, p), pair(PM, p), True, True, a, step=(p == BLK - 1))
                n2, bank2 = self.mat.take()
                for p in range(BLK):
                    mt = self.mm(pair(bank2, p), pair(PM, p), pair(TT, p), True, True, step=(p == BLK - 1))
                self.mat.free[n] = self.tt(TI, TI, bank, ALU.subtract, mi)
                self.mat.free[n2] = tm = self.tt(TT, TT, bank2, ALU.subtract, mt)
            yield
            n, bank = self.mat.take()
            for p in range(BLK):
                m = self.tr(pair(bank, p), pair(k, p), P, step=(p == BLK - 1))
            col = lambda x: x[:, :, h:h + 1].to_broadcast([P, BLK, P])
            self.tt(wide(KB), wide(bank), col(self.gcol_bg), ALU.mult, m)
            self.mat.free[n] = self.tt(wide(KDT(h)), wide(bank), col(cols[:, 3]), ALU.mult)
            n, bank = self.mat.take()
            for p in range(BLK):
                m = self.tr(pair(bank, p), pair(v, p), P, step=(p == BLK - 1))
            vb = self.tt(wide(GAM), wide(bank), col(cols[:, 1]), ALU.mult, m)
            self.mat.free[n] = vb
            yield
            n, bank = self.mat.take()
            for p in range(BLK):
                m = self.mm(pair(bank, p), pair(TT, p), pair(GAM, p), True, True, vb, tm, step=(p == BLK - 1))
            self.mat.free[n] = self.act(UV[:, h, :], bank, ACT.Copy, m)
            n, bank = self.mat.take()
            for p in range(BLK):
                m = self.mm(pair(bank, p), pair(KB, p), pair(TT, p), True, True, step=(p == BLK - 1))
            self.mat.free[n] = self.act(WT(h), bank, ACT.Copy, m)
            n, bank, m = row(96)
            self.copy(elast[:, h, :], bank[:, CH - 1::CH], m)
            self.mat.free[n] = self.tt(q, q, bank, ALU.mult)
            yield

        sets = [[t(52), t(53), t(54), t(55), S[:, 0, :], S[:, 1, :], S[:, 2, :]],
                [t(i) for i in (67, 68, 70, 62, 72, 71, 66)]]
        for h in range(0, HEADS, 2):
            yield from in_step(head(h, *sets[0]), head(h + 1, *sets[1]))
        st = lambda c: t(52 + c % 4)
        O = [Dt(8 + h) for h in range(HEADS)]
        O4 = t(36, 4)
        UV5 = UV.rearrange("p h (b v) -> p h b v", v=P)
        b = VE.last()
        for c in range(NCH):
            r, p = (c % 2) * CH, c // 2
            if c:
                n, bank = self.mat.take()
                for h in range(HEADS):
                    m = self.mm(bank[r:r + CH, h * P:(h + 1) * P], WT(h)[:, p * P + r:p * P + r + CH],
                                st(c)[:, h * P:(h + 1) * P], True, True, b, self.AC.last(), step=(h == HEADS - 1))
                b = self.tt(UV5[r:r + CH, :, p, :], UV5[r:r + CH, :, p, :], wide(bank)[r:r + CH], ALU.subtract, m)
                self.mat.free[n] = b
                yield
            else:
                b = self.AC.last()
            if c < NCH - 1:
                n, bank = self.mat.take()
                for h in range(HEADS):
                    m = self.mm(bank[:, h * P:(h + 1) * P], KDT(h)[r:r + CH, p * P:(p + 1) * P],
                                UV[r:r + CH, h, p * P:(p + 1) * P], True, True, b, step=(h == HEADS - 1))
                if c == 0:
                    b = self.copy(st(c + 1), bank, m)
                else:
                    e4 = elast[:, :, c:c + 1].to_broadcast([P, HEADS, P])
                    self.tt(wide(st(c + 1)), wide(st(c)), e4, ALU.mult, self.PE.last())
                    b = self.tt(st(c + 1), st(c + 1), bank, ALU.add, m)
                self.mat.free[n] = b
                yield
            if c % 2 == 1:
                n, bank = self.mat.take()
                for h in range(HEADS):
                    self.mm(pair(bank, h), UV[:, h, p * P:(p + 1) * P], pair(ATN(h), p), True, False, b)
                    for cc in (c - 1, c):
                        if cc:
                            m = self.mm(bank[:, h * P + (cc % 2) * CH:h * P + (cc % 2 + 1) * CH],
                                        st(cc)[:, h * P:(h + 1) * P], Dt(h)[:, cc * CH:(cc + 1) * CH], False,
                                        cc == c, step=(h == HEADS - 1 and cc == c))
                self.mat.free[n] = self.act(O4[:, :, p * P:(p + 1) * P], wide(bank), ACT.Copy, m)
        for h in range(HEADS):
            self.head_norm(O[h], Dt(12 + h), t(52 + h), "gdn_norm_g_2", S[:, h % 2, :], S[:, 2, :], None,
                           VE.last(), self.PE.last())
            yield

    def block3(self, x_marks):
        t, S, VE = self.t, self.scratch, self.VE
        name = "w_in_3"
        UU, VV, ZZ, XS, BM, CM, GATE = 0, 8, 16, 32, 48, 56, 64
        YA, YB, M, VN = (lambda k, o=o: t(o + k) for o in (32, 32, 24, 24))
        sp = self.load(t(66, 2).rearrange("p a (g i) -> p (a g) i", i=P), self.dram["w_spatial_T"]
                       .rearrange("p (g i) -> p g i", i=P), self.met)
        bs = self.load(t(68, 2).rearrange("p a t -> p (a t)"), self.dram["b_spatial_rows"], self.met)
        total = self.summed(x_marks, t, self.norm_sum(True))
        um = self.rms_norm(t, total, lambda k: t(8 + k), "norm_mix_g_3")
        raw = t(57)[0:MH, :]
        raw_mark, steps = self.narrow(raw, 24, MH, lambda k: t(8 + k), um, ACT.Copy)
        U, um = self.split_tiles(8, 16, um, steps)
        self.low_lane = self.GP
        vmk, umk = [None] * KD, [None] * KD

        def gelu_to(dst, marks):
            def evacuate(f, bank, m):
                marks[f % KD] = self.act(dst(f % KD), bank, ACT.Gelu, m)
                return marks[f % KD]
            return evacuate
        pump(self.linear(name, range(VV, VV + 8), U, um, KD, gelu_to(VN, vmk)), self.ssd_rates(raw, raw_mark), 0.5)
        uu = self.linear(name, range(UU, UU + 8), U, um, KD, gelu_to(YA, umk))
        next(uu)
        total = self.summed(vmk, VN, self.norm_sum(False))
        vm = self.layer_norm(VN, total, VN, ACT.Identity, "v_norm_g_3", "v_norm_b_3")
        for _ in range(4):
            next(uu)

        ya_marks = [None] * KD

        def spatial():
            WS = t(66, 2).rearrange("p a (g i) -> p (a g) i", i=P)
            BS = t(68, 2).rearrange("p a (g i) -> p (a g) i", i=P)
            causal = self.c("causal").unsqueeze(1).to_broadcast([P, KD, P])
            w3 = lambda x: x.rearrange("p (b i) -> p b i", i=P)
            wm = self.tt(WS, WS, causal, ALU.mult, sp, bs)
            read = [None, None]
            for g in range(KD):
                n, bank = self.mat.take()
                for c in range(BLK):
                    m = self.tr(bank[:, c * P:(c + 1) * P], VN(g)[:, c * P:(c + 1) * P], P, vm[g], step=(c == BLK - 1))
                vt = S[:, 3 + g % 2, :]
                a = self.act(vt, bank, ACT.Copy, m, read[g % 2])
                self.mat.free[n] = a
                yield
                n, bank = self.mat.take()
                for c in range(BLK):
                    m = self.mm(bank[:, c * P:(c + 1) * P], vt[:, c * P:(c + 1) * P], WS[:, g, :], True, True, a, wm,
                                step=(c == BLK - 1))
                read[g % 2] = m
                b = self.tt(w3(VN(g)), w3(bank), BS[:, g:g + 1, :].to_broadcast([P, BLK, P]), ALU.add, m)
                self.mat.free[n] = b
                b = self.tt(YA(g), YA(g), VN(g), ALU.mult, umk[g])
                ya_marks[g] = self.split(self.r(40 + g), self.r(32 + g), YA(g), b)
                yield
        mixing = spatial()
        pump(uu, mixing, 2)

        ins = [[t(48 + 12 * i + j) for j in range(6)] for i in range(2)]
        free = [None, None]
        in_marks = {}

        def inputs(g):
            x0, x1, bb, cc, z0, z1 = ins[g % 2]
            tiles = [(XS + 2 * g, x0, 2 * g), (XS + 2 * g + 1, x1, 2 * g + 1), (BM + g, bb, 16 + g),
                     (CM + g, cc, 24 + g), (ZZ + 2 * g, z0, None), (ZZ + 2 * g + 1, z1, None)]
            for j, (f, dst, ch) in enumerate(tiles):
                n, bank = self.lin.take()
                m = yield from self.product_parts(bank, name, f, U, um, KD)
                if ch is None:
                    self.lin.free[n] = in_marks[g, j] = self.act(dst, bank, ACT.Silu, m, free[g % 2])
                else:
                    raw = S[:, ch % 2, :]
                    a = self.act(raw, bank, ACT.Copy, m, in_marks.get((g, j - 2)))
                    self.lin.free[n] = a
                    for b in self.taps(dst, raw, lambda i, ch=ch: self.v("conv_w_3", i * 32 + ch),
                                       self.v("conv_b_3", ch), 4, a, free[g % 2]):
                        pass
                    in_marks[g, j] = self.act(dst, dst, ACT.Silu, b)
                yield
        pump(inputs(0), mixing, 1)
        drain(mixing)

        def gated(f, branch, proj, src, marks, kts, out):
            n, gate_bank = self.lin.take()
            gm = self.product(gate_bank, name, GATE + branch * 8 + f, U, um, KD)
            tmp = S[:, 3, :]
            a = self.act(tmp, gate_bank, ACT.Sigmoid, gm, VE.last(), bias=self.v("b_gates_3", branch * 8 + f))
            self.lin.free[n] = a
            n, bank = self.lin.take()
            m = self.product(bank, proj, f, src, marks, kts)
            self.lin.free[n] = b = self.tt(out, tmp, bank, ALU.mult, a, m)
            return b
        merged = [gated(f, 0, "w_proj_a_3", lambda k: (self.r(40 + k), self.r(32 + k)), ya_marks, KD, M(f))
                  for f in range(KD)]
        group_done, squares_used = [self.PE.last(), self.GP.last()], [None]
        last_norm = iter(())
        for g in range(MG):
            following = inputs(g + 1) if g + 1 < MG else iter(())
            marks = [in_marks[g, j] for j in range(6)]
            group_done = pump(self.ssd_group(g, ins[g % 2], marks, YB, last_norm, group_done), following, 1.1)
            free[g % 2] = [self.PE.last(), VE.last(), self.AC.last(), self.GP.last()]
            drain(following)
            last_norm = self.group_norm(g, YB, squares_used)
        drain(last_norm)
        self.low_lane = self.VE
        groups_done = [self.PE.last(), self.GP.last()]
        yb_marks = [self.split(self.r(48 + k), self.r(32 + k), YB(k), VE.last(), groups_done) for k in range(2 * KD)]
        for f in range(KD):
            gated(f, 1, "w_proj_b_3", lambda k: (self.r(48 + k), self.r(32 + k)), yb_marks, 2 * KD, S[:, 4, :])
            b = self.tt(M(f), M(f), S[:, 4, :], ALU.add)
            merged[f] = self.split(self.r(64 + f), self.r(24 + f), M(f), b)
        evac, total = self.add_to_x()
        drain(self.linear("w_out_3", range(8), lambda k: (self.r(64 + k), self.r(24 + k)), merged, KD, evac))
        um = self.rms_norm(t, total, lambda k: t(8 + k), "norm_mlp_g_3")
        u, um = self.split_tiles(8, 40, um)

        def hidden(j, out):
            n, bank = self.lin.take()
            m = self.product(bank, "w_mlp_up_3", j, u, um, KD)
            relu = S[:, j % 2, :]
            a = self.act(relu, bank, ACT.Relu, m, VE.last())
            self.lin.free[n] = a
            return self.tt(out, relu, relu, ALU.mult, a)
        evac, total = self.add_to_x()
        drain(self.feed_forward(hidden, 32, "w_mlp_down_3", evac))
        return self.rms_norm(t, total, lambda k: t(8 + k), "norm_final_g_3")

    def ssd_rates(self, raw, raw_mark):
        t, VE, CS = self.t, self.VE, self.rows[0:MH, :]
        DT, DD = t(54)[0:MH, :], t(56)[0:MH, :]
        self.ts(raw, raw, self.v("dt_bias_3", rows=MH), None, ALU.add, None, raw_mark)
        self.softplus(DT, raw, 1.0, t(60, 4).rearrange("p a t -> p (a t)"), T, MH)
        yield
        ea = self.small[0:MH, 4:5]
        a = self.act(ea, self.v("a_log_3", rows=MH), ACT.Exp, VE.last())
        self.ts(raw, DT, ea, -1.0, ALU.mult, ALU.mult, a)
        self.scan(CS, self.c("start128")[0:MH, :], raw)
        c3 = CS.rearrange("p (c i) -> p c i", i=P)
        b = self.tt(DD.rearrange("p (c i) -> p c i", i=P), c3[:, :, P - 1:P].to_broadcast([MH, BLK, P]), c3,
                    ALU.subtract)
        a = self.act(DD, DD, ACT.Exp, b)
        b = self.tt(DD, DD, DT, ALU.mult, a)
        yield
        yield
        n, bank = self.mat.take()
        for q, x in enumerate((DT, CS, DD)):
            for c in range(BLK):
                o = (q * BLK + c) * MH
                m = self.tr(bank[:, o:o + MH], x[:, c * P:(c + 1) * P], MH, b, step=(q == 2 and c == BLK - 1))
        self.mat.free[n] = self.copy(t(72)[:, 0:384], bank[:, 0:384], m)
        self.rate_columns = t(72)[:, 0:384].rearrange("p (q c h) -> p q c h", q=3, h=MH)
        yield

    def ssd_group(self, g, tiles, marks, YB, last_norm, earlier):
        t, VE = self.t, self.VE
        x0, x1, BMt, CMt, z0, z1 = tiles
        xm, bm, cm, zm = marks[0:2], marks[2], marks[3], marks[4:6]
        cols = self.rate_columns
        blk = lambda x, c: x[:, c * P:(c + 1) * P]
        wide = lambda x: x.rearrange("p (b i) -> p b i", i=P)
        CB, BT = t(54), t(55)
        XD = t(56, 2).rearrange("p a (c f) -> p (a c) f", f=256)
        XE = t(58, 2).rearrange("p a (c f) -> p (a c) f", f=256)
        L = [t(66), t(67)]
        CE = [t(68), t(69)]
        HS = t(70, 2).rearrange("p a (c f) -> p (a c) f", f=256)
        dec = self.small[:, 208:224].rearrange("p (h c) -> p h c", h=MHG)
        sts, y_steps = [], {}

        def decays(hh):
            head, i = 4 * g + hh, hh % 2
            n, bank = self.lin.take()
            sel = self.c("ident")[0:MH, head:head + 1].to_broadcast([MH, P])
            m = self.mm(bank, sel, self.rows[0:MH, :], True, True, step=True)
            a = self.act(CE[i], bank, ACT.Exp, m, y_steps.get(hh - 2, earlier))
            self.copy(dec[:, hh, :], CE[i][:, P - 1::P], a)
            for c in range(BLK):
                b = self.ts(blk(L[i], c), blk(bank, c), cols[:, 1, c, head:head + 1], 0.0, ALU.subtract, ALU.min, m,
                            y_steps.get(hh - 2, earlier))
            self.lin.free[n] = b
            a = self.act(L[i], L[i], ACT.Exp, b)
            ce = self.tt(CE[i], CE[i], CMt, ALU.mult)
            return ce, self.tt(L[i], L[i], CB, ALU.mult, a)

        def states(hh):
            hsl = slice(hh * MP, (hh + 1) * MP)
            for c in range(BLK - 1):
                ns, sbank, sm = sts[c]
                s = sbank[:, (c % 2) * 256 + hh * MP:(c % 2) * 256 + (hh + 1) * MP]
                if c == 0:
                    hb = self.copy(HS[:, 1, hsl], s, sm)
                else:
                    hb = self.stt(HS[:, c + 1, hsl], HS[:, c, hsl], dec[:, hh, c:c + 1], s, ALU.mult, ALU.add, sm)
                self.mat.free[ns] = hb
            return hb

        n, bank = self.mat.take()
        for c in range(BLK):
            m = self.mm(blk(bank, c), blk(BMt, c), blk(CMt, c), True, True, bm, cm, step=(c == BLK - 1))
        causal = self.c("causal").unsqueeze(1).to_broadcast([P, BLK, P])
        self.mat.free[n] = self.tt(wide(CB), wide(bank), causal, ALU.mult, m)
        n, bank = self.mat.take()
        for c in range(BLK):
            m = self.tr(blk(bank, c), blk(BMt, c), P, step=(c == BLK - 1))
        self.mat.free[n] = bt = self.act(BT, bank, ACT.Copy, m, earlier)
        yield
        next(last_norm, None)
        for i, x in enumerate((x0, x1)):
            n, bank = self.mat.take()
            for c in range(BLK):
                m = self.tr(blk(bank, c), blk(x, c), P, xm[i], step=(c == BLK - 1))
            x4 = bank.rearrange("p (c e f) -> p c e f", c=BLK, e=2)
            h0 = 4 * g + 2 * i
            for q, dst in ((0, XD), (2, XE)):
                col = cols[:, q, :, h0:h0 + 2].unsqueeze(3).to_broadcast([P, BLK, 2, MP])
                d4 = dst[:, :, i * P:(i + 1) * P].rearrange("p c (e f) -> p c e f", e=2)
                xe = self.tt(d4, x4, col, ALU.mult, m, earlier)
            self.mat.free[n] = xe
        yield
        next(last_norm, None)
        decayed = {0: decays(0)}
        yield
        next(last_norm, None)
        for c in range(BLK - 1):
            if c % 2 == 0:
                n, bank = self.mat.take()
            m = self.mm(bank[:, (c % 2) * 256:(c % 2 + 1) * 256], blk(BT, c), XE[:, c, :], True, True, xe, bt,
                        step=True)
            sts = sts[:c - c % 2] + [(n, bank, m)] * (c % 2 + 1)
        state = {0: states(0)}
        yield
        for hh in range(MHG):
            i, hsl = hh % 2, slice(hh * MP, (hh + 1) * MP)
            if hh + 1 < MHG:
                decayed[hh + 1], state[hh + 1] = decays(hh + 1), states(hh + 1)
            yield
            if i == 0:
                yn, ybank = self.mat.take()
            r = i * MP
            for c in range(BLK):
                m = self.mm(blk(ybank, c)[r:r + MP], XD[:, c, hsl], blk(L[i], c), True, c == 0, state[hh],
                            *decayed[hh])
                if c:
                    m = self.mm(blk(ybank, c)[r:r + MP], HS[:, c, hsl], blk(CE[i], c), False, True,
                                step=(c == BLK - 1))
            y_steps[hh] = m
            if i == 1:
                k = hh // 2
                y = YB(2 * g + k)
                self.mat.free[yn] = self.stt(y, (x0, x1)[k], self.v("d_skip_3", 2 * g + k), ybank, ALU.mult,
                                             ALU.add, m)
                self.tt(y, y, (z0, z1)[k], ALU.mult, zm[k])
            yield
        return m

    def group_norm(self, g, YB, squares_used):
        S, y_mark = self.scratch, self.VE.last()
        n, bank = self.mat.take()
        for k in range(2):
            a = self.act(S[:, 3 + k, :], YB(2 * g + k), ACT.Square, y_mark, squares_used[0])
            m = self.mm(bank, self.c("mean_group"), S[:, 3 + k, :], k == 0, k == 1, a, step=True)
        squares_used[0] = m
        yield
        r = self.inverse_std(bank, n, m, 1e-6, S[:, 2, :], self.mat)
        yield
        for k in range(2):
            self.stt(YB(2 * g + k), YB(2 * g + k), self.v("ssm_norm_g_3", 2 * g + k), S[:, 2, :], ALU.mult, ALU.mult, r)
        yield

    def build(self):
        self.setup()
        x_marks = self.block1()
        x_marks = self.block2(x_marks)
        self.met = self.meet()
        om = self.block3(x_marks)
        out_sem = self.semaphore("stored")
        o = self.dram["out"].rearrange("p (k t) -> p k t", k=KD)
        self.SP.issue(lambda e: e.dma_start(o, self.t(8, 8)).then_inc(out_sem, 16), *om)
        self.SP.wait(("stored", out_sem, 16))

    def run(self):
        with self.nc.Block() as block:
            @block.tensor
            def _(e):
                self.PE.run(e)

            @block.scalar
            def _(e):
                self.AC.run(e)

            @block.vector
            def _(e):
                self.VE.run(e)

            @block.gpsimd
            def _(e):
                self.GP.run(e)

            @block.sync
            def _(e):
                self.SP.run(e)


INPUTS = [("x", (P, KD * T)), ("c", (1, D)), ("c_columns", (P, KD)), ("vectors", (P, NVEC)), ("constants", (P, NCONST)),
          ("small_weights", (P, KD * 64)), ("gla_w_gate_up", (16, T)), ("rel_rows", (P, ATT_HEADS * T)),
          ("w_spatial_T", (P, KD * P)), ("b_spatial", (1, KD * P))]


def build_program(nc, out_shape=(P, KD * T)):
    dram = {name: nc.dram_tensor(name, shape, F32, kind="ExternalInput").ap() for name, shape in INPUTS}
    n_blocks = weight_blocks()
    dram["weights"] = nc.dram_tensor("weights", (n_blocks * P * P,), F32, kind="ExternalInput").ap()
    dram["out"] = nc.dram_tensor("out", out_shape, F32, kind="ExternalOutput").ap()
    dram["c_rows"] = bass.AP(dram["c"].tensor, 0, [[0, P], [1, D]])
    dram["b_spatial_rows"] = bass.AP(dram["b_spatial"].tensor, 0, [[0, P], [1, KD * P]])
    memory = Memory(nc)
    first = Program(nc, dram, memory)
    first.build()
    plan = first.plan
    program = Program(nc, dram, memory, plan)
    program.build()
    program.run()
    assert sum(map(len, plan)) == n_blocks
    return plan


def weight_blocks():
    swiglu = 3 * KD * KF
    one = 72 * KD + 2 * swiglu + KD * 48 + 2 * KD + 3 * KD * KD
    two = KD * 68 + 3 * 4 * KD + KD * KD + swiglu
    three = KD * 80 + KD * KD + 2 * KD * KD + KD * KD + 2 * KD * 32
    return one + two + three


def lay_out(inputs, plan):
    a = {k: np.asarray(v) for k, v in inputs.items()}
    a = {k: (v[0] if k.endswith(("_2", "_3")) and k not in ("final_norm_g_2", "norm_final_g_3") else v)
         for k, v in a.items()}
    columns = lambda v: np.ascontiguousarray(v).reshape(-1, P).T
    a["d_skip_3"] = np.repeat(a["d_skip_3"], MP)
    vectors = np.zeros((P, NVEC), np.float32)
    for name, w in VECTORS:
        c = VCOL[name]
        if name in ("gdn_a_log_2", "gdn_dt_bias_2", "dt_bias_3", "a_log_3"):
            vectors[:a[name].size, c] = a[name]
        else:
            vectors[:, c:c + w] = columns(a[name])
    w2, w3 = a["w_in_2"], a["w_in_3"]
    a["w_in_2"] = np.concatenate([w2[:, :2048], w2[:, 2064:5648], w2[:, 5656:]], axis=1)
    a["w_in_3"] = np.concatenate([w3[:, :8192], w3[:, 8224:]], axis=1)
    small = np.zeros((D, 64), np.float32)
    small[:, 0:16], small[:, 16:24], small[:, 24:56] = w2[:, 2048:2064], w2[:, 5648:5656], w3[:, 8192:8224]
    small = small.reshape(KD, P, 64).transpose(1, 0, 2).reshape(P, KD * 64)
    rel = a["att_rel_bias_2"][:, ::-1]
    padded = np.zeros((ATT_HEADS, 640), np.float32)
    padded[:, :255] = rel[:, :1]
    padded[:, 255:255 + REL] = rel
    rows = np.stack([padded[:, P - 1 - p:P - 1 - p + T] for p in range(P)]).reshape(P, ATT_HEADS * T)
    for name in ("rglru_w_r", "rglru_w_i"):
        a[name] = a[name].reshape(D, P)
    stream = np.empty((weight_blocks() * P * P,), np.float32)
    at = 0
    for blocks in plan:
        n = len(blocks)
        part = stream[at:at + n * P * P].reshape(P, n, P)
        for i, (name, k, f) in enumerate(blocks):
            w = a["ada_w"] if name == "ada_w_T" else a[name]
            b = w[k * P:(k + 1) * P, f * P:(f + 1) * P]
            part[:, i, :] = b.T if name == "ada_w_T" else b
        at += n * P * P
    spatial = a["w_spatial_3"].transpose(2, 0, 1).reshape(P, KD * P)
    x = a["x"].reshape(T, KD, P).transpose(2, 1, 0).reshape(P, KD * T)
    return {"x": np.ascontiguousarray(x), "c": a["c"].reshape(1, D),
            "c_columns": np.ascontiguousarray(columns(a["c"])), "vectors": vectors, "constants": constants(),
            "small_weights": np.ascontiguousarray(small), "gla_w_gate_up": np.ascontiguousarray(a["gla_w_gate_up_2"]),
            "rel_rows": rows, "w_spatial_T": np.ascontiguousarray(spatial),
            "b_spatial": np.ascontiguousarray(a["b_spatial_3"]).reshape(1, KD * P), "weights": stream}


def kernel(**inputs):
    import concourse.bacc as bacc
    from concourse.bass_utils import run_bass_kernel_spmd

    nc = bacc.Bacc("TRN2", target_bir_lowering=False, num_devices=1)
    plan = build_program(nc)
    result = run_bass_kernel_spmd(nc, [lay_out(inputs, plan)], core_ids=[0])
    out = result.results[0]["out"]
    return np.ascontiguousarray(out.reshape(P, KD, T).transpose(2, 1, 0)).reshape(1, T, D)
```
